# Optimizing a Trainium2 kernel written in Bass

```python
import jax
import jax.numpy as jnp
from jax import lax
import numpy as np
import math
import jax, jax.numpy as jnp

D_MODEL = 1024
BATCH = 1
SEQ = 256
DEPTH = 1

PLE_DIM = 256
D_FF = 2816
N_HEADS = 8
N_KV_HEADS = 2
HEAD_DIM = 64
HEADS_PER_GROUP = N_HEADS // N_KV_HEADS
NSA_WIDTH = N_HEADS * HEAD_DIM
KV_WIDTH = N_KV_HEADS * HEAD_DIM
S5_WIDTH = D_MODEL - NSA_WIDTH
S5_GROUP = 16
S5_GROUPS = S5_WIDTH // S5_GROUP
S5_STATE = 64
CMP_LEN = 32
CMP_STRIDE = 16
CMP_HIDDEN = 256
SEL_BLOCK = 64
SEL_TOPK = 16
WINDOW = 512
Q_BLOCK = 128
ROPE_THETA = 10000.0
RMS_EPS = 1e-6
NEG = -1e30
BIG = 1e9
IN_COLS = NSA_WIDTH + 6 * KV_WIDTH + 3 * N_HEADS + S5_WIDTH


def rmsnorm(x, g):
    xf = x.astype(jnp.float32)
    y = xf * lax.rsqrt(jnp.mean(xf * xf, axis=-1, keepdims=True) + RMS_EPS)
    return (y * g.astype(jnp.float32)).astype(x.dtype)

def swiglu(x, w1, w3, w2):
    return (jax.nn.silu(x @ w1) * (x @ w3)) @ w2

def rope(x, pos):
    half = HEAD_DIM // 2
    inv = ROPE_THETA ** (-jnp.arange(half, dtype=jnp.float32) / half)
    ang = pos[:, None] * inv[None, :]
    cos = jnp.cos(ang)[None, :, None, :]
    sin = jnp.sin(ang)[None, :, None, :]
    xf = x.astype(jnp.float32)
    x1, x2 = xf[..., :half], xf[..., half:]
    return jnp.concatenate([x1 * cos - x2 * sin, x1 * sin + x2 * cos], axis=-1).astype(x.dtype)

def masked_softmax(s, mask):
    s = jnp.where(mask, s, NEG)
    m = jnp.max(s, axis=-1, keepdims=True)
    e = jnp.where(mask, jnp.exp(s - m), 0.0)
    return e / jnp.maximum(jnp.sum(e, axis=-1, keepdims=True), 1e-30)

def compress(kv, pe, w1, w2):
    B, L = kv.shape[:2]
    n_cmp = (L - CMP_LEN) // CMP_STRIDE + 1
    tok = jnp.arange(n_cmp)[:, None] * CMP_STRIDE + jnp.arange(CMP_LEN)[None, :]
    blk = kv[:, tok] + pe[None, None, :, None, :]
    blk = jnp.transpose(blk, (0, 1, 3, 2, 4)).reshape(B, n_cmp, N_KV_HEADS, CMP_LEN * HEAD_DIM)
    return jax.nn.gelu(blk @ w1) @ w2

def nsa_attention(q, k_cmp, v_cmp, k_slc, v_slc, k_win, v_win, gates, pe_k, pe_v, wk1, wk2, wv1, wv2):
    B, L = q.shape[:2]
    G, HPG, DK = N_KV_HEADS, HEADS_PER_GROUP, HEAD_DIM
    n_cmp = (L - CMP_LEN) // CMP_STRIDE + 1
    n_sel = L // SEL_BLOCK
    n_qb = L // Q_BLOCK
    top_k = min(SEL_TOPK, n_sel)
    scale = DK ** -0.5

    kc = compress(k_cmp, pe_k, wk1, wk2)
    vc = compress(v_cmp, pe_v, wv1, wv2)
    c_start = jnp.arange(n_cmp) * CMP_STRIDE
    c_end = c_start + CMP_LEN - 1
    s_start = jnp.arange(n_sel) * SEL_BLOCK
    overlap = ((c_start[:, None] < s_start[None, :] + SEL_BLOCK)
               & (c_start[:, None] + CMP_LEN > s_start[None, :])).astype(jnp.float32)

    ks_blk = jnp.transpose(k_slc.reshape(B, n_sel, SEL_BLOCK, G, DK), (0, 3, 1, 2, 4))
    vs_blk = jnp.transpose(v_slc.reshape(B, n_sel, SEL_BLOCK, G, DK), (0, 3, 1, 2, 4))
    kw_pad = jnp.pad(k_win, ((0, 0), (WINDOW, 0), (0, 0), (0, 0)))
    vw_pad = jnp.pad(v_win, ((0, 0), (WINDOW, 0), (0, 0), (0, 0)))
    b_ix = jnp.arange(B)[:, None, None, None]
    g_ix = jnp.arange(G)[None, :, None, None]
    blk_ids = jnp.arange(n_sel)

    q_blocks = jnp.transpose(q.reshape(B, n_qb, Q_BLOCK, G, HPG, DK), (1, 0, 2, 3, 4, 5))
    g_blocks = jnp.transpose(gates.reshape(B, n_qb, Q_BLOCK, G, HPG, 3), (1, 0, 2, 3, 4, 5))

    def one_block(args):
        c, qc, gc = args
        t = c * Q_BLOCK + jnp.arange(Q_BLOCK)
        s = jnp.einsum('bqghd,bcgd->bghqc', qc, kc).astype(jnp.float32) * scale
        p_cmp = masked_softmax(s, c_end[None, :] <= t[:, None])
        o_cmp = jnp.einsum('bghqc,bcgd->bqghd', p_cmp.astype(vc.dtype), vc)
        imp = jnp.einsum('bghqc,cs->bgqs', p_cmp, overlap)
        cur = (t // SEL_BLOCK)[:, None]
        valid = blk_ids[None, :] <= cur
        forced = (blk_ids[None, :] == 0) | (blk_ids[None, :] == cur) | (blk_ids[None, :] == cur - 1)
        score = jnp.where(valid & forced, BIG, jnp.where(valid, imp, -BIG))
        _, idx = lax.top_k(score, top_k)
        k_sel = ks_blk[b_ix, g_ix, idx]
        v_sel = vs_blk[b_ix, g_ix, idx].reshape(B, G, Q_BLOCK, top_k * SEL_BLOCK, DK)
        s = jnp.einsum('bqghd,bgqkrd->bghqkr', qc, k_sel).astype(jnp.float32) * scale
        s = s.reshape(B, G, HPG, Q_BLOCK, top_k * SEL_BLOCK)
        kpos = (idx[..., None] * SEL_BLOCK + jnp.arange(SEL_BLOCK)).reshape(B, G, 1, Q_BLOCK, top_k * SEL_BLOCK)
        p_slc = masked_softmax(s, kpos <= t[:, None])
        o_slc = jnp.einsum('bghqn,bgqnd->bqghd', p_slc.astype(v_sel.dtype), v_sel)
        start = c * Q_BLOCK
        k_w = lax.dynamic_slice_in_dim(kw_pad, start, WINDOW + Q_BLOCK, axis=1)
        v_w = lax.dynamic_slice_in_dim(vw_pad, start, WINDOW + Q_BLOCK, axis=1)
        spos = start - WINDOW + jnp.arange(WINDOW + Q_BLOCK)
        dist = t[:, None] - spos[None, :]
        wmask = (spos[None, :] >= 0) & (dist >= 0) & (dist < WINDOW)
        s = jnp.einsum('bqghd,bsgd->bghqs', qc, k_w).astype(jnp.float32) * scale
        p_win = masked_softmax(s, wmask)
        o_win = jnp.einsum('bghqs,bsgd->bqghd', p_win.astype(v_w.dtype), v_w)
        o = gc[..., 0:1] * o_cmp + gc[..., 1:2] * o_slc + gc[..., 2:3] * o_win
        return o.astype(qc.dtype)

    out = lax.map(one_block, (jnp.arange(n_qb), q_blocks, g_blocks))
    return jnp.transpose(out, (1, 0, 2, 3, 4, 5)).reshape(B, L, NSA_WIDTH)

def s5_mixer(u, a_re, a_im, log_dt, b_re, b_im, c_re, c_im, d_skip, w_glu, b_glu):
    B, L = u.shape[:2]
    f32 = jnp.float32
    uf = u.astype(f32).reshape(B, L, S5_GROUPS, S5_GROUP)
    lam = lax.complex(a_re.astype(f32), a_im.astype(f32))
    dt = jnp.exp(log_dt.astype(f32))[:, None]
    a_bar = jnp.exp(lam * dt)
    b_coef = (a_bar - 1.0) / lam
    bu_re = jnp.einsum('blgi,gni->blgn', uf, b_re.astype(f32))
    bu_im = jnp.einsum('blgi,gni->blgn', uf, b_im.astype(f32))
    bu = lax.complex(bu_re, bu_im) * b_coef
    a_seq = jnp.broadcast_to(a_bar, (1, L) + a_bar.shape)

    def combine(e1, e2):
        a1, x1 = e1
        a2, x2 = e2
        return a2 * a1, a2 * x1 + x2

    _, state = lax.associative_scan(combine, (a_seq, bu), axis=1)
    y = (jnp.einsum('blgn,gon->blgo', jnp.real(state), c_re.astype(f32))
         - jnp.einsum('blgn,gon->blgo', jnp.imag(state), c_im.astype(f32))
         + d_skip.astype(f32) * uf)
    y = jax.nn.gelu(y.reshape(B, L, S5_WIDTH))
    out = y * jax.nn.sigmoid(y @ w_glu.astype(f32) + b_glu.astype(f32))
    return out.astype(u.dtype)

def first_inputs(seed: int = 0) -> dict:
    key = jax.random.key(seed)
    ks = jax.random.split(key, 40)
    f32 = jnp.float32

    def nrm(k, shape, fan_in):
        return jax.random.normal(k, shape, f32) * (fan_in ** -0.5)

    def gain(k, shape):
        return 1.0 + 0.05 * jax.random.normal(k, shape, f32)

    n_idx = jnp.arange(S5_STATE, dtype=f32)
    return {
        "x": jax.random.normal(ks[0], (BATCH, SEQ, D_MODEL), f32),
        "p": jax.random.normal(ks[1], (DEPTH, BATCH, SEQ, PLE_DIM), f32),
        "norm_ffn1": gain(ks[2], (DEPTH, D_MODEL)),
        "ffn1_w1": nrm(ks[3], (DEPTH, D_MODEL, D_FF), D_MODEL),
        "ffn1_w3": nrm(ks[4], (DEPTH, D_MODEL, D_FF), D_MODEL),
        "ffn1_w2": nrm(ks[5], (DEPTH, D_FF, D_MODEL), D_FF),
        "norm_mix": gain(ks[6], (DEPTH, D_MODEL)),
        "w_in": nrm(ks[7], (DEPTH, D_MODEL, IN_COLS), D_MODEL),
        "cmp_pe_k": 0.1 * jax.random.normal(ks[8], (DEPTH, CMP_LEN, HEAD_DIM), f32),
        "cmp_pe_v": 0.1 * jax.random.normal(ks[9], (DEPTH, CMP_LEN, HEAD_DIM), f32),
        "cmp_wk1": nrm(ks[10], (DEPTH, CMP_LEN * HEAD_DIM, CMP_HIDDEN), CMP_LEN * HEAD_DIM),
        "cmp_wk2": nrm(ks[11], (DEPTH, CMP_HIDDEN, HEAD_DIM), CMP_HIDDEN),
        "cmp_wv1": nrm(ks[12], (DEPTH, CMP_LEN * HEAD_DIM, CMP_HIDDEN), CMP_LEN * HEAD_DIM),
        "cmp_wv2": nrm(ks[13], (DEPTH, CMP_HIDDEN, HEAD_DIM), CMP_HIDDEN),
        "s5_a_re": -0.5 + 0.01 * jax.random.normal(ks[14], (DEPTH, S5_GROUPS, S5_STATE), f32),
        "s5_a_im": jnp.pi * n_idx + 0.01 * jax.random.normal(ks[15], (DEPTH, S5_GROUPS, S5_STATE), f32),
        "s5_log_dt": jax.random.uniform(ks[16], (DEPTH, S5_GROUPS), f32, jnp.log(0.001), jnp.log(0.1)),
        "s5_b_re": nrm(ks[17], (DEPTH, S5_GROUPS, S5_STATE, S5_GROUP), 2 * S5_GROUP),
        "s5_b_im": nrm(ks[18], (DEPTH, S5_GROUPS, S5_STATE, S5_GROUP), 2 * S5_GROUP),
        "s5_c_re": nrm(ks[19], (DEPTH, S5_GROUPS, S5_GROUP, S5_STATE), S5_STATE),
        "s5_c_im": nrm(ks[20], (DEPTH, S5_GROUPS, S5_GROUP, S5_STATE), S5_STATE),
        "s5_d": jax.random.normal(ks[21], (DEPTH, S5_GROUPS, S5_GROUP), f32),
        "s5_w_glu": nrm(ks[22], (DEPTH, S5_WIDTH, S5_WIDTH), S5_WIDTH),
        "s5_b_glu": 0.01 * jax.random.normal(ks[23], (DEPTH, S5_WIDTH), f32),
        "w_out": nrm(ks[24], (DEPTH, D_MODEL, D_MODEL), D_MODEL),
        "norm_ffn2": gain(ks[25], (DEPTH, D_MODEL)),
        "ffn2_w1": nrm(ks[26], (DEPTH, D_MODEL, D_FF), D_MODEL),
        "ffn2_w3": nrm(ks[27], (DEPTH, D_MODEL, D_FF), D_MODEL),
        "ffn2_w2": nrm(ks[28], (DEPTH, D_FF, D_MODEL), D_FF),
        "norm_ple": gain(ks[29], (DEPTH, D_MODEL)),
        "w_ple_gate": nrm(ks[30], (DEPTH, D_MODEL, D_MODEL), D_MODEL),
        "w_ple": nrm(ks[31], (DEPTH, PLE_DIM, D_MODEL), PLE_DIM),
        "norm_final": gain(ks[32], (D_MODEL,)),
    }

def first_block(x, p, norm_ffn1, ffn1_w1, ffn1_w3, ffn1_w2, norm_mix, w_in,
              cmp_pe_k, cmp_pe_v, cmp_wk1, cmp_wk2, cmp_wv1, cmp_wv2,
              s5_a_re, s5_a_im, s5_log_dt, s5_b_re, s5_b_im, s5_c_re, s5_c_im, s5_d,
              s5_w_glu, s5_b_glu, w_out, norm_ffn2, ffn2_w1, ffn2_w3, ffn2_w2,
              norm_ple, w_ple_gate, w_ple, norm_final):
    B, L = x.shape[:2]
    pos = jnp.arange(L, dtype=jnp.float32)
    split_at = [NSA_WIDTH + k * KV_WIDTH for k in range(7)] + [NSA_WIDTH + 6 * KV_WIDTH + 3 * N_HEADS]
    h = x
    for i in range(DEPTH):
        h = h + 0.5 * swiglu(rmsnorm(h, norm_ffn1[i]), ffn1_w1[i], ffn1_w3[i], ffn1_w2[i])
        z = rmsnorm(h, norm_mix[i]) @ w_in[i]
        q, kc, vc, ksl, vsl, kw, vw, g, u = jnp.split(z, split_at, axis=-1)
        kvshape = (B, L, N_KV_HEADS, HEAD_DIM)
        q = rope(q.reshape(B, L, N_HEADS, HEAD_DIM), pos)
        kc = rope(kc.reshape(kvshape), pos)
        ksl = rope(ksl.reshape(kvshape), pos)
        kw = rope(kw.reshape(kvshape), pos)
        gates = jax.nn.sigmoid(g.reshape(B, L, N_HEADS, 3))
        o_nsa = nsa_attention(q, kc, vc.reshape(kvshape), ksl, vsl.reshape(kvshape), kw, vw.reshape(kvshape),
                              gates, cmp_pe_k[i], cmp_pe_v[i], cmp_wk1[i], cmp_wk2[i], cmp_wv1[i], cmp_wv2[i])
        o_s5 = s5_mixer(u, s5_a_re[i], s5_a_im[i], s5_log_dt[i], s5_b_re[i], s5_b_im[i],
                        s5_c_re[i], s5_c_im[i], s5_d[i], s5_w_glu[i], s5_b_glu[i])
        h = h + jnp.concatenate([o_nsa, o_s5], axis=-1) @ w_out[i]
        h = h + 0.5 * swiglu(rmsnorm(h, norm_ffn2[i]), ffn2_w1[i], ffn2_w3[i], ffn2_w2[i])
        gate = jax.nn.sigmoid(rmsnorm(h, norm_ple[i]) @ w_ple_gate[i])
        h = h + gate * (p[i] @ w_ple[i])
    return rmsnorm(h, norm_final)


DEPTH_2 = 2

CTX_LEN = 256
GRID_W = 64
N_BRANCH = 3
BRANCH_W = D_MODEL // 2
RET_HEADS = 4
RET_DK = BRANCH_W // RET_HEADS
DIFF_HEADS = 4
DIFF_DV = BRANCH_W // DIFF_HEADS
DIFF_DQK = DIFF_DV // 2
MLP_GROUPS = 4
MLP_GW = BRANCH_W // MLP_GROUPS
CHUNK = 128
RET_CHUNK = 128
ROPE_BASE = 10000.0
EPS = 1e-6
KV_SIZES = (BRANCH_W, BRANCH_W, BRANCH_W, BRANCH_W)
REST_SIZES = (BRANCH_W,) * 7 + (N_BRANCH * D_MODEL,)
IN_SIZES = KV_SIZES + REST_SIZES
KV_COLS = 4 * BRANCH_W
IN_COLS_2 = KV_COLS + 7 * BRANCH_W + N_BRANCH * D_MODEL


def rms_norm(x, g=None):
    xf = x.astype(jnp.float32)
    y = xf * lax.rsqrt(jnp.mean(xf * xf, axis=-1, keepdims=True) + EPS)
    if g is not None:
        y = y * g.astype(jnp.float32)
    return y.astype(x.dtype)

def layer_norm(x):
    xf = x.astype(jnp.float32)
    mu = jnp.mean(xf, axis=-1, keepdims=True)
    var = jnp.mean(jnp.square(xf - mu), axis=-1, keepdims=True)
    return ((xf - mu) * lax.rsqrt(var + EPS)).astype(x.dtype)

def modulate(x, g, shift, scale):
    return rms_norm(x, g) * (1.0 + scale) + shift

def split_cols(z, sizes):
    idx = np.cumsum(sizes)[:-1].tolist()
    return jnp.split(z, idx, axis=-1)

def to_heads(t, n_heads):
    b, n, w = t.shape
    return t.reshape(b, n, n_heads, w // n_heads).transpose(0, 2, 1, 3)

def to_diff_heads(t):
    b, n, _ = t.shape
    return t.reshape(b, n, DIFF_HEADS, 2, DIFF_DQK).transpose(0, 2, 3, 1, 4)

def from_heads(t):
    b, h, n, d = t.shape
    return t.transpose(0, 2, 1, 3).reshape(b, n, h * d)

def rope_angles(row_pos, col_pos, head_dim):
    n_freq = head_dim // 4
    inv = ROPE_BASE ** (-jnp.arange(n_freq, dtype=jnp.float32) / n_freq)
    ang = jnp.concatenate([row_pos[:, None] * inv, col_pos[:, None] * inv], axis=-1)
    return jnp.cos(ang), jnp.sin(ang)

def apply_rope(x, cos, sin):
    x1, x2 = jnp.split(x, 2, axis=-1)
    cos = cos.astype(x.dtype)
    sin = sin.astype(x.dtype)
    return jnp.concatenate([x1 * cos - x2 * sin, x1 * sin + x2 * cos], axis=-1)

def retention_chunkwise(q, k, v, log_gamma, state0):
    in_dtype = q.dtype
    q, k, v = q.astype(jnp.float32), k.astype(jnp.float32), v.astype(jnp.float32)
    b, h, n, dk = q.shape
    dv = v.shape[-1]
    nc = n // RET_CHUNK
    qc = q.reshape(b, h, nc, RET_CHUNK, dk)
    kc = k.reshape(b, h, nc, RET_CHUNK, dk)
    vc = v.reshape(b, h, nc, RET_CHUNK, dv)
    pos = jnp.arange(RET_CHUNK, dtype=jnp.float32)
    lg = log_gamma.astype(jnp.float32)[:, None]
    dist = pos[:, None] - pos[None, :]
    d_in = jnp.where(dist >= 0, jnp.exp(lg[:, :, None] * jnp.maximum(dist, 0.0)), 0.0)
    q_dec = jnp.exp(lg * (pos + 1.0))
    k_dec = jnp.exp(lg * (RET_CHUNK - 1.0 - pos))
    chunk_dec = jnp.exp(lg[:, 0] * RET_CHUNK)
    s = jnp.einsum('bhnid,bhnjd->bhnij', qc, kc) * d_in[None, :, None]
    inner = jnp.einsum('bhnij,bhnje->bhnie', s, vc)
    kv = jnp.einsum('bhnjd,hj,bhnje->bhnde', kc, k_dec, vc)

    def step(state, kv_n):
        return chunk_dec[None, :, None, None] * state + kv_n, state

    final, prev = lax.scan(step, state0.astype(jnp.float32), jnp.moveaxis(kv, 2, 0))
    prev = jnp.moveaxis(prev, 0, 2)
    cross = jnp.einsum('bhnid,hi,bhnde->bhnie', qc, q_dec, prev)
    out = (inner + cross).reshape(b, h, n, dv)
    return out.astype(in_dtype), final

def retention_final_state(k, v, log_gamma):
    n = k.shape[2]
    w = jnp.exp(log_gamma[:, None] * (n - 1.0 - jnp.arange(n, dtype=jnp.float32)))
    return jnp.einsum('bhjd,hj,bhje->bhde', k.astype(jnp.float32), w, v.astype(jnp.float32))

def bidir_retention(q, k, v, log_gamma, state_f, state_b):
    out_f, fin_f = retention_chunkwise(q, k, v, log_gamma[0], state_f)
    out_b, fin_b = retention_chunkwise(jnp.flip(q, 2), jnp.flip(k, 2), jnp.flip(v, 2), log_gamma[1], state_b)
    return out_f + jnp.flip(out_b, 2), fin_f, fin_b

def diff_attend(q, k, v, lam):
    s = jnp.einsum('bhmqd,bhmkd->bhmqk', q.astype(jnp.float32), k.astype(jnp.float32)) * (DIFF_DQK ** -0.5)
    p = jax.nn.softmax(s, axis=-1)
    a = p[:, :, 0] - lam * p[:, :, 1]
    return jnp.einsum('bhqk,bhkv->bhqv', a, v.astype(jnp.float32)).astype(v.dtype)

def diff_attend_blocked(q, k, v, lam):
    b, h, _, n, d = q.shape
    nb = n // Q_BLOCK
    qb = jnp.moveaxis(q.reshape(b, h, 2, nb, Q_BLOCK, d), 3, 0)
    o = lax.map(lambda blk: diff_attend(blk, k, v, lam), qb)
    return jnp.moveaxis(o, 0, 2).reshape(b, h, n, -1)

def chunk_mlp(u, v, gate, w_s, b_s):
    b, n, _ = u.shape
    nch = n // CHUNK
    vn = layer_norm(v).reshape(b, nch, CHUNK, MLP_GROUPS, MLP_GW)
    sp = jnp.einsum('gij,bnjgc->bnigc', w_s, vn) + b_s.T[:, :, None]
    return u * sp.reshape(b, n, BRANCH_W) * jax.nn.silu(gate)

def merge_branches(o_ret, o_mlp, o_diff, merge_logits, w_bo, w_o):
    g_ret, g_mlp, g_diff = jnp.split(jax.nn.sigmoid(merge_logits), N_BRANCH, axis=-1)
    y = g_ret * (o_ret @ w_bo[0]) + g_mlp * (o_mlp @ w_bo[1]) + g_diff * (o_diff @ w_bo[2])
    return y @ w_o

def second_inputs(seed: int = 0) -> dict:
    key = jax.random.key(seed)
    ks = jax.random.split(key, 16)
    f32 = jnp.float32
    nrm = jax.random.normal
    x = nrm(ks[0], (BATCH, SEQ, D_MODEL), f32)
    c = nrm(ks[1], (BATCH, D_MODEL), f32)
    ctx = nrm(ks[2], (BATCH, CTX_LEN, D_MODEL), f32)
    c_ctx = nrm(ks[3], (D_MODEL,), f32)
    w_mod = nrm(ks[4], (DEPTH_2, D_MODEL, 3 * D_MODEL), f32) * (0.5 * D_MODEL ** -0.5)
    b_mod = 0.02 * nrm(ks[5], (DEPTH_2, 3 * D_MODEL), f32)
    g_pre = 1.0 + 0.05 * nrm(ks[6], (DEPTH_2, D_MODEL), f32)
    g_post = 1.0 + 0.05 * nrm(ks[7], (DEPTH_2, D_MODEL), f32)
    w_in = nrm(ks[8], (DEPTH_2, D_MODEL, IN_COLS_2), f32) * (D_MODEL ** -0.5)
    base = jnp.log(2.0 ** (5.0 + jnp.arange(RET_HEADS, dtype=f32)) - 1.0)
    ret_decay_logit = base[None, None, :] + 0.1 * nrm(ks[9], (DEPTH_2, 2, RET_HEADS), f32)
    mlp_w_s = nrm(ks[10], (DEPTH_2, MLP_GROUPS, CHUNK, CHUNK), f32) * (CHUNK ** -0.5)
    mlp_b_s = 1.0 + 0.1 * nrm(ks[11], (DEPTH_2, MLP_GROUPS, CHUNK), f32)
    diff_lambda_q = 0.1 * nrm(ks[12], (DEPTH_2, 2, DIFF_DQK), f32)
    diff_lambda_k = 0.1 * nrm(ks[13], (DEPTH_2, 2, DIFF_DQK), f32)
    w_branch_out = nrm(ks[14], (DEPTH_2, N_BRANCH, BRANCH_W, D_MODEL), f32) * (BRANCH_W ** -0.5)
    w_out = nrm(ks[15], (DEPTH_2, D_MODEL, D_MODEL), f32) * (D_MODEL ** -0.5)
    return {"x": x, "c": c, "ctx": ctx, "c_ctx": c_ctx, "w_mod": w_mod, "b_mod": b_mod,
            "g_pre": g_pre, "g_post": g_post, "w_in": w_in, "ret_decay_logit": ret_decay_logit,
            "mlp_w_s": mlp_w_s, "mlp_b_s": mlp_b_s, "diff_lambda_q": diff_lambda_q,
            "diff_lambda_k": diff_lambda_k, "w_branch_out": w_branch_out, "w_out": w_out}

def second_block(x, c, ctx, c_ctx, w_mod, b_mod, g_pre, g_post, w_in, ret_decay_logit,
              mlp_w_s, mlp_b_s, diff_lambda_q, diff_lambda_k, w_branch_out, w_out):
    b = x.shape[0]
    n_lat = x.shape[1]
    rows = n_lat // GRID_W
    row_pos = jnp.repeat(jnp.arange(rows, dtype=jnp.float32), GRID_W)
    col_pos = jnp.tile(jnp.arange(GRID_W, dtype=jnp.float32), rows)
    cos_r, sin_r = rope_angles(row_pos, col_pos, RET_DK)
    cos_d, sin_d = rope_angles(row_pos, col_pos, DIFF_DQK)
    silu_c = jax.nn.silu(c)
    silu_cc = jax.nn.silu(c_ctx)
    ret_scale = RET_DK ** -0.5

    for l in range(DEPTH_2):
        last = l == DEPTH_2 - 1
        shift, scale, gate = jnp.split((silu_c @ w_mod[l] + b_mod[l])[:, None, :], 3, axis=-1)
        shift_c, scale_c, gate_c = jnp.split(silu_cc @ w_mod[l] + b_mod[l], 3, axis=-1)
        h = modulate(x, g_pre[l], shift, scale)
        hc = modulate(ctx, g_pre[l], shift_c, scale_c)
        log_gamma = -jax.nn.softplus(-ret_decay_logit[l].astype(jnp.float32))
        lam_init = 0.8 - 0.6 * math.exp(-0.3 * l)
        lam = (jnp.exp(jnp.sum(diff_lambda_q[l, 0] * diff_lambda_k[l, 0]))
               - jnp.exp(jnp.sum(diff_lambda_q[l, 1] * diff_lambda_k[l, 1])) + lam_init).astype(jnp.float32)

        if last:
            c_rk, c_rv, c_dk, c_dv = split_cols(hc @ w_in[l][:, :KV_COLS], KV_SIZES)
        else:
            zc = split_cols(hc @ w_in[l], IN_SIZES)
            c_rk, c_rv, c_dk, c_dv = zc[:4]
        crk = to_heads(c_rk, RET_HEADS) * ret_scale
        crv = to_heads(c_rv, RET_HEADS)
        cdk = to_diff_heads(c_dk)
        cdv = to_heads(c_dv, DIFF_HEADS)
        if last:
            s_f = retention_final_state(crk, crv, log_gamma[0])
            s_b = retention_final_state(jnp.flip(crk, 2), jnp.flip(crv, 2), log_gamma[1])
        else:
            c_rq, c_rg, c_dq, c_dg, c_mu, c_mv, c_mg, c_mlog = zc[4:]
            zero = jnp.zeros((b, RET_HEADS, RET_DK, RET_DK), jnp.float32)
            c_ret, s_f, s_b = bidir_retention(to_heads(c_rq, RET_HEADS), crk, crv, log_gamma, zero, zero)
            co_ret = from_heads(rms_norm(c_ret)) * jax.nn.silu(c_rg)
            c_diff = diff_attend(to_diff_heads(c_dq), cdk, cdv, lam)
            co_diff = from_heads(rms_norm(c_diff) * (1.0 - lam_init)) * jax.nn.silu(c_dg)
            co_mlp = chunk_mlp(c_mu, c_mv, c_mg, mlp_w_s[l], mlp_b_s[l])
            c_out = merge_branches(co_ret, co_mlp, co_diff, c_mlog, w_branch_out[l], w_out[l])
            ctx_next = ctx + gate_c * rms_norm(c_out, g_post[l])

        rk_, rv_, dk_, dv_, rq_, rg_, dq_, dg_, mu_, mv_, mg_, mlog_ = split_cols(h @ w_in[l], IN_SIZES)
        rq = apply_rope(to_heads(rq_, RET_HEADS), cos_r, sin_r)
        rk = apply_rope(to_heads(rk_, RET_HEADS), cos_r, sin_r) * ret_scale
        rv = to_heads(rv_, RET_HEADS)
        ret_o, _, _ = bidir_retention(rq, rk, rv, log_gamma, s_f, s_b)
        o_ret = from_heads(rms_norm(ret_o)) * jax.nn.silu(rg_)

        dq = apply_rope(to_diff_heads(dq_), cos_d, sin_d)
        dk = apply_rope(to_diff_heads(dk_), cos_d, sin_d)
        dv = to_heads(dv_, DIFF_HEADS)
        k_all = jnp.concatenate([cdk, dk], axis=3)
        v_all = jnp.concatenate([cdv, dv], axis=2)
        diff_o = diff_attend_blocked(dq, k_all, v_all, lam)
        o_diff = from_heads(rms_norm(diff_o) * (1.0 - lam_init)) * jax.nn.silu(dg_)

        o_mlp = chunk_mlp(mu_, mv_, mg_, mlp_w_s[l], mlp_b_s[l])
        out = merge_branches(o_ret, o_mlp, o_diff, mlog_, w_branch_out[l], w_out[l])
        x = x + gate * rms_norm(out, g_post[l])
        if not last:
            ctx = ctx_next
    return x


def setup_inputs(seed=0):
    out = dict(first_inputs(seed))
    for name, value in second_inputs(seed + 1).items():
        if name != "x":
            out[name + "_2"] = value
    return out


def reference(
    x, p, norm_ffn1, ffn1_w1, ffn1_w3, ffn1_w2, norm_mix, w_in, cmp_pe_k, cmp_pe_v, cmp_wk1,
    cmp_wk2, cmp_wv1, cmp_wv2, s5_a_re, s5_a_im, s5_log_dt, s5_b_re, s5_b_im, s5_c_re, s5_c_im,
    s5_d, s5_w_glu, s5_b_glu, w_out, norm_ffn2, ffn2_w1, ffn2_w3, ffn2_w2, norm_ple, w_ple_gate,
    w_ple, norm_final, c_2, ctx_2, c_ctx_2, w_mod_2, b_mod_2, g_pre_2, g_post_2, w_in_2,
    ret_decay_logit_2, mlp_w_s_2, mlp_b_s_2, diff_lambda_q_2, diff_lambda_k_2, w_branch_out_2,
    w_out_2,
):
    x = first_block(
        x, p, norm_ffn1, ffn1_w1, ffn1_w3, ffn1_w2, norm_mix, w_in, cmp_pe_k, cmp_pe_v, cmp_wk1,
        cmp_wk2, cmp_wv1, cmp_wv2, s5_a_re, s5_a_im, s5_log_dt, s5_b_re, s5_b_im, s5_c_re,
        s5_c_im, s5_d, s5_w_glu, s5_b_glu, w_out, norm_ffn2, ffn2_w1, ffn2_w3, ffn2_w2,
        norm_ple, w_ple_gate, w_ple, norm_final,
    )
    return second_block(
        x, c_2, ctx_2, c_ctx_2, w_mod_2, b_mod_2, g_pre_2, g_post_2, w_in_2, ret_decay_logit_2,
        mlp_w_s_2, mlp_b_s_2, diff_lambda_q_2, diff_lambda_k_2, w_branch_out_2, w_out_2,
    )


_drawn_inputs = setup_inputs


def setup_inputs(seed=0):
    import zlib

    import numpy as np

    out = dict(_drawn_inputs(seed))
    spreads = {}
    factors = {'norm_mix': 3.14,
     'cmp_pe_k': 8.0,
     'cmp_pe_v': 2.784,
     's5_a_re': 8.0,
     's5_a_im': 2.718,
     's5_log_dt': 2.754,
     's5_b_re': 3.87,
     's5_b_im': 3.838,
     's5_c_re': 3.842,
     's5_c_im': 3.794,
     's5_b_glu': 8.0,
     'norm_ffn2': 2.827,
     'norm_ple': 6.127,
     'g_post_2': 2.675,
     'diff_lambda_q_2': 4.123,
     'diff_lambda_k_2': 8.0}
    for name, (base, spread) in spreads.items():
        noise = np.random.default_rng([zlib.crc32(name.encode()), seed]).standard_normal(out[name].shape)
        drawn = base * np.exp(spread * noise) if base else spread * noise
        out[name] = jnp.asarray(drawn.astype(out[name].dtype))
    for name, factor in factors.items():
        out[name] = (out[name] * factor).astype(out[name].dtype)
    return out
```

```python
from contextlib import ExitStack

import numpy as np

import concourse.bass as bass
from concourse import mybir

ACT = mybir.ActivationFunctionType
ALU = mybir.AluOpType
AX_X = mybir.AxisListType.X
F32 = mybir.dt.float32
I32 = mybir.dt.int32
BF16 = mybir.dt.bfloat16

P = 128
AREA = 29500
D = 1024
KT = D // P
T = 256
TT = T // P
FF = 2816
FT = FF // P
UW = 1024
RING = 4
HEADS, HD = 8, 64
NCMP, CLEN, CSTR = 15, 32, 16
NST = 16
BW = 512
EPS = 1e-6
NEG = -1e30
LAYERS = 2
LAM_INIT = [0.8 - 0.6 * float(np.exp(-0.3 * l)) for l in range(LAYERS)]
INV2PI = float(np.float32(1.0 / (2.0 * np.pi)))
TWO_PI = float(np.nextafter(np.float32(2.0 * np.pi), np.float32(0.0)))
PI2_HI = 6.28125
PI2_LO = float(np.float32(2.0 * np.pi - 6.28125))
MAGIC = float(np.float32(1.5 * 2 ** 23))
LOG2E = float(np.float32(np.log2(np.e)))
LN2_HI = 0.693359375
LN2_LO = float(np.float32(np.log(2.0) - 0.693359375))
TAYLOR = [1.0 / 5040, 1.0 / 720, 1.0 / 120, 1.0 / 24, 1.0 / 6, 0.5, 1.0]


def stream_plan():
    names = []

    def ffn(tag):
        names.extend([(tag, "w1", 0), (tag, "w3", 0)])
        for f in range(FT - 1):
            names.extend([(tag, "w1", f + 1), (tag, "w3", f + 1), (tag, "w2", f)])
        names.append((tag, "w2", FT - 1))

    ffn("ffn1")
    names.extend([("u", j) for j in range(4)] + [("kc",), ("vc",)])
    names.extend([("q", j) for j in range(4)] + [("ks",), ("kw",)])
    names.extend([("vg", c) for c in range(3)])
    names.extend([("cmpk", c) for c in range(4)] + [("cmpv", c) for c in range(4)])
    names.extend([("mod", l, f) for l in range(LAYERS) for f in range(3 * KT)])
    names.extend([("glu", c) for c in range(2)])
    names.extend([("wout", j) for j in range(KT)])
    ffn("ffn2")
    names.extend([("plew", c) for c in range(2)] + [("pleg", j) for j in range(KT)])
    for l in range(LAYERS):
        for part in ("dk", "dq"):
            names.extend([(part, l, j) for j in range(4)])
        names.extend([("dv", l, c) for c in range(4)])
        names.extend([("dg", l, j) for j in range(4)])
        for part in ("rk", "rq"):
            names.extend([(part, l, j) for j in range(4)])
        names.extend([("rv", l, c) for c in range(4)])
        names.extend([("rg", l, j) for j in range(4)])
        names.extend([("mv", l, c) for c in range(4)])
        names.extend([(part, l, j) for part in ("mu", "mg") for j in range(4)])
        for f in range(KT):
            names.extend([("mlog", l, b, f) for b in range(3)] + [("wbo", l, f, 0), ("wbo", l, f, 1)])
        names.extend([("wo", l, j) for j in range(KT)])
    return names


UNITS = stream_plan()
UNIT = {name: i for i, name in enumerate(UNITS)}
NU = len(UNITS)

PACK = [
    ("g_ffn1", 8), ("g_mix", 8), ("g_ffn2", 8), ("g_ple", 8), ("g_final", 8), ("g_pre", 16), ("g_post", 16),
    ("b_mod", 48), ("a_re", 16), ("a_im", 16), ("log_dt", 16), ("s5_d", 4), ("b_glu", 4), ("b_re", 512),
    ("b_im", 512), ("c_re", 512), ("c_im", 512), ("pe", 32), ("w2k", 128), ("w2v", 128), ("cc", 16),
    ("lamq", 256), ("lamk", 256), ("ret_logit", 16), ("wsT", 1024), ("pT", 512),
    ("ident", 128), ("ones", 128), ("rot64", 128), ("rot128", 128), ("cos1", 256), ("sin1", 256),
    ("cosr", 256), ("sinr", 256), ("cosd", 256), ("sind", 256), ("causal", 128), ("cmask", 32), ("cneg", 32),
    ("gmask", 2), ("steps", 256), ("dist", 512), ("jrow", 4),
]
OFF = {}
for _name, _n in PACK:
    OFF[_name] = (sum(n for _, n in PACK[: len(OFF)]), _n)
NPK = sum(n for _, n in PACK)

BANK_USES = (
    [(("u", j), "act") for j in range(4)] + [(("kc",), "act"), (("vc",), "act")]
    + [(("q", j), "act") for j in range(4)] + [(("ks",), "act"), (("kw",), "act")]
    + [(("vg", t), "act") for t in range(2)]
    + [(("glu", j), "act") for j in range(4)]
    + [(("wout", j), "dve") for j in range(KT)]
)
BANK_USES += [(("plew", _j), "act") for _j in range(4)] + [(("pleg", _j), "act") for _j in range(KT)]
for _l in range(LAYERS):
    for _p in ("d", "r"):
        for _part in (_p + "k", _p + "q"):
            BANK_USES += [((_part, _l, j), "act") for j in range(4)]
        BANK_USES += [((_p + "v", _l, t), "act") for t in range(4)]
        BANK_USES += [((_p + "g", _l, j), "act") for j in range(4)]
    BANK_USES += [(("mv", _l, t), "dve") for t in range(4 if _l == 0 else 2)]
    BANK_USES += [((part, _l, j), "act") for part in ("mu", "mg") for j in range(4)]
    for _f in range(KT):
        BANK_USES += [(("mlog", _l, _b, _f), "act") for _b in range(3)]
        BANK_USES += [(("wbo", _l, _b, _f), "dve") for _b in range(3)]
    BANK_USES += [(("wo", _l, j), "act") for j in range(KT)]
BANK = {}
_taken = {"act": 0, "dve": 0}
for _n, (_name, _eng) in enumerate(BANK_USES):
    _taken[_eng] += 1
    BANK[_name] = (_n % 4, _n, _eng, _taken[_eng])


NORMED = [0, 8, 16, 24]
RESID_BLOCK2 = 4 + 4 + KT + KT
DIFF = [[(st, hh, qt) for st in streams for hh in range(4) for qt in range(2)] for streams in ((0, 1), (0,))]
RET = [[(st, hh) for st in streams for hh in range(4)] for streams in ((0, 1), (0,))]
DIFF_AT = [0, len(DIFF[0]), len(DIFF[0]) + len(DIFF[1])]
HEAD_AT = [n // 2 for n in DIFF_AT]
RET_AT = [0, len(RET[0]), len(RET[0]) + len(RET[1])]
VN_AT = [0, 4, 6]
ROPES = {(part, l): 4 * l + n for l in range(LAYERS) for n, part in enumerate(("dk", "dq", "rk", "rq"))}


def slot_units(l):
    return [(part, l, j) for part in ("rk", "rq", "rv", "rg", "mv", "mu", "mg") for j in range(4)]


def head_steps(l):
    slots = [[] for _ in slot_units(l)]
    for hh in range(4):
        slots[hh].append(("tables", hh))
    for step in range(len(DIFF[l]) + 2):
        slots[step // 2 if l == 0 else step].append(("diff", step))
    slots[11].append(("rot", "rk"))
    slots[12].append(("rot", "rq"))
    for step in range(len(RET[l]) + 2):
        slots[16 + step].append(("ret", step))
    return slots


SLOTS = [head_steps(l) for l in range(LAYERS)]


def two_block_kernel(nc, stream, pack, bs_rows, x_in, ctx_in, out):
    with ExitStack() as es:
        def sb(name, shape, dt=F32):
            return es.enter_context(nc.sbuf_tensor(name, shape, dt))

        def sem(name):
            return es.enter_context(nc.semaphore(name))

        pk = sb("pk", [P, NPK])

        def c(name, a=0, b=None):
            off, n = OFF[name]
            return pk[:, off + a:off + (n if b is None else b)]

        ring = sb("ring", [P, RING, UW])
        bsrow = sb("bsrow", [1, 2 * BW])
        h = sb("h", [P, KT, T])
        hc = sb("hc", [P, KT, T])
        hn = sb("hn", [P, KT, 2 * T])
        lnr = sb("lnr", [P, 2 * T])
        rstd = sb("rstd", [P, 2 * T])
        eps = sb("eps", [P, 1])
        negc = sb("negc", [P, P], BF16)
        idb = sb("idb", [P, P], BF16)
        cs = sb("cs", [P, KT, 2])
        mods = sb("mods", [P, LAYERS, 3 * KT, 2])
        amp = sb("amp", [P, LAYERS, KT, 2])
        pgate = sb("pgate", [P, LAYERS, KT, 2])
        area = sb("area", [P, AREA])

        class Area:
            at = 0

        def cut(*shape):
            n = int(np.prod(shape))
            v = area[:, Area.at:Area.at + n]
            Area.at += n
            if len(shape) == 2:
                v = v.rearrange("p (a b) -> p a b", a=shape[0])
            if len(shape) == 3:
                v = v.rearrange("p (a b c) -> p a b c", a=shape[0], b=shape[1])
            return v

        sil = cut(4, T)
        hid = cut(4, T)
        sq = cut(KT, 2 * T)
        yg = sil
        costab = cut(NST, T)
        sintab = cut(NST, T)
        uT = cut(4, T)
        bT = cut(2, 4, P)
        cneg_re = cut(512)
        cneg_im = cut(512)
        s5v = cut(24, NST)
        zq = cut(7, T)
        vcT = cut(T)
        vtok = cut(2, 280)
        gates = cut(2, 24)
        blk = cut(2, 16 * 32)
        ghid = cut(2, 2 * 32)
        grep = cut(2, P)
        kbd = cut(32)
        vbd = cut(P)
        csc = cut(2 * P)
        cex = cut(2 * P)
        cst = cut(4, NST)
        pct = cut(2 * P)
        exprob = cut(2, 2, 384)
        ex, prob = exprob[:, 0, :, :], exprob[:, 1, :, :]
        bre, bim = (exprob[:, n, :, :].rearrange("p a b -> p (a b)")[:, 0:512] for n in range(2))
        pt = cut(2, 384)
        stat = cut(2, 16)
        bakA = cut(2, 2 * T)
        bakB = cut(2, 2 * T)
        oT = cut(KT, T)
        rotA, rotB, zin, wst = (sq[:, 2 * n:2 * n + 2, :] for n in range(4))
        sg = hid
        pwp = costab
        plg = sintab
        assert Area.at <= AREA, Area.at
        Area.at = 0
        diffz = cut(12, 2 * T)
        diffv = cut(4, BW)
        retz = cut(12, 2 * T)
        retv = cut(4, BW)
        mlpu = cut(8, 2 * T)
        dmat = cut(4, 2 * T)
        aux = cut(10, 2 * T)
        lay = cut(LAYERS, 40)
        st2 = cut(2, 16)
        states = cut(2, 4, P)
        ktok = cut(2, 2, P)
        sp = cut(4, 16)
        assert Area.at <= AREA, Area.at
        o_dif, o_ret, o_mlp = diffz[:, 8:12, :], retz[:, 8:12, :], mlpu[:, 0:4, :]
        ymrg = retz
        sq2 = aux
        vn = diffv
        unnormed = diffz

        ps = es.enter_context(nc.psum_tensor("ps", [P, 8 * 512], F32))

        def bank(b, a=0, n=512):
            return ps[:, 512 * b + a:512 * b + a + n]

        consts_loaded = sem("consts_loaded")
        unit_loaded = [sem(f"unit_loaded{s}") for s in range(RING)]
        units_multiplied = sem("units_multiplied")
        act_evac = sem("act_evac")
        dve_evac = sem("dve_evac")
        dve_step = sem("dve_step")
        act_step = sem("act_step")
        pool_step = sem("pool_step")
        squares_ready = sem("squares_ready")
        sumsq_ready = sem("sumsq_ready")
        rstd_ready = sem("rstd_ready")
        scaled_ready = sem("scaled_ready")
        normed_ready = sem("normed_ready")
        silu_ready = sem("silu_ready")
        hidden_ready = sem("hidden_ready")
        resid_ready = sem("resid_ready")
        masks_ready = sem("masks_ready")
        cs_ready = sem("cs_ready")
        mods_ready = sem("mods_ready")
        stored = sem("stored")
        S = {}

        def s(name):
            if name not in S:
                S[name] = sem(name)
            return S[name]

        EV = {"act": act_evac, "dve": dve_evac}

        def wait_taken(eng, name):
            _, _, who, count = BANK[name]
            eng.wait_ge(EV[who], count)

        def bank_free(pe, name):
            n = BANK[name][1]
            if n >= 4:
                wait_taken(pe, BANK_USES[n - 4][0])

        def product(eng, *name):
            eng.wait_ge(units_multiplied, UNIT[name] + 1)

        NC_DMAS = 4
        block = es.enter_context(nc.Block())

        @block.sync
        def _(sp):
            sp.dma_start(h[:, :, :], x_in).then_inc(consts_loaded, 16)
            sp.dma_start(pk[:, :], pack).then_inc(consts_loaded, 16)
            for u in range(RING):
                sp.dma_start(ring[:, u, :], stream[u]).then_inc(unit_loaded[u], 16)
            sp.dma_start(hc[:, :, :], ctx_in).then_inc(consts_loaded, 16)
            sp.dma_start(bsrow[:, :], bs_rows).then_inc(consts_loaded, 16)
            rounds = NU // RING
            with sp.Fori(1, rounds) as r:
                for u in range(RING):
                    sp.wait_ge(units_multiplied, RING * r + (u + 1 - RING))
                    sp.dma_start(ring[:, u, :], stream[RING * r + u]).then_inc(unit_loaded[u], 16)
            for u in range(rounds * RING, NU):
                sp.wait_ge(units_multiplied, u + 1 - RING)
                sp.dma_start(ring[:, u % RING, :], stream[u]).then_inc(unit_loaded[u % RING], 16)
            sp.wait_ge(resid_ready, RESID_BLOCK2 + LAYERS * KT)
            sp.dma_start(out, h[:, :, :]).then_inc(stored, 16)
            sp.wait_ge(stored, 16)

        @block.tensor
        def _(pe):
            def unit(name, rounds=0):
                u = UNIT[name]
                pe.wait_ge(unit_loaded[u % RING], 16 * (u // RING + 1) + 16 * rounds)
                return ring[:, u % RING, :]

            def sumsq(n, tokens):
                for k in range(KT):
                    pe.wait_ge(squares_ready, KT * n + k + 1)
                    src = (sq if n < 5 else sq2)[:, k, 0:tokens]
                    m = pe.matmul(bank(7, 0, tokens), c("ones"), src, start=(k == 0), stop=(k == KT - 1))
                m.then_inc(sumsq_ready, 1)

            def ffn(tag, n_norm, n_ffn):
                sumsq(n_norm, T)

                def up(f, rounds=0):
                    for half, w in enumerate(("w1", "w3")):
                        wt = unit((tag, w, f), rounds)
                        for k in range(KT):
                            if f == 0 and half == 0:
                                pe.wait_ge(normed_ready, NORMED[n_norm] + k + 1)
                            m = pe.matmul(bank(4 + f % 4, T * half, T), wt[:, P * k:P * k + P], hn[:, k, 0:T],
                                          start=(k == 0 and half == 0), stop=(k == KT - 1), skip_group_check=True)
                        m.then_inc(units_multiplied, 1)

                def down(f, rounds=0, hidden=0):
                    wt = unit((tag, "w2", f), rounds)
                    pe.wait_ge(hidden_ready, FT * n_ffn + f + 1 + hidden)
                    for j in range(KT):
                        m = pe.matmul(bank(j // 2, T * (j % 2), T), wt[:, P * j:P * j + P], hid[:, f % 4, :],
                                      start=(f == 0 and j % 2 == 0), stop=(f == FT - 1), skip_group_check=True)
                    m.then_inc(units_multiplied, 1)

                up(0)
                up(1)
                down(0)
                with pe.Fori(0, (FT - 2) // 4) as it:
                    for f in range(1, 5):
                        up(f + 1, 3 * it)
                        down(f, 3 * it, 4 * it)
                down(FT - 1)

            pe.wait_ge(consts_loaded, 16 * NC_DMAS)
            ffn("ffn1", 0, 0)
            pe.wait_ge(s("s5_b_ready"), 2)
            for part, src in enumerate((bre, bim)):
                for j in range(4):
                    m = pe.transpose(bank(4 + part, P * j, P), src[:, P * j:P * j + P], c("ident"))
            m.then_inc(s("s5_bt"), 1)

            sumsq(1, T)

            def project(name, first=False, tokens=T, cols=None, n_norm=0, kt=KT, src=None):
                wt = unit(name)
                bank_free(pe, name)
                b = BANK[name][0]
                for k in range(kt):
                    if first:
                        pe.wait_ge(normed_ready, NORMED[n_norm] + k + 1)
                    m = pe.matmul(bank(b, 0, tokens), wt[:, P * k:P * k + P], (hn if src is None else src)[:, k, 0:tokens],
                                  start=(k == 0), stop=(k == kt - 1))
                m.then_inc(units_multiplied, 1)

            for j in range(4):
                project(("u", j), first=(j == 0), n_norm=1)
            project(("kc",))
            project(("vc",))

            def rotate(src, dst, rot, who, count):
                pe.wait_ge(who, count)
                return pe.matmul(dst, c(rot), src, start=True, stop=True)

            for j in range(4):
                project(("q", j))
            project(("ks",))
            project(("kw",))
            for cc_ in range(3):
                wt = unit(("vg", cc_))
                for tt in range(2):
                    if cc_ == 0:
                        bank_free(pe, ("vg", tt))
                    for k in range(3 * cc_, min(3 * cc_ + 3, KT)):
                        m = pe.matmul(bank(BANK["vg", tt][0], 0, 280), hn[:, k, P * tt:P * tt + P],
                                      wt[:, 280 * (k - 3 * cc_):280 * (k - 3 * cc_) + 280],
                                      start=(k == 0), stop=(k == KT - 1), skip_group_check=True)
                m.then_inc(units_multiplied, 1)
            for n in range(7):
                wait_taken(pe, [("q", 0), ("q", 1), ("q", 2), ("q", 3), ("ks",), ("kw",), ("kc",)][n])
                m = pe.matmul(ps[:, 4 * 512 + T * n:4 * 512 + T * n + T], c("rot64"), zq[:, n, :],
                              start=(n % 2 == 0), stop=True, skip_group_check=True)
            m.then_inc(s("rotated"), 1)
            for kv, tag in enumerate(("cmpk", "cmpv")):
                for cc_ in range(4):
                    wt = unit((tag, cc_))
                    if cc_ == 0:
                        pe.wait_ge(s("blk_ready"), kv + 1)
                    for lp in range(4 * cc_, 4 * cc_ + 4):
                        for ht in range(2):
                            m = pe.matmul(bank(kv, 32 * ht, 32), wt[:, 256 * (lp % 4) + P * ht:256 * (lp % 4) + P * ht + P],
                                          blk[:, kv, 32 * lp:32 * lp + 32], start=(lp == 0 and ht == 0),
                                          stop=(lp == 15), skip_group_check=True)
                    m.then_inc(units_multiplied, 1)
            pe.wait_ge(s("ghid_ready"), 1)
            for g in range(2):
                for ht in range(2):
                    m = pe.matmul(ps[HD * g:HD * g + HD, 2 * 512:2 * 512 + 16], c("w2k", HD * ht, HD * ht + HD),
                                  ghid[:, 0, 32 * ht + 16 * g:32 * ht + 16 * g + 16], start=(ht == 0), stop=(ht == 1))
            m.then_inc(s("kcmp"), 1)
            pe.wait_ge(s("grep_ready"), 1)
            for ht in range(2):
                m = pe.matmul(bank(3, 0, HD), grep[:, ht, :], c("w2v", HD * ht, HD * ht + HD), start=(ht == 0), stop=(ht == 1))
            m.then_inc(s("vcmp"), 1)
            pe.wait_ge(s("kbd_ready"), 2)
            pe.wait_ge(s("roped"), 3)
            for qt in range(2):
                for j in range(4):
                    m = pe.matmul(bank(0, P * qt + 32 * j, 32), zq[:, j, P * qt:P * qt + P], kbd, start=True, stop=True)
            m.then_inc(s("cmp_scores"), 1)
            pe.wait_ge(s("cmp_probs"), 1)
            for qt in range(2):
                m = pe.transpose(bank(1, P * qt, P), cex[:, P * qt:P * qt + P], c("ident"))
            m.then_inc(s("cmp_probsT"), 1)
            pe.wait_ge(s("vbd_ready"), 2)
            pe.wait_ge(s("pct_ready"), 1)

            def s5_in(i):
                if i == 0:
                    pe.wait_ge(s("s5_b_copied"), 1)
                    wait_taken(pe, ("u", 3))
                    pe.wait_ge(s("roped"), 3)
                if i >= 1:
                    pe.wait_ge(s("s5_prod"), i)
                rows = slice(32 * (i % 4), 32 * (i % 4) + 32)
                for part in range(2):
                    m = pe.matmul(bank(6, T * part, T), bT[rows, part, i // 4, :], uT[rows, i // 4, :],
                                  start=(part == 0), stop=True, skip_group_check=True)
                m.then_inc(s("s5_bu"), 1)

            def s5_out(i):
                pe.wait_ge(s("s5_back"), 2 * i + 2)
                if i % 4 == 0 and i >= 4:
                    pe.wait_ge(s("s5_y_taken"), i // 4)
                rows = slice(32 * (i % 4), 32 * (i % 4) + 32)
                o = ps[rows, 7 * 512 + T * (i // 4 % 2):7 * 512 + T * (i // 4 % 2) + T]
                cols = slice(32 * i, 32 * i + 32)
                a, b2 = bakA[:, i % 2, :], bakB[:, i % 2, :]
                pe.matmul(o, c("c_re")[:, cols], a[:, 0:T], start=True, stop=False, skip_group_check=True)
                pe.matmul(o, cneg_re[:, cols], b2[:, T:2 * T], start=False, stop=False, skip_group_check=True)
                pe.matmul(o, cneg_im[:, cols], a[:, T:2 * T], start=False, stop=False, skip_group_check=True)
                pe.matmul(o, cneg_im[:, cols], b2[:, 0:T], start=False, stop=True, skip_group_check=True)\
                    .then_inc(s("s5_y"), 1)

            def scores(i):
                if i == 0:
                    pe.wait_ge(masks_ready, 2)
                j, g, br = i // 4, i // 2 % 2, i % 2
                if i >= 2:
                    pe.wait_ge(s("exps"), 2 * (i - 1))
                rows = slice(HD * g, HD * g + HD)
                kk = zq[rows, 4 + br, :]
                o = bank(i % 2)
                pe.matmul(o[:, 0:P], zq[rows, j, 0:P], kk[:, 0:P], start=True, stop=False, skip_group_check=True)
                pe.matmul(o[:, P:3 * P], zq[rows, j, P:2 * P], kk[:, 0:2 * P], start=False, stop=False, skip_group_check=True)
                pe.matmul(o[:, 0:P], idb[:, :], negc[:, :], start=False, stop=True, skip_group_check=True)
                pe.matmul(o[:, 2 * P:3 * P], idb[:, :], negc[:, :], start=False, stop=True, skip_group_check=True)\
                    .then_inc(s("scored"), 1)

            def turn(i):
                pe.wait_ge(s("probs"), 2 * i + 2)
                if i >= 2:
                    pe.wait_ge(s("pt_ready"), i - 1)
                for n in range(3):
                    m = pe.transpose(bank(2 + i % 2, P * n, P), prob[:, i % 2, P * n:P * n + P], c("ident"))
                m.then_inc(s("turned"), 1)

            def weigh(i):
                j, g, br = i // 4, i // 2 % 2, i % 2
                pe.wait_ge(s("pt_ready"), i + 1)
                if i % 4 == 0 and i >= 4:
                    pe.wait_ge(s("o_taken"), j)
                col = 5 * 512 + T * (j % 2)
                rows = slice(HD * g, HD * g + HD)
                if i % 4 == 0:
                    pe.matmul(ps[:, col:col + T], vbd[32 * j:32 * j + 32, :], pct[32 * j:32 * j + 32, :],
                              start=True, stop=False, skip_group_check=True)
                vv = P * br + HD * g
                pe.matmul(ps[rows, col:col + T], vtok[:, 0, vv:vv + HD], pt[:, i % 2, 0:2 * P],
                          start=False, stop=False, skip_group_check=True)
                pe.matmul(ps[rows, col + P:col + T], vtok[:, 1, vv:vv + HD], pt[:, i % 2, 2 * P:3 * P],
                          start=False, stop=(br == 1), skip_group_check=True).then_inc(s("weighed"), 1)

            def modulation(n):
                l, f = divmod(n, 3 * KT)
                wt = unit(("mod", l, f))
                if n == 0:
                    pe.wait_ge(cs_ready, 1)
                    pe.wait_ge(s("roped"), 3)
                for k in range(KT):
                    m = pe.matmul(bank(4, 2 * n, 2), wt[:, P * k:P * k + P], cs[:, k, :], start=(k == 0), stop=(k == KT - 1))
                m.then_inc(units_multiplied, 1)

            for i in range(NST + 2):
                if i < NST:
                    s5_in(i)
                    scores(i)
                    for n in range(3 * i, 3 * i + 3):
                        modulation(n)
                if 1 <= i <= NST:
                    turn(i - 1)
                if 1 <= i <= NST:
                    s5_out(i - 1)
                if i >= 2:
                    weigh(i - 2)
            for cc_ in range(2):
                wt = unit(("glu", cc_))
                for j in (2 * cc_, 2 * cc_ + 1):
                    bank_free(pe, ("glu", j))
                    if j == 0:
                        pe.wait_ge(s("pt_ready"), NST)
                        pe.wait_ge(s("gelu_ready"), 4)
                    for k in range(4):
                        m = pe.matmul(bank(BANK["glu", j][0], 0, T), wt[:, 512 * (j % 2) + P * k:512 * (j % 2) + P * k + P],
                                      yg[:, k, :], start=(k == 0), stop=(k == 3))
                m.then_inc(units_multiplied, 1)
            for j in range(KT):
                if j == 0:
                    pe.wait_ge(s("o_taken"), 4)
                    pe.wait_ge(s("s5_out"), 4)
                project(("wout", j), src=oT)

            ffn("ffn2", 2, 1)
            for cc_ in range(2):
                wt = unit(("plew", cc_))
                for j in range(4):
                    if j % 2 == 0:
                        b = BANK["plew", 2 * cc_ + j // 2][0]
                        if cc_ == 0 and j == 0:
                            pe.wait_ge(resid_ready, 8)
                    for k in range(2):
                        m = pe.matmul(bank(b, T * (j % 2), T), wt[:, P * (2 * j + k):P * (2 * j + k) + P],
                                      c("pT", T * k, T * k + T), start=(k == 0 and j % 2 == 0), stop=(k == 1),
                                      skip_group_check=True)
                m.then_inc(units_multiplied, 1)
            sumsq(3, T)
            for j in range(KT):
                project(("pleg", j), first=(j == 0), n_norm=3)
            sumsq(4, T)

            def project2(name, l, tokens, first=False, src=None):
                wt = unit(name)
                bank_free(pe, name)
                for k in range(KT):
                    if first:
                        pe.wait_ge(s("modulated"), 16 * l + 2 * k + 2)
                    m = pe.matmul(bank(BANK[name][0], 0, tokens), wt[:, P * k:P * k + P],
                                  (hn if src is None else src)[:, k, 0:tokens], start=(k == 0), stop=(k == KT - 1))
                m.then_inc(units_multiplied, 1)

            def project_values(part, l, cc_, tiles):
                wt = unit((part, l, cc_))
                for tt in range(tiles):
                    if cc_ == 0:
                        bank_free(pe, (part, l, tt))
                    for k in range(2):
                        m = pe.matmul(bank(BANK[part, l, tt][0]), hn[:, 2 * cc_ + k, P * tt:P * tt + P],
                                      wt[:, BW * k:BW * k + BW], start=(cc_ == 0 and k == 0), stop=(cc_ == 3 and k == 1))
                m.then_inc(units_multiplied, 1)

            def rotate4(part, l):
                n = ROPES[part, l]
                if n > 0:
                    pe.wait_ge(s("roped2"), n)
                wait_taken(pe, (part, l, 3))
                z = (diffz if part[0] == "d" else retz)
                a0 = 0 if part[1] == "k" else 4
                for j in range(4):
                    m = pe.matmul(ps[:, 4 * 512 + T * j:4 * 512 + T * j + T], c("rot64" if part[0] == "d" else "rot128"),
                                  z[:, a0 + j, 0:T], start=(j % 2 == 0), stop=True, skip_group_check=True)
                m.then_inc(s("rotated2"), 1)

            def diff(l, step):
                nd = len(DIFF[l])
                if step < nd:
                    n, (st, hh, qt) = DIFF_AT[l] + step, DIFF[l][step]
                    if step == 0:
                        pe.wait_ge(s("roped2"), ROPES["dq", l] + 1)
                    for m_ in range(2):
                        if n > 0:
                            pe.wait_ge(s("exps2"), 2 * (n - 1) + m_ + 1)
                        rows = slice(HD * m_, HD * m_ + HD)
                        keys = slice(T * st, 2 * T)
                        q0 = T * st + P * qt
                        pe.matmul(bank(4 + m_, T * st, 2 * T - T * st), diffz[rows, 4 + hh, q0:q0 + P], diffz[rows, hh, keys],
                                  start=True, stop=True).then_inc(s("scored2"), 1)
                if 1 <= step <= nd:
                    n, (st, hh, qt) = DIFF_AT[l] + step - 1, DIFF[l][step - 1]
                    pe.wait_ge(s("attn2"), n + 1)
                    if n >= 1:
                        pe.wait_ge(s("attnT2"), n)
                    for kt in range(2 * st, 4):
                        m = pe.transpose(bank(6, P * kt, P), aux[:, 4 + n % 2, P * kt:P * kt + P], c("ident"))
                    m.then_inc(s("turned2"), 1)
                if 2 <= step <= nd + 1:
                    n, (st, hh, qt) = DIFF_AT[l] + step - 2, DIFF[l][step - 2]
                    pe.wait_ge(s("attnT2"), n + 1)
                    if qt == 0 and n >= 2:
                        pe.wait_ge(s("diff_scaled"), n // 2)
                    for kt in range(2 * st, 4):
                        m = pe.matmul(bank(7, P * qt, P), diffv[:, kt, P * hh:P * hh + P], aux[:, 6 + n % 2, P * kt:P * kt + P],
                                      start=(kt == 2 * st), stop=(kt == 3), skip_group_check=True)
                    m.then_inc(s("weighed2"), 1)
                    if qt == 1:
                        pe.wait_ge(s("head_sq"), HEAD_AT[l] + (step - 2) // 2 + 1)
                        pe.matmul(bank(7, T, T), c("ones"), aux[:, 8, 0:T], start=True, stop=True, skip_group_check=True)\
                            .then_inc(s("head_ss"), 1)

            def states_of(l):
                for hh in range(4):
                    n = 4 * l + hh
                    for tt in range(2):
                        if hh == 0 and tt == 0:
                            pe.wait_ge(s("roped2"), ROPES["rq", l] + 1)
                            pe.wait_ge(s("diff_scaled"), HEAD_AT[l + 1])
                        if hh > 0:
                            pe.wait_ge(s("ktok_ready"), 8 * l + 2 * hh)
                        pe.transpose(bank(4, P * tt, P), retz[:, hh, T + P * tt:T + P * tt + P], c("ident")) \
                            .then_inc(s("k_turned"), 1)
                    pe.wait_ge(s("ktok_ready"), 8 * l + 2 * hh + 2)
                    if hh > 0:
                        pe.wait_ge(s("states_ready"), n)
                    for dr in range(2):
                        for tt in range(2):
                            m = pe.matmul(bank(5, P * dr, P), ktok[:, dr, tt, :], retv[:, 2 + tt, P * hh:P * hh + P],
                                          start=(dr == 0 and tt == 0), stop=(tt == 1), skip_group_check=True)
                    m.then_inc(s("states_done"), 1)

            def ret(l, step):
                nr = len(RET[l])
                if step == 0:
                    states_of(l)
                if step < nr:
                    n, (st, hh) = RET_AT[l] + step, RET[l][step]
                    if step == 0:
                        pe.wait_ge(s("states_ready"), 4 * l + 4)
                    if n >= 2:
                        pe.wait_ge(s("decayed"), n - 1)
                    for kt in range(2):
                        m = pe.matmul(bank(4 + n % 2, T * kt, T), retz[:, hh, T * st + P * kt:T * st + P * kt + P],
                                      retz[:, 4 + hh, T * st:T * st + T], start=(kt == 0), stop=True, skip_group_check=True)
                    m.then_inc(s("ret_scored"), 1)
                if 2 <= step <= nr + 1:
                    n = RET_AT[l] + step - 2
                    pe.wait_ge(s("ret_sq"), n + 1)
                    pe.matmul(bank(7, 0, T), c("ones"), aux[:, 8, 0:T], start=True, stop=True).then_inc(s("ret_ss"), 1)
                if 1 <= step <= nr:
                    n, (st, hh) = RET_AT[l] + step - 1, RET[l][step - 1]
                    pe.wait_ge(s("decayed"), n + 1)
                    if n >= 1:
                        pe.wait_ge(s("ret_scaled"), n)
                    if st == 0:
                        pe.wait_ge(s("q_decayed"), 2 * (4 * l + hh) + 2)
                    for kt in range(2):
                        m = pe.matmul(bank(6, 0, T), retv[:, 2 * st + kt, P * hh:P * hh + P], aux[:, n % 2, T * kt:T * kt + T],
                                      start=(kt == 0), stop=(st == 1 and kt == 1),
                                      skip_group_check=True)
                    if st == 0:
                        for dr in range(2):
                            m = pe.matmul(bank(6, 0, T), states[:, dr, hh, :], aux[:, 2 + n % 2, T * dr:T * dr + T],
                                          start=False, stop=(dr == 1), skip_group_check=True)
                    m.then_inc(s("ret_out"), 1)

            for l in range(LAYERS):
                tok = 2 * T if l == 0 else T
                sumsq(5 + 2 * l, 2 * T)
                for j in range(4):
                    project2(("dk", l, j), l, 2 * T, first=(j == 0))
                for j in range(4):
                    project2(("dq", l, j), l, tok)
                    if j == 1:
                        rotate4("dk", l)
                for cc_ in range(4):
                    project_values("dv", l, cc_, 4)
                rotate4("dq", l)
                for j in range(4):
                    project2(("dg", l, j), l, tok)
                for slot, name in enumerate(slot_units(l)):
                    part = name[0]
                    if part in ("rv", "mv"):
                        project_values(part, l, name[2], 4 if part == "rv" or l == 0 else 2)
                    else:
                        project2(name, l, 2 * T if part == "rk" else tok)
                    for kind, step in SLOTS[l][slot]:
                        if kind == "diff":
                            diff(l, step)
                        elif kind == "rot":
                            rotate4(step, l)
                        elif kind == "ret":
                            ret(l, step)
                for g in range(4):
                    n = 4 * l + g
                    if g == 0:
                        wait_taken(pe, ("mv", l, tok // P - 1))
                        pe.wait_ge(s("ret_scaled"), RET_AT[l + 1])
                    if n >= 2:
                        pe.wait_ge(s("mixed"), n - 1)
                    for tt in range(tok // P):
                        pe.matmul(bank(4 + g % 2, P * tt, P), vn[:, tt, P * g:P * g + P], c("wsT", BW * l + P * g, BW * l + P * g + P),
                                  start=(tt == 0), stop=False, skip_group_check=True)
                        m = pe.matmul(bank(4 + g % 2, P * tt, P), c("ones")[0:1, :], bsrow[0:1, BW * l + P * g:BW * l + P * g + P],
                                      start=False, stop=True, skip_group_check=True)
                    m.then_inc(s("mix_done"), 1)
                for f in range(KT):
                    for b in range(3):
                        project2(("mlog", l, b, f), l, tok)
                    for b, o in enumerate((o_ret, o_mlp, o_dif)):
                        if b != 1:
                            wt = unit(("wbo", l, f, b // 2))
                        if f == 0 and b == 0:
                            pe.wait_ge(s("mixed"), 4 * l + 4)
                        bank_free(pe, ("wbo", l, b, f))
                        for k in range(4):
                            m = pe.matmul(bank(BANK["wbo", l, b, f][0], 0, tok), wt[:, BW * (b % 2) + P * k:BW * (b % 2) + P * k + P],
                                          o[:, k, 0:tok], start=(k == 0), stop=(k == 3))
                        if b != 0:
                            m.then_inc(units_multiplied, 1)
                for j in range(KT):
                    if j == 0:
                        pe.wait_ge(s("merged"), 8 * l + 8)
                    project2(("wo", l, j), l, tok, src=ymrg)
                sumsq(6 + 2 * l, tok)

        @block.scalar
        def _(act):
            steps = [0]

            def link(ins):
                steps[0] += 1
                ins.then_inc(act_step, 1)
                act.wait_ge(act_step, steps[0])

            def squares(n, x, who, counts, tokens=T):
                for k in range(KT):
                    act.wait_ge(who, counts[k])
                    act.activation(sq[:, k, 0:T], x[:, k, :], ACT.Square).then_inc(squares_ready, 1)

            def root(n, src, tokens, sumsq_sem, count, width, done, col=0):
                act.wait_ge(sumsq_sem, count)
                link(act.activation(lnr[:, col:col + tokens], src, ACT.Ln, bias=eps[:, 0:1], scale=1.0 / width))
                act.activation(rstd[:, col:col + tokens], lnr[:, col:col + tokens], ACT.Exp, scale=-0.5).then_inc(done, 1)

            def ffn(tag, n):
                def gate(f, count):
                    act.wait_ge(units_multiplied, count)
                    act.activation(sil[:, f % 4, :], bank(4 + f % 4, 0, T), ACT.Silu).then_inc(silu_ready, 1)

                gate(0, UNIT[tag, "w3", 0] + 1)
                with act.Fori(0, (FT - 2) // 4) as it:
                    for f in range(1, 5):
                        gate(f, UNIT[tag, "w3", f] + 1 + 12 * it)
                gate(FT - 1, UNIT[tag, "w3", FT - 1] + 1)

            act.wait_ge(consts_loaded, 16 * NC_DMAS)
            act.wait_ge(s("eps_set"), 1)
            squares(0, h, consts_loaded, [16 * NC_DMAS] * KT)
            root(0, bank(7, 0, T), T, sumsq_ready, 1, D, rstd_ready)
            act.activation(cs[:, :, :].rearrange("p a b -> p (a b)"), c("cc"), ACT.Silu).then_inc(cs_ready, 1)
            act.wait_ge(s("angle_ready"), 1)
            act.activation(s5v[:, 7:9, :], s5v[:, 5:7, :], ACT.Sin, scale=TWO_PI).then_inc(s("angle_sin"), 1)
            ffn("ffn1", 0)
            for i in range(NST):
                act.wait_ge(s("turns_ready"), 2 * i + 2)
                act.activation(costab[:, i, :], costab[:, i, :], ACT.Sin, scale=TWO_PI)
                act.activation(sintab[:, i, :], sintab[:, i, :], ACT.Sin, scale=TWO_PI).then_inc(s("tables_ready"), 1)
            squares(1, h, resid_ready, [k // 2 + 1 for k in range(KT)])
            root(1, bank(7, 0, T), T, sumsq_ready, 2, D, rstd_ready)

            def take(name, dst, func=ACT.Copy, tokens=T, unit=None, **kw):
                product(act, *(unit or name))
                act.activation(dst, bank(BANK[name][0], 0, tokens), func, **kw).then_inc(act_evac, 1)

            for j in range(4):
                take(("u", j), uT[:, j, :])
            take(("kc",), zq[:, 6, :])
            take(("vc",), vcT)
            for j in range(4):
                take(("q", j), zq[:, j, :])
            take(("ks",), zq[:, 4, :])
            take(("kw",), zq[:, 5, :])
            product(act, "vg", 2)
            for tt in range(2):
                b = BANK["vg", tt][0]
                act.activation(gates[:, tt, :], bank(b, 256, 24), ACT.Sigmoid)
                act.activation(vtok[:, tt, :], bank(b, 0, 280), ACT.Copy).then_inc(act_evac, 1)
            act.wait_ge(s("blk_cleared"), 1)
            wait_taken(act, ("vc",))
            act.wait_ge(s("roped"), 1)
            for kv, src in enumerate((zq[:, 6, :], vcT)):
                bv = blk[:, kv, :].rearrange("p (l g c) -> p c g l", l=16, g=2)
                sv = src.rearrange("p (c l two) -> p c l two", l=8, two=2)
                for g in range(2):
                    for par in range(2):
                        for half in range(2):
                            m = act.activation(bv[HD * par:HD * par + HD, 0:NCMP, g, 8 * half:8 * half + 8],
                                               sv[HD * g:HD * g + HD, half:half + NCMP, :, par], ACT.Copy)
                m.then_inc(s("blk_filled"), 1)
            for kv, tag in enumerate(("cmpk", "cmpv")):
                product(act, tag, 3)
                act.activation(ghid[:, kv, :], bank(kv, 0, 64), ACT.Gelu_apprx_tanh).then_inc(s("ghid_ready"), 1)
            act.wait_ge(s("kcmp"), 1)
            for g in range(2):
                act.activation(kbd[HD * g:HD * g + HD, 16 * g:16 * g + 16], ps[HD * g:HD * g + HD, 2 * 512:2 * 512 + 16],
                               ACT.Copy).then_inc(s("kbd_ready"), 1)
            act.wait_ge(s("cmp_shifted"), 1)
            act.activation(cex, csc, ACT.Exp, scale=HD ** -0.5).then_inc(s("cmp_exp"), 1)
            act.wait_ge(s("cmp_probsT"), 1)
            act.activation(pct, bank(1, 0, 2 * P), ACT.Copy).then_inc(s("pct_ready"), 1)

            def turn_copy(i):
                act.wait_ge(s("turned"), i + 1)
                if i >= 2:
                    act.wait_ge(s("weighed"), i - 1)
                act.activation(pt[:, i % 2, :], bank(2 + i % 2, 0, 384), ACT.Copy).then_inc(s("pt_ready"), 1)

            for i in range(NST + 2):
                if i < NST:
                    act.wait_ge(s("maxes"), i + 1)
                    act.activation(ex[:, i % 2, 0:P], bank(i % 2, 0, P), ACT.Exp, scale=HD ** -0.5,
                                   bias=stat[:, i % 2, 2:3], accum_out=stat[:, i % 2, 4:5]).then_inc(s("exps"), 1)
                    act.activation(ex[:, i % 2, P:3 * P], bank(i % 2, P, 2 * P), ACT.Exp, scale=HD ** -0.5,
                                   bias=stat[:, i % 2, 3:4], accum_out=stat[:, i % 2, 5:6]).then_inc(s("exps"), 1)
                if 1 <= i <= NST:
                    turn_copy(i - 1)
                if i < NST:
                    act.wait_ge(s("factors"), i + 1)
                    act.activation(prob[:, i % 2, 0:P], ex[:, i % 2, 0:P], ACT.Copy, scale=stat[:, i % 2, 8:9])\
                        .then_inc(s("probs"), 1)
                    act.activation(prob[:, i % 2, P:3 * P], ex[:, i % 2, P:3 * P], ACT.Copy, scale=stat[:, i % 2, 9:10])\
                        .then_inc(s("probs"), 1)
                if i >= 5 and (i - 5) % 4 == 0:
                    j = (i - 5) // 4
                    act.wait_ge(s("weighed"), 4 * j + 4)
                    act.activation(oT[:, j, :], ps[:, 5 * 512 + T * (j % 2):5 * 512 + T * (j % 2) + T], ACT.Copy)\
                        .then_inc(s("o_taken"), 1)
            for j in range(4):
                act.wait_ge(s("s5_y_taken"), j + 1)
                act.activation(yg[:, j, :], yg[:, j, :], ACT.Gelu_apprx_tanh).then_inc(s("gelu_ready"), 1)
            for j in range(4):
                take(("glu", j), sg[:, j, :], ACT.Sigmoid, unit=("glu", j // 2), bias=c("b_glu", j, j + 1))
            n_wout = BANK["wout", 0][3]
            squares(2, h, dve_evac, [n_wout + k for k in range(KT)])
            root(2, bank(7, 0, T), T, sumsq_ready, 3, D, rstd_ready)
            ffn("ffn2", 1)
            squares(3, h, resid_ready, [4 + k // 2 + 1 for k in range(KT)])
            for j in range(4):
                take(("plew", j), pwp[:, 2 * j:2 * j + 2, :].rearrange("p a b -> p (a b)"), tokens=2 * T, unit=("plew", j // 2))
            root(3, bank(7, 0, T), T, sumsq_ready, 4, D, rstd_ready)
            for j in range(KT):
                take(("pleg", j), plg[:, j, :], ACT.Sigmoid)
            squares(4, h, resid_ready, [8 + k + 1 for k in range(KT)])
            root(4, bank(7, 0, T), T, sumsq_ready, 5, D, rstd_ready)

            act.wait_ge(resid_ready, RESID_BLOCK2)
            link(act.activation(sp[:, 0, :], c("ret_logit"), ACT.Exp, scale=-1.0))
            act.activation(sp[:, 1, :], sp[:, 0, :], ACT.Ln, bias=1.0).then_inc(s("lay_act"), 1)
            act.wait_ge(s("lay_dve"), 1)
            act.activation(sp[:, 3, 0:4], sp[:, 2, 0:4], ACT.Exp).then_inc(s("lay_act"), 1)
            act.wait_ge(s("lay_dve"), 2)
            act.activation(lay[:, :, 0:16], lay[:, :, 0:16], ACT.Exp).then_inc(s("lay_act"), 1)

            def diff(l, step):
                nd = len(DIFF[l])
                if step < nd:
                    n, (st, hh, qt) = DIFF_AT[l] + step, DIFF[l][step]
                    for m_ in range(2):
                        act.wait_ge(s("maxes2"), 2 * n + m_ + 1)
                        e = aux[:, 2 * (n % 2) + m_, T * st:2 * T]
                        act.activation(e, bank(4 + m_, T * st, 2 * T - T * st), ACT.Exp, scale=HD ** -0.5,
                                       bias=st2[:, n % 2, 2 + m_:3 + m_], accum_out=st2[:, n % 2, 4 + m_:5 + m_])\
                            .then_inc(s("exps2"), 1)
                if 1 <= step <= nd:
                    n, (st, hh, qt) = DIFF_AT[l] + step - 1, DIFF[l][step - 1]
                    act.wait_ge(s("turned2"), n + 1)
                    if n >= 2:
                        act.wait_ge(s("weighed2"), n - 1)
                    act.activation(aux[:, 6 + n % 2, T * st:2 * T], bank(6, T * st, 2 * T - T * st), ACT.Copy)\
                        .then_inc(s("attnT2"), 1)
                if 2 <= step <= nd + 1 and DIFF[l][step - 2][2] == 1:
                    n, k = DIFF_AT[l] + step - 2, HEAD_AT[l] + (step - 2) // 2
                    act.wait_ge(s("weighed2"), n + 1)
                    act.activation(aux[:, 8, 0:T], bank(7, 0, T), ACT.Square).then_inc(s("head_sq"), 1)
                    root(0, bank(7, T, T), T, s("head_ss"), k + 1, P, s("head_rstd"))

            def states_of(l):
                for hh in range(4):
                    for tt in range(2):
                        act.wait_ge(s("k_turned"), 8 * l + 2 * hh + 2)
                        if hh > 0:
                            act.wait_ge(s("states_done"), 4 * l + hh)
                        for dr in range(2):
                            m = act.activation(ktok[:, dr, tt, :], bank(4, P * tt, P), ACT.Copy,
                                               scale=lay[:, l, 8 * dr + 2 * hh + tt:8 * dr + 2 * hh + tt + 1])
                        m.then_inc(s("ktok_ready"), 1)

            def ret(l, step):
                nr = len(RET[l])
                if step == 0:
                    states_of(l)
                if step < nr and RET[l][step][0] == 0:
                    n, (st, hh) = RET_AT[l] + step, RET[l][step]
                    k = 4 * l + hh
                    if k >= 2:
                        act.wait_ge(s("q_decayed"), 2 * (k - 1))
                    for dr in range(2):
                        act.activation(aux[:, 4 + k % 2, T * dr:T * dr + T], c("steps"), ACT.Exp,
                                       scale=lay[:, l, 16 + 8 * dr + hh:17 + 8 * dr + hh],
                                       bias=lay[:, l, 16 + 12 * dr + hh:17 + 12 * dr + hh]).then_inc(s("state_decay"), 1)
                if 2 <= step <= nr + 1:
                    n = RET_AT[l] + step - 2
                    act.wait_ge(s("ret_out"), n + 1)
                    act.activation(aux[:, 8, 0:T], bank(6, 0, T), ACT.Square).then_inc(s("ret_sq"), 1)
                    if n >= 1:
                        act.wait_ge(s("ret_scaled"), n)
                    root(0, bank(7, 0, T), T, s("ret_ss"), n + 1, P, s("ret_rstd"))

            def decay_tables(l, hh):
                n = 4 * l + hh
                if hh == 0 and l == 1:
                    act.wait_ge(s("decayed"), RET_AT[1])
                act.activation(dmat[:, hh, :], c("dist"), ACT.Exp, scale=lay[:, l, 16 + hh:17 + hh]).then_inc(s("decay_exp"), 1)
                if n > 0:
                    act.wait_ge(s("decay_masked"), 2 * n)
                act.activation(aux[:, 9, :], c("dist"), ACT.Exp, scale=lay[:, l, 24 + hh:25 + hh]).then_inc(s("decay_exp"), 1)

            for l in range(LAYERS):
                tok = 2 * T if l == 0 else T
                for k in range(KT):
                    if l == 1:
                        act.wait_ge(resid_ready, RESID_BLOCK2 + KT)
                        act.wait_ge(s("ctx_ready"), KT)
                    else:
                        act.wait_ge(resid_ready, RESID_BLOCK2)
                    act.activation(sq2[:, k, 0:T], h[:, k, :], ACT.Square)
                    act.activation(sq2[:, k, T:2 * T], hc[:, k, :], ACT.Square).then_inc(squares_ready, 1)
                root(0, bank(7), 2 * T, sumsq_ready, 6 + 2 * l, D, rstd_ready)
                for k in range(KT):
                    for st in range(2):
                        act.wait_ge(scaled_ready, 16 * l + 2 * k + st + 1)
                        v = hn[:, k, T * st:T * st + T]
                        act.activation(v, v, ACT.Identity, bias=mods[:, l, k, st:st + 1]).then_inc(s("modulated"), 1)
                for part in ("dk", "dq"):
                    for j in range(4):
                        t_ = 2 * T if part == "dk" else tok
                        take((part, l, j), diffz[:, (0 if part == "dk" else 4) + j, 0:t_], tokens=t_)
                for tt in range(4):
                    take(("dv", l, tt), diffv[:, tt, :], tokens=BW, unit=("dv", l, 3))
                for j in range(4):
                    take(("dg", l, j), diffz[:, 8 + j, 0:tok], ACT.Silu, tokens=tok)
                if l == 0:
                    act.wait_ge(s("lay_dve"), 3)
                for slot, name in enumerate(slot_units(l)):
                    part, j = name[0], name[2]
                    if part == "rk":
                        take(name, retz[:, j, 0:2 * T], tokens=2 * T)
                    if part == "rq":
                        take(name, retz[:, 4 + j, 0:tok], tokens=tok)
                    if part == "rv" and j == 3:
                        for tt in range(4):
                            take(("rv", l, tt), retv[:, tt, :], tokens=BW, unit=name)
                    if part == "rg":
                        take(name, retz[:, 8 + j, 0:tok], ACT.Silu, tokens=tok)
                    if part == "mu":
                        take(name, mlpu[:, j, 0:tok], tokens=tok)
                    if part == "mg":
                        take(name, mlpu[:, 4 + j, 0:tok], ACT.Silu, tokens=tok)
                    for kind, step in SLOTS[l][slot]:
                        if kind == "diff":
                            diff(l, step)
                        if kind == "tables":
                            decay_tables(l, step)
                        if kind == "ret":
                            ret(l, step)
                    if part == "mv" and j == 3:
                        for tt in range(tok // P):
                            n = VN_AT[l] + tt
                            act.wait_ge(s("var_ready"), n + 1)
                            link(act.activation(st2[:, n % 2, 10:11], st2[:, n % 2, 9:10], ACT.Ln, bias=eps[:, 0:1]))
                            act.activation(st2[:, n % 2, 11:12], st2[:, n % 2, 10:11], ACT.Exp, scale=-0.5)\
                                .then_inc(s("ln_rstd"), 1)
                for f in range(KT):
                    for b in range(3):
                        n = 8 * l + f
                        if n >= 2:
                            act.wait_ge(s("merged"), n - 1)
                        if f == 0:
                            act.wait_ge(s("ret_scaled"), RET_AT[l + 1])
                        take(("mlog", l, b, f), aux[:, 3 * (f % 2) + b, 0:tok], ACT.Sigmoid, tokens=tok)
                for j in range(KT):
                    take(("wo", l, j), unnormed[:, j, 0:tok], tokens=tok)
                for k in range(KT):
                    wait_taken(act, ("wo", l, k))
                    act.activation(sq2[:, k, 0:tok], unnormed[:, k, 0:tok], ACT.Square).then_inc(squares_ready, 1)
                root(0, bank(7, 0, tok), tok, sumsq_ready, 7 + 2 * l, D, rstd_ready)

        @block.vector
        def _(dve):
            steps = [0]

            def link(ins):
                steps[0] += 1
                ins.then_inc(dve_step, 1)
                dve.wait_ge(dve_step, steps[0])

            tt_, ts, stt = dve.tensor_tensor, dve.tensor_scalar, dve.scalar_tensor_tensor

            def norm(n, gain, dst, done):
                dve.wait_ge(rstd_ready, n + 1)
                for k in range(KT):
                    stt(dst[:, k, 0:T], h[:, k, :], c(gain, k, k + 1), rstd[:, 0:T], ALU.mult, ALU.mult).then_inc(done, 1)

            def ffn(tag, n):
                def gated(f, count):
                    dve.wait_ge(silu_ready, count)
                    tt_(hid[:, f % 4, :], sil[:, f % 4, :], bank(4 + f % 4, T, T), ALU.mult).then_inc(hidden_ready, 1)

                gated(0, FT * n + 1)
                with dve.Fori(0, (FT - 2) // 4) as it:
                    for f in range(1, 5):
                        gated(f, FT * n + f + 1 + 4 * it)
                gated(FT - 1, FT * n + FT)
                product(dve, tag, "w2", FT - 1)
                for m in range(4):
                    hh = h[:, 2 * m:2 * m + 2, :].rearrange("p a b -> p (a b)")
                    stt(hh, bank(m), 0.5, hh, ALU.mult, ALU.add).then_inc(resid_ready, 1)

            col = lambda n: s5v[:, n, :]

            def exact_exp(dst, src):
                x, n, f, q, e = (col(k) for k in (16, 17, 18, 19, 20))
                link(ts(x, src, -87.0, 88.0, ALU.max, ALU.min))
                link(ts(n, x, LOG2E, MAGIC, ALU.mult, ALU.add))
                link(ts(n, n, MAGIC, None, ALU.subtract))
                link(stt(f, n, -LN2_HI, x, ALU.mult, ALU.add))
                link(stt(f, n, -LN2_LO, f, ALU.mult, ALU.add))
                link(ts(q, f, TAYLOR[0], None, ALU.mult))
                for k in TAYLOR[1:]:
                    link(stt(q, q, k, f, ALU.add, ALU.mult))
                link(ts(e.bitcast(I32), n, 127.0, None, ALU.add))
                link(ts(e.bitcast(I32), e.bitcast(I32), 23, None, ALU.logical_shift_left))
                link(stt(dst, q, 1.0, e, ALU.add, ALU.mult))

            dve.memset(eps[:, :], EPS).then_inc(s("eps_set"), 1)
            dve.wait_ge(consts_loaded, 16 * NC_DMAS)
            dve.tensor_copy(negc[:, :], c("causal")).then_inc(masks_ready, 1)
            dve.tensor_copy(idb[:, :], c("ident")).then_inc(masks_ready, 1)
            norm(0, "g_ffn1", hn, normed_ready)
            DT, LRE, LIM, R, K, GC, GS, COS, SIN, PR, QI, DEN, CR, CI, TMP = range(15)
            exact_exp(col(DT), c("log_dt"))
            link(tt_(col(LRE), c("a_re"), col(DT), ALU.mult))
            link(tt_(col(LIM), c("a_im"), col(DT), ALU.mult))
            link(ts(col(K), col(LIM), INV2PI, MAGIC, ALU.mult, ALU.add))
            link(ts(col(K), col(K), MAGIC, None, ALU.subtract))
            link(stt(col(GS), col(K), -PI2_HI, col(LIM), ALU.mult, ALU.add))
            link(stt(col(GS), col(K), -PI2_LO, col(GS), ALU.mult, ALU.add))
            link(ts(col(GS), col(GS), INV2PI, None, ALU.mult))
            link(ts(col(GS), col(GS), 0.5, -0.5, ALU.min, ALU.max))
            link(ts(col(GC), col(GS), 0.25, None, ALU.add))
            link(ts(col(K), col(GC), MAGIC, MAGIC, ALU.add, ALU.subtract))
            tt_(col(GC), col(GC), col(K), ALU.subtract).then_inc(s("angle_ready"), 1)
            exact_exp(col(R), col(LRE))
            dve.wait_ge(s("angle_sin"), 1)
            link(tt_(col(PR), col(R), col(COS), ALU.mult))
            link(ts(col(PR), col(PR), 1.0, None, ALU.subtract))
            link(tt_(col(QI), col(R), col(SIN), ALU.mult))
            link(tt_(col(DEN), c("a_re"), c("a_re"), ALU.mult))
            link(tt_(col(TMP), c("a_im"), c("a_im"), ALU.mult))
            link(tt_(col(DEN), col(DEN), col(TMP), ALU.add))
            link(dve.reciprocal(col(DEN), col(DEN)))
            for dst, x, y, op in ((CR, PR, QI, ALU.add), (CI, QI, PR, ALU.subtract)):
                link(tt_(col(dst), col(x), c("a_re"), ALU.mult))
                link(tt_(col(TMP), col(y), c("a_im"), ALU.mult))
                link(tt_(col(dst), col(dst), col(TMP), op))
                link(tt_(col(dst), col(dst), col(DEN), ALU.mult))
            wide = lambda v: v.rearrange("p (a b) -> p a b", b=32)
            over = lambda n: col(n).unsqueeze(2).broadcast_to([P, NST, 32])
            t512 = bakA[:, 0, :]
            for dst, x, y, op in ((bre, "b_re", "b_im", ALU.subtract), (bim, "b_im", "b_re", ALU.add)):
                link(tt_(wide(dst), wide(c(x)), over(CR), ALU.mult))
                link(tt_(wide(t512), wide(c(y)), over(CI), ALU.mult))
                tt_(dst, dst, t512, op).then_inc(s("s5_b_ready"), 1)
                dve.wait_ge(s("s5_b_ready"), 1 if dst is bre else 2)
            link(ts(cneg_re, c("c_re"), -1.0, None, ALU.mult))
            link(ts(cneg_im, c("c_im"), -1.0, None, ALU.mult))

            ffn("ffn1", 0)
            dve.wait_ge(s("s5_bt"), 1)
            dve.tensor_copy(bT.rearrange("p a b c -> p (a b c)"), ps[:, 4 * 512:6 * 512]).then_inc(s("s5_b_copied"), 1)
            norm(1, "g_mix", hn, normed_ready)

            dve.wait_ge(s("rotated"), 1)
            t1024 = sq[:, 0:2, :].rearrange("p a b -> p (a b)")
            for n, (a, b) in enumerate(((6, 7), (4, 6), (0, 4))):
                w = b - a
                z = zq[:, a:b, :]
                tmp = t1024[:, 0:T * w].rearrange("p (a b) -> p a b", b=T)
                rot = ps[:, 4 * 512 + T * a:4 * 512 + T * b].rearrange("p (a b) -> p a b", b=T)
                tab = lambda name: c(name).unsqueeze(1).broadcast_to([P, w, T])
                if n > 0:
                    dve.wait_ge(s("roped"), n)
                tt_(tmp, rot, tab("sin1"), ALU.mult)
                link(tt_(z, z, tab("cos1"), ALU.mult))
                tt_(z, z, tmp, ALU.add).then_inc(s("roped"), 1)
            for kv in range(2):
                dve.wait_ge(s("blk_filled"), kv + 1)
                bv = blk[:, kv, :].rearrange("p (l c) -> p l c", l=16)
                tt_(bv, bv, c("pe", 16 * kv, 16 * kv + 16).unsqueeze(2).broadcast_to([P, 16, 32]), ALU.add)\
                    .then_inc(s("blk_ready"), 1)
            dve.wait_ge(s("ghid_ready"), 2)
            dve.tensor_copy(grep.rearrange("p h (j c) -> p h j c", j=4),
                            ghid[:, 1, :].rearrange("p (h c) -> p h c", h=2).unsqueeze(2).broadcast_to([P, 2, 4, 32]))\
                .then_inc(s("grep_ready"), 1)
            dve.wait_ge(s("vcmp"), 1)
            for g in range(2):
                ts(vbd[:, HD * g:HD * g + HD], bank(3, 0, HD), c("gmask", g, g + 1), None, ALU.mult).then_inc(s("vbd_ready"), 1)
            dve.wait_ge(s("cmp_scores"), 1)
            heads = lambda v: v.rearrange("p (q h c) -> p q h c", q=2, c=16)
            flat = lambda v: v.rearrange("p (h c) -> p h c", c=16)
            mask = lambda name: c(name).rearrange("p (q c) -> p q c", q=2).unsqueeze(2).broadcast_to([P, 2, 8, 16])
            each = lambda n: cst[:, n, :].unsqueeze(2).broadcast_to([P, 16, 16])
            link(tt_(heads(csc), heads(bank(0, 0, 2 * P)), mask("cneg"), ALU.add))
            link(dve.tensor_reduce(cst[:, 0, :], flat(csc), AX_X, ALU.max))
            tt_(flat(csc), flat(csc), each(0), ALU.subtract).then_inc(s("cmp_shifted"), 1)
            dve.wait_ge(s("cmp_exp"), 1)
            link(tt_(heads(cex), heads(cex), mask("cmask"), ALU.mult))
            link(dve.tensor_reduce(cst[:, 1, :], flat(cex), AX_X, ALU.add))
            link(ts(cst[:, 1, :], cst[:, 1, :], 1e-30, None, ALU.max))
            link(dve.reciprocal(cst[:, 2, :], cst[:, 1, :]))
            wait_taken(dve, ("vg", 1))
            link(tt_(cst[:, 2, :].rearrange("p (q h) -> p q h", q=2), cst[:, 2, :].rearrange("p (q h) -> p q h", q=2),
                     gates[:, :, 0:8], ALU.mult))
            tt_(flat(cex), flat(cex), each(2), ALU.mult).then_inc(s("cmp_probs"), 1)

            for i in range(NST + 1):
                if i < NST:
                    st = stat[:, i % 2, :]
                    dve.wait_ge(s("scored"), i + 1)
                    dve.tensor_reduce(st[:, 0:1], bank(i % 2, 0, P), AX_X, ALU.max)
                    link(dve.tensor_reduce(st[:, 1:2], bank(i % 2, P, 2 * P), AX_X, ALU.max))
                    ts(st[:, 2:4], st[:, 0:2], -HD ** -0.5, None, ALU.mult).then_inc(s("maxes"), 1)
                    dve.wait_ge(s("s5_bu"), i + 1)
                    dve.wait_ge(s("tables_ready"), i + 1)
                    two = lambda v: v.rearrange("p (a b) -> p a b", a=2)
                    tab = lambda v: v[:, i, :].unsqueeze(1).broadcast_to([P, 2, T])
                    ra, rb, zi, ws = rotA[:, i % 2, :], rotB[:, i % 2, :], zin[:, i % 2, :], wst[:, i % 2, :]
                    tt_(two(ra), two(bank(6)), tab(costab), ALU.mult)
                    tt_(two(rb), two(bank(6)), tab(sintab), ALU.mult).then_inc(s("s5_prod"), 1)
                    dve.wait_ge(s("s5_prod"), i + 1)
                    tt_(zi[:, 0:T], ra[:, 0:T], rb[:, T:2 * T], ALU.add)
                    link(tt_(zi[:, T:2 * T], ra[:, T:2 * T], rb[:, 0:T], ALU.subtract))
                    if i >= 2:
                        dve.wait_ge(s("s5_back"), 2 * (i - 1))
                    for part in range(2):
                        v = slice(T * part, T * part + T)
                        dve.tensor_tensor_scan(ws[:, v], s5v[:, R, i:i + 1].broadcast_to([P, T]), zi[:, v], 0.0,
                                               ALU.mult, ALU.add).then_inc(s("s5_scanned"), 1)
                    dve.wait_ge(s("exps"), 2 * i + 2)
                    link(dve.reciprocal(st[:, 6:8], st[:, 4:6]))
                    gc = 8 * (1 + i % 2) + 2 * (i // 4) + i // 2 % 2
                    tt_(st[:, 8:10], st[:, 6:8], gates[:, :, gc:gc + 1].rearrange("p a b -> p (a b)"), ALU.mult)\
                        .then_inc(s("factors"), 1)
                if i >= 4 and i % 4 == 0:
                    j = i // 4 - 1
                    dve.wait_ge(s("s5_y"), i)
                    stt(yg[:, j, :], uT[:, j, :], c("s5_d", j, j + 1), bank(7, T * (j % 2), T), ALU.mult, ALU.add)\
                        .then_inc(s("s5_y_taken"), 1)
            product(dve, "mod", LAYERS - 1, 3 * KT - 1)
            mv = mods[:, :, :, :].rearrange("p l f s -> p (l f) s")
            tt_(mv, bank(4, 0, 96).rearrange("p (f s) -> p f s", s=2), c("b_mod").unsqueeze(2).broadcast_to([P, 48, 2]),
                ALU.add).then_inc(mods_ready, 1)
            dve.wait_ge(mods_ready, 1)
            for l in range(LAYERS):
                gp = lambda name: c(name, KT * l, KT * l + KT).unsqueeze(2).broadcast_to([P, KT, 2])
                stt(amp[:, l, :, :], mods[:, l, KT:2 * KT, :], 1.0, gp("g_pre"), ALU.add, ALU.mult).then_inc(mods_ready, 1)
                tt_(pgate[:, l, :, :], mods[:, l, 2 * KT:3 * KT, :], gp("g_post"), ALU.mult).then_inc(mods_ready, 1)
            for j in range(4):
                wait_taken(dve, ("glu", j))
                tt_(oT[:, 4 + j, :], yg[:, j, :], sg[:, j, :], ALU.mult).then_inc(s("s5_out"), 1)
            for j in range(KT):
                product(dve, "wout", j)
                tt_(h[:, j, :], h[:, j, :], bank(BANK["wout", j][0], 0, T), ALU.add).then_inc(dve_evac, 1)
            norm(2, "g_ffn2", hn, normed_ready)
            ffn("ffn2", 1)
            norm(3, "g_ple", hn, normed_ready)
            for j in range(KT):
                wait_taken(dve, ("pleg", j))
                link(tt_(plg[:, j, :], plg[:, j, :], pwp[:, j, :], ALU.mult))
                tt_(h[:, j, :], h[:, j, :], plg[:, j, :], ALU.add).then_inc(resid_ready, 1)
            norm(4, "g_final", h, resid_ready)

            link(tt_(aux[:, 0, 0:256], c("lamq"), c("lamk"), ALU.mult))
            dve.tensor_reduce(sp[:, 2, 0:4], aux[:, 0, 0:256].rearrange("p (a b) -> p a b", b=HD), AX_X, ALU.add)\
                .then_inc(s("lay_dve"), 1)
            dve.wait_ge(s("lay_act"), 1)
            both = sp[:, 1, :].rearrange("p (l n) -> p l n", l=2)
            link(ts(lay[:, :, 16:24], both, -1.0, None, ALU.mult))
            ts(lay[:, :, 28:32], lay[:, :, 20:24], float(T), None, ALU.mult)
            ts(lay[:, :, 24:28], both[:, :, 4:8], 1.0, None, ALU.mult)
            for l in range(LAYERS):
                m = tt_(lay[:, l, 0:16].rearrange("p (d h t) -> p d h t", d=2, h=4),
                        lay[:, l, 16:24].rearrange("p (d h) -> p d h", d=2).unsqueeze(3).broadcast_to([P, 2, 4, 2]),
                        c("jrow").rearrange("p (d t) -> p d t", d=2).unsqueeze(2).broadcast_to([P, 2, 4, 2]), ALU.mult)
            m.then_inc(s("lay_dve"), 1)
            dve.wait_ge(s("lay_act"), 3)
            for l in range(LAYERS):
                stt(lay[:, l, 39:40], sp[:, 3, 2 * l + 1:2 * l + 2], -LAM_INIT[l], sp[:, 3, 2 * l:2 * l + 1],
                    ALU.add, ALU.subtract)
            ts(lay[:, :, 0:16], lay[:, :, 0:16], float(P) ** -0.5, None, ALU.mult).then_inc(s("lay_dve"), 1)

            def rope(part, l):
                n = ROPES[part, l]
                z = (diffz if part[0] == "d" else retz)[:, (0 if part[1] == "k" else 4):(4 if part[1] == "k" else 8), 0:T]
                tmp_c = aux[:, 0:2, :].rearrange("p a b -> p (a b)").rearrange("p (a b) -> p a b", b=T)
                tmp_s = aux[:, 2:4, :].rearrange("p a b -> p (a b)").rearrange("p (a b) -> p a b", b=T)
                rot = ps[:, 4 * 512:6 * 512].rearrange("p (a b) -> p a b", b=T)
                dve.wait_ge(s("rotated2"), n + 1)
                link(tt_(tmp_s, rot, c("sin" + part[0]).unsqueeze(1).broadcast_to([P, 4, T]), ALU.mult))
                dve.wait_ge(s("cos2"), n + 1)
                tt_(z, tmp_c, tmp_s, ALU.add).then_inc(s("roped2"), 1)

            def diff(l, step):
                nd = len(DIFF[l])
                if step < nd:
                    n, (st, hh, qt) = DIFF_AT[l] + step, DIFF[l][step]
                    v = st2[:, n % 2, :]
                    for m_ in range(2):
                        dve.wait_ge(s("scored2"), 2 * n + m_ + 1)
                        link(dve.tensor_reduce(v[:, m_:m_ + 1], bank(4 + m_, T * st, 2 * T - T * st), AX_X, ALU.max))
                        ts(v[:, 2 + m_:3 + m_], v[:, m_:m_ + 1], -HD ** -0.5, None, ALU.mult).then_inc(s("maxes2"), 1)
                    dve.wait_ge(s("exps2"), 2 * n + 2)
                    link(dve.reciprocal(v[:, 6:8], v[:, 4:6]))
                    link(tt_(v[:, 7:8], v[:, 7:8], lay[:, l, 39:40], ALU.mult))
                    e0, e1 = (aux[:, 2 * (n % 2) + m_, T * st:2 * T] for m_ in range(2))
                    link(ts(e0, e0, v[:, 6:7], None, ALU.mult))
                    if n >= 2:
                        dve.wait_ge(s("turned2"), n - 1)
                    stt(aux[:, 4 + n % 2, T * st:2 * T], e1, v[:, 7:8], e0, ALU.mult, ALU.add).then_inc(s("attn2"), 1)
                if 2 <= step <= nd + 1 and DIFF[l][step - 2][2] == 1:
                    st, hh, _ = DIFF[l][step - 2]
                    dve.wait_ge(s("head_rstd"), HEAD_AT[l] + (step - 2) // 2 + 1)
                    stt(aux[:, 8, T:2 * T], bank(7, 0, T), 1.0 - LAM_INIT[l], rstd[:, 0:T], ALU.mult, ALU.mult)\
                        .then_inc(s("diff_scaled"), 1)
                    dve.wait_ge(s("diff_scaled"), HEAD_AT[l] + (step - 2) // 2 + 1)
                    o = o_dif[:, hh, T * st:T * st + T]
                    if hh == 0 and st == 0:
                        wait_taken(dve, ("dg", l, 3))
                    link(tt_(o, aux[:, 8, T:2 * T], o, ALU.mult))

            def states_of(l):
                for hh in range(4):
                    dve.wait_ge(s("states_done"), 4 * l + hh + 1)
                    dve.tensor_copy(states[:, :, hh, :], bank(5, 0, 2 * P).rearrange("p (d n) -> p d n", d=2))\
                        .then_inc(s("states_ready"), 1)

            def ret(l, step):
                nr = len(RET[l])
                if step == 0:
                    states_of(l)
                    dve.wait_ge(s("decay_masked"), 8 * l + 8)
                if step < nr:
                    n, (st, hh) = RET_AT[l] + step, RET[l][step]
                    dve.wait_ge(s("ret_scored"), n + 1)
                    if n >= 2:
                        dve.wait_ge(s("ret_out"), n - 1)
                    stt(aux[:, n % 2, :], bank(4 + n % 2), float(P) ** -0.5, dmat[:, hh, :], ALU.mult, ALU.mult)\
                        .then_inc(s("decayed"), 1)
                if 2 <= step <= nr + 1:
                    n, (st, hh) = RET_AT[l] + step - 2, RET[l][step - 2]
                    dve.wait_ge(s("ret_rstd"), n + 1)
                    tt_(aux[:, 8, T:2 * T], bank(6, 0, T), rstd[:, 0:T], ALU.mult).then_inc(s("ret_scaled"), 1)
                    dve.wait_ge(s("ret_scaled"), n + 1)
                    o = o_ret[:, hh, T * st:T * st + T]
                    if n == RET_AT[l]:
                        wait_taken(dve, ("rg", l, 3))
                    link(tt_(o, aux[:, 8, T:2 * T], o, ALU.mult))

            for l in range(LAYERS):
                tok = 2 * T if l == 0 else T
                if l == 0:
                    dve.wait_ge(mods_ready, 1 + 2 * LAYERS)
                dve.wait_ge(rstd_ready, 6 + 2 * l)
                for k in range(KT):
                    for st, x in enumerate((h, hc)):
                        stt(hn[:, k, T * st:T * st + T], x[:, k, :], amp[:, l, k, st:st + 1], rstd[:, T * st:T * st + T],
                            ALU.mult, ALU.mult).then_inc(scaled_ready, 1)
                rope("dk", l)
                rope("dq", l)
                for slot, name in enumerate(slot_units(l)):
                    for kind, step in SLOTS[l][slot]:
                        if kind == "diff":
                            diff(l, step)
                        if kind == "rot":
                            rope(step, l)
                        if kind == "ret":
                            ret(l, step)
                    if name[0] == "mv" and name[2] == 3:
                        for tt in range(tok // P):
                            n = VN_AT[l] + tt
                            product(dve, *name)
                            b = BANK["mv", l, tt][0]
                            link(dve.bn_stats(out=st2[:, n % 2, 0:6], in_=bank(b)))
                            dve.bn_aggr(out=st2[:, n % 2, 8:10], in_=st2[:, n % 2, 0:6]).then_inc(s("var_ready"), 1)
                            dve.wait_ge(s("ln_rstd"), n + 1)
                            ts(vn[:, tt, :], bank(b), st2[:, n % 2, 8:9], st2[:, n % 2, 11:12], ALU.subtract, ALU.mult)\
                                .then_inc(dve_evac, 1)
                for g in range(4):
                    n = 4 * l + g
                    dve.wait_ge(s("mix_done"), n + 1)
                    wait_taken(dve, ("mg", l, g))
                    tt_(mlpu[:, g, 0:tok], mlpu[:, g, 0:tok], bank(4 + g % 2, 0, tok), ALU.mult).then_inc(s("mixed_raw"), 1)
                    dve.wait_ge(s("mixed_raw"), n + 1)
                    tt_(mlpu[:, g, 0:tok], mlpu[:, g, 0:tok], mlpu[:, 4 + g, 0:tok], ALU.mult).then_inc(s("mixed"), 1)
                for f in range(KT):
                    y = ymrg[:, f, 0:tok]
                    for b in range(3):
                        product(dve, "wbo", l, f, 1 if b == 2 else 0)
                        wait_taken(dve, ("mlog", l, b, f))
                        t = y if b == 0 else aux[:, 5 + b, 0:tok]
                        tt_(t, bank(BANK["wbo", l, b, f][0], 0, tok), aux[:, 3 * (f % 2) + b, 0:tok], ALU.mult)\
                            .then_inc(dve_evac, 1)
                        if b > 0:
                            wait_taken(dve, ("wbo", l, b, f))
                            if b == 1:
                                link(tt_(y, y, t, ALU.add))
                            else:
                                tt_(y, y, t, ALU.add).then_inc(s("merged"), 1)
                dve.wait_ge(rstd_ready, 7 + 2 * l)
                for st in range(tok // T):
                    for k in range(KT):
                        x = (h, hc)[st]
                        v = unnormed[:, k, T * st:T * st + T]
                        link(stt(v, v, pgate[:, l, k, st:st + 1], rstd[:, T * st:T * st + T], ALU.mult, ALU.mult))
                        tt_(x[:, k, :], x[:, k, :], v, ALU.add).then_inc(resid_ready if st == 0 else s("ctx_ready"), 1)

        @block.gpsimd
        def _(pool):
            steps = [0]

            def link(ins):
                steps[0] += 1
                ins.then_inc(pool_step, 1)
                pool.wait_ge(pool_step, steps[0])

            pool.wait_ge(s("angle_ready"), 1)
            for i in range(NST):
                for n, tab in enumerate((costab, sintab)):
                    v, k = tab[:, i, :], uT[:, n, :]
                    link(pool.tensor_scalar(v, c("steps"), s5v[:, 6, i:i + 1], 0.25 if n == 0 else 0.0, ALU.mult, ALU.add))
                    link(pool.tensor_scalar(k, v, MAGIC, MAGIC, ALU.add, ALU.subtract))
                    pool.tensor_tensor(v, v, k, ALU.subtract).then_inc(s("turns_ready"), 1)
            link(pool.memset(blk, 0.0))
            pool.memset(kbd, 0.0).then_inc(s("blk_cleared"), 1)
            for i in range(NST):
                pool.wait_ge(s("s5_scanned"), 2 * i + 2)
                if i >= 2:
                    pool.wait_ge(s("s5_y"), i - 1)
                two = lambda v: v.rearrange("p (a b) -> p a b", a=2)
                for dst, tab in ((bakA, costab), (bakB, sintab)):
                    pool.tensor_tensor(two(dst[:, i % 2, :]), two(wst[:, i % 2, :]), tab[:, i, :].unsqueeze(1).broadcast_to([P, 2, T]),
                                       ALU.mult).then_inc(s("s5_back"), 1)
            def rope(part, l):
                n = ROPES[part, l]
                z = (diffz if part[0] == "d" else retz)[:, (0 if part[1] == "k" else 4):(4 if part[1] == "k" else 8), 0:T]
                tmp_c = aux[:, 0:2, :].rearrange("p a b -> p (a b)").rearrange("p (a b) -> p a b", b=T)
                pool.wait_ge(s("rotated2"), n + 1)
                pool.tensor_tensor(tmp_c, z, c("cos" + part[0]).unsqueeze(1).broadcast_to([P, 4, T]), ALU.mult)\
                    .then_inc(s("cos2"), 1)

            def decay_tables(l, hh):
                n = 4 * l + hh
                f, b = dmat[:, hh, :], aux[:, 9, :]
                three = lambda v: v.rearrange("p (a b) -> p a b", a=2)
                pool.wait_ge(s("decay_exp"), 2 * n + 1)
                link(pool.affine_select(out=three(f), in_=three(f), compare_op=ALU.is_ge, fill=0.0, base=0,
                                        pattern=[[-P, 2], [1, T]], channel_multiplier=-1))
                pool.wait_ge(s("decay_exp"), 2 * n + 2)
                pool.affine_select(out=three(b), in_=three(b), compare_op=ALU.is_ge, fill=0.0, base=0,
                                   pattern=[[P, 2], [-1, T]], channel_multiplier=1).then_inc(s("decay_masked"), 1)
                pool.wait_ge(s("decay_masked"), 2 * n + 1)
                pool.tensor_tensor(f, f, b, ALU.add).then_inc(s("decay_masked"), 1)

            def ret(l, step):
                if step < len(RET[l]) and RET[l][step][0] == 0:
                    n, (st, hh) = RET_AT[l] + step, RET[l][step]
                    k = 4 * l + hh
                    if hh == 0:
                        pool.wait_ge(s("states_ready"), 4 * l + 4)
                    if n >= 2:
                        pool.wait_ge(s("ret_out"), n - 1)
                    pool.wait_ge(s("state_decay"), 2 * k + 2)
                    for dr in range(2):
                        v = slice(T * dr, T * dr + T)
                        pool.tensor_tensor(aux[:, 2 + n % 2, v], retz[:, 4 + hh, 0:T], aux[:, 4 + k % 2, v], ALU.mult)\
                            .then_inc(s("q_decayed"), 1)

            for l in range(LAYERS):
                rope("dk", l)
                rope("dq", l)
                for slot in range(len(SLOTS[l])):
                    for kind, step in SLOTS[l][slot]:
                        if kind == "rot":
                            rope(step, l)
                        if kind == "tables":
                            decay_tables(l, step)
                        if kind == "ret":
                            ret(l, step)


def tiles(w, n_out=None):
    k, n = w.shape
    return w.reshape(k // P, P, n // P, P).transpose(2, 1, 0, 3).reshape(n // P, P, k)


def weight_stream(a):
    f32 = np.float32
    out = np.zeros((NU, P, UW), f32)

    def put(name, v):
        v = v.reshape(P, -1)
        out[UNIT[name]][:, 0:v.shape[1]] = v

    for tag in ("ffn1", "ffn2"):
        w1, w3 = tiles(a[tag + "_w1"][0]), tiles(a[tag + "_w3"][0])
        w2 = a[tag + "_w2"][0].reshape(FT, P, D)
        for f in range(FT):
            put((tag, "w1", f), w1[f])
            put((tag, "w3", f), w3[f])
            put((tag, "w2", f), w2[f])
    w = a["w_in"][0]
    at = [HEADS * HD + P * k for k in range(7)]
    q = w[:, 0:512].reshape(D, 2, 4, HD).transpose(0, 2, 1, 3).reshape(D, 512)
    for j, t in enumerate(tiles(q)):
        put(("q", j), t)
    kc, vc, ks, vs, kw, vw = (w[:, at[n]:at[n + 1]] for n in range(6))
    for name, part in (("kc", kc), ("vc", vc), ("ks", ks), ("kw", kw)):
        put((name,), tiles(part)[0])
    gate = w[:, at[6]:at[6] + 24].reshape(D, 2, 4, 3).transpose(0, 3, 2, 1).reshape(D, 24)
    vg = np.concatenate([vs, vw, gate], axis=1).reshape(KT, P, 280).transpose(1, 0, 2)
    for n in range(3):
        put(("vg", n), vg[:, 3 * n:3 * n + 3])
    for j, t in enumerate(tiles(w[:, at[6] + 24:])):
        put(("u", j), t)
    for tag, name in (("cmpk", "cmp_wk1"), ("cmpv", "cmp_wv1")):
        v = a[name][0].reshape(16, P, 256).transpose(1, 0, 2)
        for n in range(4):
            put((tag, n), v[:, 4 * n:4 * n + 4])
    glu = tiles(a["s5_w_glu"][0])
    for n in range(2):
        put(("glu", n), glu[2 * n:2 * n + 2].transpose(1, 0, 2))
    wout = a["w_out"][0]
    wout = np.concatenate([wout[0:512].reshape(2, 4, HD, D).transpose(1, 0, 2, 3).reshape(512, D), wout[512:]], axis=0)
    ple = a["w_ple"][0].reshape(2, P, KT, P).transpose(2, 1, 0, 3).reshape(KT, P, 2 * P)
    for n in range(2):
        put(("plew", n), ple[4 * n:4 * n + 4].transpose(1, 0, 2))
    for name, v in (("wout", wout), ("pleg", a["w_ple_gate"][0])):
        for j, t in enumerate(tiles(v)):
            put((name, j), t)
    order = ["rk", "rv", "dk", "dv", "rq", "rg", "dq", "dg", "mu", "mv", "mg"]
    for l in range(LAYERS):
        for f, t in enumerate(tiles(a["w_mod_2"][l])):
            put(("mod", l, f), t)
        w = a["w_in_2"][l]
        for n, name in enumerate(order):
            part = w[:, BW * n:BW * n + BW]
            if name in ("rv", "dv", "mv"):
                v = part.reshape(KT, P, BW).transpose(1, 0, 2)
                for k in range(4):
                    put((name, l, k), v[:, 2 * k:2 * k + 2])
            else:
                for j, t in enumerate(tiles(part)):
                    put((name, l, j), t)
        for n, t in enumerate(tiles(w[:, 11 * BW:])):
            put(("mlog", l, n // KT, n % KT), t)
        bo = np.stack([tiles(a["w_branch_out_2"][l, b]) for b in range(3)])
        for f in range(KT):
            put(("wbo", l, f, 0), bo[0:2, f].transpose(1, 0, 2))
            put(("wbo", l, f, 1), bo[2, f])
        for j, t in enumerate(tiles(a["w_out_2"][l])):
            put(("wo", l, j), t)
    return out


def rope_table(head, pos_of, half_freqs):
    ang = np.concatenate([pos_of[n][:, None] * half_freqs[n][None, :] for n in range(len(pos_of))], axis=1)
    ang = np.tile(ang.T.astype(np.float32), (P // (head // 2), 1))
    return np.cos(ang).astype(np.float32), np.sin(ang).astype(np.float32)


def shape_constants():
    f32 = np.float32
    t = np.arange(T, dtype=f32)
    v = {"ident": np.eye(P, dtype=f32), "ones": np.ones((P, P), f32)}
    for name, head in (("rot64", 64), ("rot128", 128)):
        m = np.zeros((P, P), f32)
        for d in range(P):
            first = d % head < head // 2
            m[d + head // 2 if first else d - head // 2, d] = -1.0 if first else 1.0
        v[name] = m
    inv = (10000.0 ** (-np.arange(32, dtype=f32) / f32(32))).astype(f32)
    v["cos1"], v["sin1"] = rope_table(64, [t], [inv])
    row, colp = np.repeat(np.arange(T // 64, dtype=f32), 64), np.tile(np.arange(64, dtype=f32), T // 64)
    for name, head in (("r", 128), ("d", 64)):
        nf = head // 4
        inv = (10000.0 ** (-np.arange(nf, dtype=f32) / f32(nf))).astype(f32)
        v["cos" + name], v["sin" + name] = rope_table(head, [row, colp], [inv, inv])
    p = np.arange(P)
    v["causal"] = np.where(p[None, :] <= p[:, None], 0.0, NEG).astype(f32)
    q = p[:, None, None] + P * np.arange(2)[None, :, None]
    blk = np.arange(16)[None, None, :]
    ok = ((blk * CSTR + CLEN - 1 <= q) & (blk < NCMP)).reshape(P, 32)
    v["cmask"] = ok.astype(f32)
    v["cneg"] = np.where(ok, 0.0, NEG).astype(f32)
    v["gmask"] = np.stack([p // 16 % 2 == 0, p // 16 % 2 == 1], axis=1).astype(f32)
    v["steps"] = np.tile(t, (P, 1))
    v["dist"] = (t[None, None, :] - (p[:, None, None] + P * np.arange(2)[None, :, None])).reshape(P, 2 * T).astype(f32)
    j = p[:, None] + P * np.arange(2)[None, :]
    v["jrow"] = np.concatenate([T - 1 - j, j], axis=1).astype(f32)
    return v


def small_inputs(a):
    f32 = np.float32
    cols = lambda v: np.asarray(v, f32).reshape(-1, P).T
    wide = lambda v: np.tile(np.asarray(v, f32).reshape(1, -1), (P, 1))
    v = shape_constants()
    for name, key in (("g_ffn1", "norm_ffn1"), ("g_mix", "norm_mix"), ("g_ffn2", "norm_ffn2"), ("g_ple", "norm_ple"),
                      ("g_final", "norm_final"), ("g_pre", "g_pre_2"), ("g_post", "g_post_2"), ("b_mod", "b_mod_2"),
                      ("b_glu", "s5_b_glu"), ("s5_d", "s5_d"), ("a_re", "s5_a_re"), ("a_im", "s5_a_im")):
        v[name] = cols(a[key])
    v["log_dt"] = cols(np.repeat(a["s5_log_dt"][0], 64))
    for name, key in (("b_re", "s5_b_re"), ("b_im", "s5_b_im"), ("c_re", "s5_c_re"), ("c_im", "s5_c_im")):
        m = a[key][0] if name[0] == "b" else a[key][0].transpose(0, 2, 1)
        out = np.zeros((2, 64, NST, 2, 16), f32)
        m = m.reshape(NST, 2, 64, 16)
        for g in range(2):
            out[g, :, :, g, :] = m[:, g].transpose(1, 0, 2)
        v[name] = out.reshape(P, 512)
    v["pe"] = np.concatenate([a[k][0].reshape(16, P).T for k in ("cmp_pe_k", "cmp_pe_v")], axis=1)
    for name, key in (("w2k", "cmp_wk2"), ("w2v", "cmp_wv2")):
        v[name] = a[key][0].reshape(2, P, HD).transpose(1, 0, 2).reshape(P, P)
    v["cc"] = np.stack([a["c_2"][0].reshape(KT, P).T, a["c_ctx_2"].reshape(KT, P).T], axis=2).reshape(P, 16)
    v["lamq"], v["lamk"], v["ret_logit"] = wide(a["diff_lambda_q_2"]), wide(a["diff_lambda_k_2"]), wide(a["ret_decay_logit_2"])
    v["wsT"] = a["mlp_w_s_2"].transpose(3, 0, 1, 2).reshape(P, 2 * 4 * P)
    v["pT"] = a["p"][0, 0].T.reshape(2, P, T).transpose(1, 0, 2).reshape(P, 2 * T)
    return np.ascontiguousarray(np.concatenate([np.asarray(v[n], f32).reshape(P, w) for n, w in PACK], axis=1))


def kernel(**inputs):
    import concourse.bacc as bacc
    from concourse.bass_utils import run_bass_kernel_spmd

    a = {k: np.asarray(v) for k, v in inputs.items()}
    by_feature = lambda x: np.ascontiguousarray(x[0].T.reshape(KT, P, T).transpose(1, 0, 2))
    arrays = {
        "stream": weight_stream(a),
        "pack": small_inputs(a),
        "bs_rows": np.ascontiguousarray(a["mlp_b_s_2"].reshape(1, 2 * BW)),
        "x_in": by_feature(a["x"]),
        "ctx_in": by_feature(a["ctx_2"]),
    }
    nc = bacc.Bacc("TRN2", target_bir_lowering=False, num_devices=1)
    args = [nc.dram_tensor(n, v.shape, mybir.dt.from_np(v.dtype), kind="ExternalInput").ap() for n, v in arrays.items()]
    out = nc.dram_tensor("out", (P, KT, T), F32, kind="ExternalOutput").ap()
    two_block_kernel(nc, *args, out)
    r = run_bass_kernel_spmd(nc, [arrays], core_ids=[0])
    y = r.results[0]["out"]
    return np.ascontiguousarray(y.transpose(1, 0, 2).reshape(D, T).T)[None]
```

```python
from contextlib import ExitStack

import numpy as np

import concourse.bass as bass
from concourse import mybir

ACT = mybir.ActivationFunctionType
ALU = mybir.AluOpType
AX_X = mybir.AxisListType.X
F32 = mybir.dt.float32
F32R = mybir.dt.float32r
I32 = mybir.dt.int32
BF16 = mybir.dt.bfloat16

P = 128
AREA = 25472
D = 1024
KT = D // P
T = 256
TT = T // P
FF = 2816
FT = FF // P
UW = 1024
RING = 4
HI = 3
HEADS, HD = 8, 64
NCMP, CLEN, CSTR = 15, 32, 16
NST = 16
BW = 512
EPS = 1e-6
NEG = -1e30
LAYERS = 2
MODS = LAYERS * 3 * KT
LAM_INIT = [0.8 - 0.6 * float(np.exp(-0.3 * l)) for l in range(LAYERS)]
INV2PI = float(np.float32(1.0 / (2.0 * np.pi)))
TWO_PI = float(np.nextafter(np.float32(2.0 * np.pi), np.float32(0.0)))
PI2_HI = 6.28125
PI2_LO = float(np.float32(2.0 * np.pi - 6.28125))
MAGIC = float(np.float32(1.5 * 2 ** 23))
LOG2E = float(np.float32(np.log2(np.e)))
LN2_HI = 0.693359375
LN2_LO = float(np.float32(np.log(2.0) - 0.693359375))
TAYLOR = [1.0 / 5040, 1.0 / 720, 1.0 / 120, 1.0 / 24, 1.0 / 6, 0.5, 1.0]


def stream_plan():
    names = []

    def ffn(tag):
        names.extend([(tag, "w1", 0), (tag, "w3", 0)])
        for f in range(FT - 1):
            names.extend([(tag, "w1", f + 1), (tag, "w3", f + 1), (tag, "w2", f)])
        names.append((tag, "w2", FT - 1))

    ffn("ffn1")
    names.extend([("u", j) for j in range(4)] + [("kc",), ("vc",)])
    names.extend([("q", j) for j in range(4)] + [("ks",), ("kw",)])
    names.extend([("vg", c) for c in range(3)])
    names.extend([("cmpk", c) for c in range(4)] + [("cmpv", c) for c in range(4)])
    names.extend([("glu", c) for c in range(2)])
    names.extend([("wout", j) for j in range(KT)])
    ffn("ffn2")
    names.extend([("plew", c) for c in range(2)] + [("pleg", j) for j in range(KT)])
    for l in range(LAYERS):
        for part in ("dk", "dq"):
            names.extend([(part, l, j) for j in range(4)])
        names.extend([("dv", l, c) for c in range(4)])
        names.extend([("dg", l, j) for j in range(4)])
        for part in ("rk", "rq"):
            names.extend([(part, l, j) for j in range(4)])
        names.extend([("rv", l, c) for c in range(4)])
        names.extend([("rg", l, j) for j in range(4)])
        names.extend([("mv", l, c) for c in range(4)])
        names.extend([(part, l, j) for part in ("mu", "mg") for j in range(4)])
        for f in range(KT):
            names.extend([("mlog", l, b, f) for b in range(3)] + [("wbo", l, f, 0), ("wbo", l, f, 1)])
        names.extend([("wo", l, j) for j in range(KT)])
    return names


UNITS = stream_plan()
UNIT = {name: i for i, name in enumerate(UNITS)}
NU = len(UNITS)

SPLIT_KINDS = ("ffn1", "ffn2", "u", "kc", "vc", "q", "ks", "kw", "vg", "pleg", "dk", "dq", "dv", "dg",
               "rk", "rq", "rv", "rg", "mv", "mu", "mg", "mlog", "wo")
SPLIT_UNITS = [name for name in UNITS if name[0] in SPLIT_KINDS]
SPLIT = {name: n for n, name in enumerate(SPLIT_UNITS)}
FU = 3 * FT
LOW = {}
for _name in SPLIT_UNITS:
    _who = "dve" if _name[0] in ("ffn1", "ffn2") else "pool"
    LOW[_name] = (_who, 1 + sum(1 for w, _ in LOW.values() if w == _who))

PACK = [
    ("g_ffn1", 8), ("g_mix", 8), ("g_ffn2", 8), ("g_ple", 8), ("g_final", 8), ("g_pre", 16), ("g_post", 16),
    ("b_mod", 48), ("pT", 512), ("ident", 128), ("ones", 128), ("rot64", 128), ("steps", 256),
]
PACK1 = [
    ("a_re", 16), ("a_im", 16), ("log_dt", 16), ("s5_d", 4), ("b_glu", 4), ("b_re", 512),
    ("b_im", 512), ("c_re", 512), ("c_im", 512), ("pe", 32), ("w2k", 128), ("w2v", 128),
    ("cos1", 256), ("sin1", 256), ("causal", 128), ("cmask", 32), ("cneg", 32), ("gmask", 2),
]
PACK2 = [
    ("lamq", 256), ("lamk", 256), ("ret_logit", 16), ("wsT", 1024), ("rot128", 128),
    ("cosr", 256), ("sinr", 256), ("cosd", 256), ("sind", 256), ("dist", 512), ("jrow", 4),
]
width = lambda parts: sum(n for _, n in parts)
OFF = {}
for _parts, _base in ((PACK, 0), (PACK1, width(PACK)), (PACK2, width(PACK))):
    for _k, (_name, _n) in enumerate(_parts):
        OFF[_name] = (_base + width(_parts[:_k]), _n)
NPK = width(PACK) + max(width(PACK1), width(PACK2))

BANK_USES = (
    [(("u", j), "act") for j in range(4)] + [(("kc",), "act"), (("vc",), "act")]
    + [(("q", j), "act") for j in range(4)] + [(("ks",), "act"), (("kw",), "act")]
    + [(("vg", t), "act") for t in range(2)]
    + [(("glu", j), "act") for j in range(4)]
    + [(("wout", j), "dve") for j in range(KT)]
)
BANK_USES += [(("plew", _j), "act") for _j in range(4)] + [(("pleg", _j), "act") for _j in range(KT)]
for _l in range(LAYERS):
    for _p in ("d", "r"):
        for _part in (_p + "k", _p + "q"):
            BANK_USES += [((_part, _l, j), "act") for j in range(4)]
        BANK_USES += [((_p + "v", _l, t), "act") for t in range(4)]
        BANK_USES += [((_p + "g", _l, j), "act") for j in range(4)]
    BANK_USES += [(("mv", _l, t), "dve") for t in range(4 if _l == 0 else 2)]
    BANK_USES += [((part, _l, j), "act") for part in ("mu", "mg") for j in range(4)]
    for _f in range(KT):
        BANK_USES += [(("mlog", _l, _b, _f), "act") for _b in range(3)]
        BANK_USES += [(("wbo", _l, _b, _f), "dve") for _b in range(3)]
    BANK_USES += [(("wo", _l, j), "act") for j in range(KT)]
BANK = {}
_taken = {"act": 0, "dve": 0}
for _n, (_name, _eng) in enumerate(BANK_USES):
    _taken[_eng] += 1
    BANK[_name] = (_n % 4, _n, _eng, _taken[_eng])


NORMED = [0, 8, 16, 24]
RESID_BLOCK2 = 4 + 4 + KT + KT
DIFF = [[(st, hh, qt) for st in streams for hh in range(4) for qt in range(2)] for streams in ((0, 1), (0,))]
RET = [[(st, hh) for st in streams for hh in range(4)] for streams in ((0, 1), (0,))]
DIFF_AT = [0, len(DIFF[0]), len(DIFF[0]) + len(DIFF[1])]
HEAD_AT = [n // 2 for n in DIFF_AT]
RET_AT = [0, len(RET[0]), len(RET[0]) + len(RET[1])]
VN_AT = [0, 4, 6]
ROPES = {(part, l): 4 * l + n for l in range(LAYERS) for n, part in enumerate(("dk", "dq", "rk", "rq"))}


def slot_units(l):
    return [(part, l, j) for part in ("rk", "rq", "rv", "rg", "mv", "mu", "mg") for j in range(4)]


def head_steps(l):
    slots = [[] for _ in slot_units(l)]
    for hh in range(4):
        slots[hh].append(("tables", hh))
    for step in range(len(DIFF[l]) + 2):
        slots[step // 2 if l == 0 else step].append(("diff", step))
    slots[11].append(("rot", "rk"))
    slots[12].append(("rot", "rq"))
    for step in range(len(RET[l]) + 2):
        slots[16 + step].append(("ret", step))
    return slots


SLOTS = [head_steps(l) for l in range(LAYERS)]


def two_block_kernel(nc, stream, mod_stream, cond, pack, pack2, bs_rows, x_in, ctx_in, out):
    with ExitStack() as es:
        def sb(name, shape, dt=F32):
            return es.enter_context(nc.sbuf_tensor(name, shape, dt))

        def sem(name):
            return es.enter_context(nc.semaphore(name))

        pk = sb("pk", [P, NPK])

        def c(name, a=0, b=None):
            off, n = OFF[name]
            return pk[:, off + a:off + (n if b is None else b)]

        with nc.sbuf_tensor("ring", [P, RING, UW], F32) as ring:
            pass
        w_lo = sb("w_lo", [P, RING, UW], F32R)
        w_hi = sb("w_hi", [P, HI, UW], F32R)
        bsrow = sb("bsrow", [1, 2 * BW])
        h = sb("h", [P, KT, T])
        hc = sb("hc", [P, KT, T])
        with nc.sbuf_tensor("cond_at", [P, KT, 2 * T], F32) as cond_at:
            pass
        hn_hi = sb("hn_hi", [P, KT, 2 * T], F32R)
        with nc.sbuf_tensor("mod_at", [P, KT, 2 * T], F32) as mod_at:
            pass
        hn_lo = sb("hn_lo", [P, KT, 2 * T], F32R)
        hn = [hn_hi, hn_lo]
        quarter = lambda v: v.rearrange("p (a b) -> p a b", a=4)
        mod_slot = lambda m: mod_at[:, 4 * (m % 2):4 * (m % 2) + 4, T:2 * T]
        cond_silu = lambda st: cond_at[:, 4 * st:4 * st + 4, T:2 * T]
        lnr = sb("lnr", [P, 2 * T])
        rstd = sb("rstd", [P, 2 * T])
        eps = sb("eps", [P, 1])
        negc = sb("negc", [P, P], BF16)
        idb = sb("idb", [P, P], BF16)
        mods = sb("mods", [P, LAYERS, 3 * KT, 2])
        amp = sb("amp", [P, LAYERS, KT, 2])
        pgate = sb("pgate", [P, LAYERS, KT, 2])
        with nc.sbuf_tensor("hid_hi", [P, 4, T], F32R) as hid_hi, nc.sbuf_tensor("hid_lo", [P, 4, T], F32R) as hid_lo:
            pass
        hid = [hid_hi, hid_lo]
        area = sb("area", [P, AREA])

        class Area:
            at = 0

        def cut(*shape):
            n = int(np.prod(shape))
            v = area[:, Area.at:Area.at + n]
            Area.at += n
            if len(shape) == 2:
                v = v.rearrange("p (a b) -> p a b", a=shape[0])
            if len(shape) == 3:
                v = v.rearrange("p (a b c) -> p a b c", a=shape[0], b=shape[1])
            return v

        bakA = cut(2, 2 * T)
        bakB = cut(2, 2 * T)
        sil = cut(4, T)
        sq = cut(KT, 2 * T)
        yg = sil
        costab = cut(NST, T)
        sintab = cut(NST, T)
        uT = cut(4, T)
        bT = cut(2, 4, P)
        cneg_re = cut(512)
        cneg_im = cut(512)
        s5v = cut(24, NST)
        zq = cut(7, T)
        vcT = cut(T)
        vtok = cut(2, 280)
        gates = cut(2, 24)
        blk_all = cut(2 * 16 * 32)
        blk = blk_all.rearrange("p (a b) -> p a b", a=2)
        ghid = cut(2, 2 * 32)
        grep = cut(2, P)
        kbd = cut(32)
        vbd = cut(P)
        csc = cut(2 * P)
        cex = cut(2 * P)
        gelu_rows = [csc, cex]
        cst = cut(4, NST)
        pct = cut(2 * P)
        exprob = cut(2, 2, 384)
        ex, prob = exprob[:, 0, :, :], exprob[:, 1, :, :]
        bre, bim = (exprob[:, n, :, :].rearrange("p a b -> p (a b)")[:, 0:512] for n in range(2))
        pt = blk_all[:, 0:2 * 384].rearrange("p (a b) -> p a b", a=2)
        stat = cut(2, 16)
        oT = hc
        rotA, rotB, zin, wst = (sq[:, 2 * n:2 * n + 2, :] for n in range(4))
        sg = zq
        pwp = costab
        plg = sintab
        assert Area.at <= AREA, Area.at
        Area.at = 0
        diffz = cut(12, 2 * T)
        diffv = cut(4, BW)
        retz = cut(12, 2 * T)
        retv = cut(4, BW)
        mlpu = diffz
        dmat = cut(4, 2 * T)
        aux = cut(10, 2 * T)
        lay = cut(LAYERS, 40)
        st2 = cut(2, 16)
        states = cut(2, 4, P)
        ktok = cut(2, 2, P)
        sp = cut(4, 16)
        assert Area.at <= AREA, Area.at
        o_dif, o_ret, o_mlp = diffz[:, 8:12, :], retz[:, 8:12, :], mlpu[:, 0:4, :]
        ymrg = retz
        sq2 = aux
        vn = diffv
        unnormed = diffz

        ps = es.enter_context(nc.psum_tensor("ps", [P, 8 * 512], F32))

        def bank(b, a=0, n=512):
            return ps[:, 512 * b + a:512 * b + a + n]

        consts_loaded = sem("consts_loaded")
        block1_loaded = sem("block1_loaded")
        block2_loaded = sem("block2_loaded")
        hi_ready = sem("hi_ready")
        lo_ready = {"dve": sem("lo_ready_dve"), "pool": sem("lo_ready_pool")}
        unit_loaded = [sem(f"unit_loaded{s}") for s in range(RING)]
        units_multiplied = sem("units_multiplied")
        act_evac = sem("act_evac")
        dve_evac = sem("dve_evac")
        dve_step = sem("dve_step")
        act_step = sem("act_step")
        pool_step = sem("pool_step")
        squares_ready = sem("squares_ready")
        sumsq_ready = sem("sumsq_ready")
        rstd_ready = sem("rstd_ready")
        scaled_ready = sem("scaled_ready")
        normed_ready = sem("normed_ready")
        silu_ready = sem("silu_ready")
        hidden_ready = sem("hidden_ready")
        resid_ready = sem("resid_ready")
        masks_ready = sem("masks_ready")
        cs_ready = sem("cs_ready")
        mods_ready = sem("mods_ready")
        stored = sem("stored")
        S = {}

        def s(name):
            if name not in S:
                S[name] = sem(name)
            return S[name]

        EV = {"act": act_evac, "dve": dve_evac}

        def wait_taken(eng, name):
            _, _, who, count = BANK[name]
            eng.wait_ge(EV[who], count)

        def bank_free(pe, name):
            n = BANK[name][1]
            if n >= 4:
                wait_taken(pe, BANK_USES[n - 4][0])

        def product(eng, *name):
            eng.wait_ge(units_multiplied, UNIT[name] + 1)

        def w_parts(name):
            return w_hi[:, SPLIT[name] % HI, :], w_lo[:, UNIT[name] % RING, :]

        def low_part(eng, name, body=0):
            who, count = LOW[name]
            raw = ring[:, UNIT[name] % RING, :]
            hi, lo = w_parts(name)
            eng.wait_ge(hi_ready, SPLIT[name] + 1 + body)
            eng.tensor_tensor(lo, raw, hi.bitcast(F32), ALU.subtract).then_inc(lo_ready[who], 1)

        def load_mod(eng, m, body=0, first=False):
            if not first:
                eng.wait_ge(s("mod_used"), m - 1 + body)
            eng.dma_start(mod_slot(m), mod_stream[m + body]).then_inc(s(f"mod_loaded{m % 2}"), 16)

        DT, LRE, LIM, R, K, GC, GS, COS, SIN, PR, QI, DEN, CR, CI, TMP = range(15)

        NC_DMAS = 2
        block = es.enter_context(nc.Block())

        @block.sync
        def _(sp):
            sp.dma_start(h[:, :, :], x_in).then_inc(consts_loaded, 16)
            sp.dma_start(pk[:, 0:width(PACK)], pack[:, 0:width(PACK)]).then_inc(consts_loaded, 16)
            for u in range(RING):
                sp.dma_start(ring[:, u, :], stream[u]).then_inc(unit_loaded[u], 16)
            sp.dma_start(pk[:, width(PACK):width(PACK + PACK1)], pack[:, width(PACK):]).then_inc(block1_loaded, 16)
            for st in range(2):
                sp.dma_start(cond_silu(st), cond[:, st]).then_inc(s("cond_loaded"), 16)
            for m in range(2):
                load_mod(sp, m, first=True)
            sp.dma_start(bsrow[:, :], bs_rows).then_inc(block1_loaded, 16)
            rounds = NU // RING
            with sp.Fori(1, rounds) as r:
                for u in range(RING):
                    sp.wait_ge(units_multiplied, RING * r + (u + 1 - RING))
                    sp.dma_start(ring[:, u, :], stream[RING * r + u]).then_inc(unit_loaded[u], 16)
            for u in range(rounds * RING, NU):
                sp.wait_ge(units_multiplied, u + 1 - RING)
                sp.dma_start(ring[:, u % RING, :], stream[u]).then_inc(unit_loaded[u % RING], 16)
            sp.wait_ge(resid_ready, RESID_BLOCK2 + LAYERS * KT)
            sp.dma_start(out, h[:, :, :]).then_inc(stored, 16)
            sp.wait_ge(stored, 16)

        @block.tensor
        def _(pe):
            def unit(name, rounds=0):
                u = UNIT[name]
                pe.wait_ge(unit_loaded[u % RING], 16 * (u // RING + 1) + 16 * rounds)
                return ring[:, u % RING, :]

            def split_unit(name, body=0):
                who, count = LOW[name]
                pe.wait_ge(lo_ready[who], count + body)
                return w_parts(name)

            def exact(dst, weights, wcols, x, xcols, start, stop, x_stationary=False):
                for n, (a, b) in enumerate(((0, 0), (0, 1), (1, 0))):
                    w_, x_ = weights[a][wcols], x[b][xcols]
                    if x_stationary:
                        w_, x_ = x_, w_
                    m = pe.matmul(dst, w_, x_, start=(start and n == 0), stop=(stop and n == 2), skip_group_check=True)
                return m

            all_p, all_t = slice(0, P), slice(0, T)

            def sumsq(n, tokens):
                for k in range(KT):
                    pe.wait_ge(squares_ready, KT * n + k + 1)
                    src = (sq if n < 5 else sq2)[:, k, 0:tokens]
                    m = pe.matmul(bank(7, 0, tokens), c("ones"), src, start=(k == 0), stop=(k == KT - 1))
                m.then_inc(sumsq_ready, 1)

            def ffn(tag, n_norm, n_ffn):
                sumsq(n_norm, T)

                def up(f, body=0):
                    for half, w in enumerate(("w1", "w3")):
                        wt = split_unit((tag, w, f), body)
                        for k in range(KT):
                            if f == 0 and half == 0:
                                pe.wait_ge(normed_ready, NORMED[n_norm] + k + 1)
                            m = exact(bank(4 + f % 4, T * half, T), wt, (all_p, slice(P * k, P * k + P)),
                                      hn, (all_p, k, slice(0, T)), k == 0 and half == 0, k == KT - 1)
                        m.then_inc(units_multiplied, 1)

                def down(f, body=0, hidden=0):
                    wt = split_unit((tag, "w2", f), body)
                    pe.wait_ge(hidden_ready, FT * n_ffn + f + 1 + hidden)
                    for j in range(KT):
                        m = exact(bank(j // 2, T * (j % 2), T), wt, (all_p, slice(P * j, P * j + P)),
                                  hid, (all_p, f % 4, all_t), f == 0 and j % 2 == 0, f == FT - 1)
                    m.then_inc(units_multiplied, 1)

                up(0)
                up(1)
                down(0)
                with pe.Fori(0, (FT - 2) // 4) as it:
                    for f in range(1, 5):
                        up(f + 1, 12 * it)
                        down(f, 12 * it, 4 * it)
                down(FT - 1)

            pe.wait_ge(consts_loaded, 16 * NC_DMAS)
            ffn("ffn1", 0, 0)
            pe.wait_ge(block1_loaded, 32)
            pe.wait_ge(s("s5_b_ready"), 2)
            for part, src in enumerate((bre, bim)):
                for j in range(4):
                    m = pe.transpose(bank(4 + part, P * j, P), src[:, P * j:P * j + P], c("ident"))
            m.then_inc(s("s5_bt"), 1)

            sumsq(1, T)

            def project(name, first=False, tokens=T, cols=None, n_norm=0, kt=KT, src=None):
                split = name in SPLIT
                wt = split_unit(name) if split else unit(name)
                bank_free(pe, name)
                b = BANK[name][0]
                for k in range(kt):
                    if first:
                        pe.wait_ge(normed_ready, NORMED[n_norm] + k + 1)
                    if split:
                        m = exact(bank(b, 0, tokens), wt, (all_p, slice(P * k, P * k + P)), hn, (all_p, k, slice(0, tokens)),
                                  k == 0, k == kt - 1)
                    else:
                        m = pe.matmul(bank(b, 0, tokens), wt[:, P * k:P * k + P], src[:, k, 0:tokens],
                                      start=(k == 0), stop=(k == kt - 1))
                m.then_inc(units_multiplied, 1)

            for j in range(4):
                project(("u", j), first=(j == 0), n_norm=1)
            project(("kc",))
            project(("vc",))

            def rotate(src, dst, rot, who, count):
                pe.wait_ge(who, count)
                return pe.matmul(dst, c(rot), src, start=True, stop=True)

            rotations = [("q", 0), ("q", 1), ("q", 2), ("q", 3), ("ks",), ("kw",), ("kc",)]

            def rotate_tile(n):
                wait_taken(pe, rotations[n])
                return pe.matmul(ps[:, 4 * 512 + T * n:4 * 512 + T * n + T], c("rot64"), zq[:, n, :],
                                 start=(n % 2 == 0), stop=True, skip_group_check=True)

            for j in range(4):
                project(("q", j))
                if j == 0:
                    rotate_tile(6).then_inc(s("rotated"), 1)
            project(("ks",))
            project(("kw",))
            for cc_ in range(3):
                wt = split_unit(("vg", cc_))
                for tt in range(2):
                    if cc_ == 0:
                        bank_free(pe, ("vg", tt))
                    for k in range(3 * cc_, min(3 * cc_ + 3, KT)):
                        m = exact(bank(BANK["vg", tt][0], 0, 280), wt, (all_p, slice(280 * (k - 3 * cc_), 280 * (k - 3 * cc_) + 280)),
                                  hn, (all_p, k, slice(P * tt, P * tt + P)), k == 0, k == KT - 1, x_stationary=True)
                m.then_inc(units_multiplied, 1)
            for n in range(6):
                m = rotate_tile(n)
            m.then_inc(s("rotated"), 1)
            for kv, tag in enumerate(("cmpk", "cmpv")):
                for cc_ in range(4):
                    wt = unit((tag, cc_))
                    if cc_ == 0:
                        pe.wait_ge(s("blk_ready"), kv + 1)
                        wait_taken(pe, ("vg", 1))
                    for lp in range(4 * cc_, 4 * cc_ + 4):
                        m = pe.matmul(ps[0:32, 512 * kv:512 * kv + 256], blk[:, kv, 32 * lp:32 * lp + 32],
                                      wt[:, 256 * (lp % 4):256 * (lp % 4) + 256], start=(lp == 0), stop=(lp == 15))
                    m.then_inc(units_multiplied, 1)
            for kv in range(2):
                pe.wait_ge(s("cmp_hidden"), kv + 1)
                for ht in range(2):
                    m = pe.transpose(bank(kv, 32 * ht, 32), gelu_rows[kv][0:32, P * ht:P * ht + P], c("ident")[0:32, 0:32])
                m.then_inc(s("cmp_turned"), 1)
            pe.wait_ge(s("ghid_ready"), 1)
            for g in range(2):
                for ht in range(2):
                    m = pe.matmul(ps[HD * g:HD * g + HD, 2 * 512:2 * 512 + 16], c("w2k", HD * ht, HD * ht + HD),
                                  ghid[:, 0, 32 * ht + 16 * g:32 * ht + 16 * g + 16], start=(ht == 0), stop=(ht == 1))
            m.then_inc(s("kcmp"), 1)
            pe.wait_ge(s("grep_ready"), 1)
            for ht in range(2):
                m = pe.matmul(bank(3, 0, HD), grep[:, ht, :], c("w2v", HD * ht, HD * ht + HD), start=(ht == 0), stop=(ht == 1))
            m.then_inc(s("vcmp"), 1)
            pe.wait_ge(s("kbd_ready"), 2)
            pe.wait_ge(s("roped"), 3)
            for qt in range(2):
                for j in range(4):
                    m = pe.matmul(bank(0, P * qt + 32 * j, 32), zq[:, j, P * qt:P * qt + P], kbd, start=True, stop=True)
            m.then_inc(s("cmp_scores"), 1)
            pe.wait_ge(s("cmp_probs"), 1)
            for qt in range(2):
                m = pe.transpose(bank(1, P * qt, P), cex[:, P * qt:P * qt + P], c("ident"))
            m.then_inc(s("cmp_probsT"), 1)
            pe.wait_ge(s("vbd_ready"), 2)
            pe.wait_ge(s("pct_ready"), 1)

            def s5_in(i):
                if i == 0:
                    pe.wait_ge(s("s5_b_copied"), 1)
                    wait_taken(pe, ("u", 3))
                    pe.wait_ge(s("roped"), 3)
                if i >= 1:
                    pe.wait_ge(s("s5_prod"), i)
                rows = slice(32 * (i % 4), 32 * (i % 4) + 32)
                for part in range(2):
                    m = pe.matmul(bank(6, T * part, T), bT[rows, part, i // 4, :], uT[rows, i // 4, :],
                                  start=(part == 0), stop=True, skip_group_check=True)
                m.then_inc(s("s5_bu"), 1)

            def s5_out(i):
                pe.wait_ge(s("s5_back"), 2 * i + 2)
                if i % 4 == 0 and i >= 4:
                    pe.wait_ge(s("s5_y_taken"), i // 4)
                rows = slice(32 * (i % 4), 32 * (i % 4) + 32)
                o = ps[rows, 7 * 512 + T * (i // 4 % 2):7 * 512 + T * (i // 4 % 2) + T]
                cols = slice(32 * i, 32 * i + 32)
                a, b2 = bakA[:, i % 2, :], bakB[:, i % 2, :]
                pe.matmul(o, c("c_re")[:, cols], a[:, 0:T], start=True, stop=False, skip_group_check=True)
                pe.matmul(o, cneg_re[:, cols], b2[:, T:2 * T], start=False, stop=False, skip_group_check=True)
                pe.matmul(o, cneg_im[:, cols], a[:, T:2 * T], start=False, stop=False, skip_group_check=True)
                pe.matmul(o, cneg_im[:, cols], b2[:, 0:T], start=False, stop=True, skip_group_check=True)\
                    .then_inc(s("s5_y"), 1)

            def scores(i):
                if i == 0:
                    pe.wait_ge(masks_ready, 2)
                j, g, br = i // 4, i // 2 % 2, i % 2
                if i >= 2:
                    pe.wait_ge(s("exps"), 2 * (i - 1))
                rows = slice(HD * g, HD * g + HD)
                kk = zq[rows, 4 + br, :]
                o = bank(i % 2)
                pe.matmul(o[:, 0:P], zq[rows, j, 0:P], kk[:, 0:P], start=True, stop=False, skip_group_check=True)
                pe.matmul(o[:, P:3 * P], zq[rows, j, P:2 * P], kk[:, 0:2 * P], start=False, stop=False, skip_group_check=True)
                pe.matmul(o[:, 0:P], idb[:, :], negc[:, :], start=False, stop=True, skip_group_check=True)
                pe.matmul(o[:, 2 * P:3 * P], idb[:, :], negc[:, :], start=False, stop=True, skip_group_check=True)\
                    .then_inc(s("scored"), 1)

            def turn(i):
                pe.wait_ge(s("probs"), 2 * i + 2)
                if i >= 2:
                    pe.wait_ge(s("pt_ready"), i - 1)
                for n in range(3):
                    m = pe.transpose(bank(2 + i % 2, P * n, P), prob[:, i % 2, P * n:P * n + P], c("ident"))
                m.then_inc(s("turned"), 1)

            def weigh(i):
                j, g, br = i // 4, i // 2 % 2, i % 2
                pe.wait_ge(s("pt_ready"), i + 1)
                if i % 4 == 0 and i >= 4:
                    pe.wait_ge(s("o_taken"), j)
                col = 5 * 512 + T * (j % 2)
                rows = slice(HD * g, HD * g + HD)
                if i % 4 == 0:
                    pe.matmul(ps[:, col:col + T], vbd[32 * j:32 * j + 32, :], pct[32 * j:32 * j + 32, :],
                              start=True, stop=False, skip_group_check=True)
                vv = P * br + HD * g
                pe.matmul(ps[rows, col:col + T], vtok[:, 0, vv:vv + HD], pt[:, i % 2, 0:2 * P],
                          start=False, stop=False, skip_group_check=True)
                pe.matmul(ps[rows, col + P:col + T], vtok[:, 1, vv:vv + HD], pt[:, i % 2, 2 * P:3 * P],
                          start=False, stop=(br == 1), skip_group_check=True).then_inc(s("weighed"), 1)

            for i in range(NST + 2):
                if i < NST:
                    s5_in(i)
                    scores(i)
                if 1 <= i <= NST:
                    turn(i - 1)
                if 1 <= i <= NST:
                    s5_out(i - 1)
                if i >= 2:
                    weigh(i - 2)
            for cc_ in range(2):
                wt = unit(("glu", cc_))
                for j in (2 * cc_, 2 * cc_ + 1):
                    bank_free(pe, ("glu", j))
                    if j == 0:
                        pe.wait_ge(s("pt_ready"), NST)
                        pe.wait_ge(s("gelu_ready"), 4)
                    for k in range(4):
                        m = pe.matmul(bank(BANK["glu", j][0], 0, T), wt[:, 512 * (j % 2) + P * k:512 * (j % 2) + P * k + P],
                                      yg[:, k, :], start=(k == 0), stop=(k == 3))
                m.then_inc(units_multiplied, 1)
            for j in range(KT):
                if j == 0:
                    pe.wait_ge(s("o_taken"), 4)
                    pe.wait_ge(s("s5_out"), 4)
                project(("wout", j), src=oT)

            ffn("ffn2", 2, 1)
            for cc_ in range(2):
                wt = unit(("plew", cc_))
                for j in range(4):
                    if j % 2 == 0:
                        b = BANK["plew", 2 * cc_ + j // 2][0]
                        if cc_ == 0 and j == 0:
                            pe.wait_ge(resid_ready, 8)
                    for k in range(2):
                        m = pe.matmul(bank(b, T * (j % 2), T), wt[:, P * (2 * j + k):P * (2 * j + k) + P],
                                      c("pT", T * k, T * k + T), start=(k == 0 and j % 2 == 0), stop=(k == 1),
                                      skip_group_check=True)
                m.then_inc(units_multiplied, 1)
            sumsq(3, T)
            for j in range(KT):
                project(("pleg", j), first=(j == 0), n_norm=3)
            sumsq(4, T)

            def project2(name, l, tokens, first=False, src=None):
                split = name in SPLIT
                wt = split_unit(name) if split else unit(name)
                bank_free(pe, name)
                o = bank(BANK[name][0], 0, tokens)
                for k in range(KT):
                    if first:
                        pe.wait_ge(*((s("y_low"), KT * l + k + 1) if name[0] == "wo" else (s("modulated"), 16 * l + 2 * k + 2)))
                    if split:
                        m = exact(o, wt, (all_p, slice(P * k, P * k + P)), hn, (all_p, k, slice(0, tokens)), k == 0, k == KT - 1)
                    else:
                        m = pe.matmul(o, wt[:, P * k:P * k + P], src[:, k, 0:tokens], start=(k == 0), stop=(k == KT - 1))
                m.then_inc(units_multiplied, 1)

            def project_values(part, l, cc_, tiles):
                wt = split_unit((part, l, cc_))
                for tt in range(tiles):
                    if cc_ == 0:
                        bank_free(pe, (part, l, tt))
                    for k in range(2):
                        m = exact(bank(BANK[part, l, tt][0]), wt, (all_p, slice(BW * k, BW * k + BW)),
                                  hn, (all_p, 2 * cc_ + k, slice(P * tt, P * tt + P)), cc_ == 0 and k == 0, cc_ == 3 and k == 1,
                                  x_stationary=True)
                m.then_inc(units_multiplied, 1)

            def rotate4(part, l):
                n = ROPES[part, l]
                if n > 0:
                    pe.wait_ge(s("roped2"), n)
                wait_taken(pe, (part, l, 3))
                z = (diffz if part[0] == "d" else retz)
                a0 = 0 if part[1] == "k" else 4
                for j in range(4):
                    m = pe.matmul(ps[:, 4 * 512 + T * j:4 * 512 + T * j + T], c("rot64" if part[0] == "d" else "rot128"),
                                  z[:, a0 + j, 0:T], start=(j % 2 == 0), stop=True, skip_group_check=True)
                m.then_inc(s("rotated2"), 1)

            def diff(l, step):
                nd = len(DIFF[l])
                if step < nd:
                    n, (st, hh, qt) = DIFF_AT[l] + step, DIFF[l][step]
                    if step == 0:
                        pe.wait_ge(s("roped2"), ROPES["dq", l] + 1)
                    for m_ in range(2):
                        if n > 0:
                            pe.wait_ge(s("exps2"), 2 * (n - 1) + m_ + 1)
                        rows = slice(HD * m_, HD * m_ + HD)
                        keys = slice(T * st, 2 * T)
                        q0 = T * st + P * qt
                        pe.matmul(bank(4 + m_, T * st, 2 * T - T * st), diffz[rows, 4 + hh, q0:q0 + P], diffz[rows, hh, keys],
                                  start=True, stop=True).then_inc(s("scored2"), 1)
                if 1 <= step <= nd:
                    n, (st, hh, qt) = DIFF_AT[l] + step - 1, DIFF[l][step - 1]
                    pe.wait_ge(s("attn2"), n + 1)
                    if n >= 1:
                        pe.wait_ge(s("attnT2"), n)
                    for kt in range(2 * st, 4):
                        m = pe.transpose(bank(6, P * kt, P), aux[:, 4 + n % 2, P * kt:P * kt + P], c("ident"))
                    m.then_inc(s("turned2"), 1)
                if 2 <= step <= nd + 1:
                    n, (st, hh, qt) = DIFF_AT[l] + step - 2, DIFF[l][step - 2]
                    pe.wait_ge(s("attnT2"), n + 1)
                    if qt == 0 and n >= 2:
                        pe.wait_ge(s("diff_scaled"), n // 2)
                    for kt in range(2 * st, 4):
                        m = pe.matmul(bank(7, P * qt, P), diffv[:, kt, P * hh:P * hh + P], aux[:, 6 + n % 2, P * kt:P * kt + P],
                                      start=(kt == 2 * st), stop=(kt == 3), skip_group_check=True)
                    m.then_inc(s("weighed2"), 1)
                    if qt == 1:
                        pe.wait_ge(s("head_sq"), HEAD_AT[l] + (step - 2) // 2 + 1)
                        pe.matmul(bank(7, T, T), c("ones"), aux[:, 8, 0:T], start=True, stop=True, skip_group_check=True)\
                            .then_inc(s("head_ss"), 1)

            def states_of(l):
                for hh in range(4):
                    n = 4 * l + hh
                    for tt in range(2):
                        if hh == 0 and tt == 0:
                            pe.wait_ge(s("roped2"), ROPES["rq", l] + 1)
                            pe.wait_ge(s("diff_scaled"), HEAD_AT[l + 1])
                        if hh > 0:
                            pe.wait_ge(s("ktok_ready"), 8 * l + 2 * hh)
                        pe.transpose(bank(4, P * tt, P), retz[:, hh, T + P * tt:T + P * tt + P], c("ident")) \
                            .then_inc(s("k_turned"), 1)
                    pe.wait_ge(s("ktok_ready"), 8 * l + 2 * hh + 2)
                    if hh > 0:
                        pe.wait_ge(s("states_ready"), n)
                    for dr in range(2):
                        for tt in range(2):
                            m = pe.matmul(bank(5, P * dr, P), ktok[:, dr, tt, :], retv[:, 2 + tt, P * hh:P * hh + P],
                                          start=(dr == 0 and tt == 0), stop=(tt == 1), skip_group_check=True)
                    m.then_inc(s("states_done"), 1)

            def ret(l, step):
                nr = len(RET[l])
                if step == 0:
                    states_of(l)
                if step < nr:
                    n, (st, hh) = RET_AT[l] + step, RET[l][step]
                    if step == 0:
                        pe.wait_ge(s("states_ready"), 4 * l + 4)
                    if n >= 2:
                        pe.wait_ge(s("decayed"), n - 1)
                    if step >= 3:
                        pe.wait_ge(s("ret_rstd"), n - 2)
                    for kt in range(2):
                        m = pe.matmul(bank(4 + n % 2, T * kt, T), retz[:, hh, T * st + P * kt:T * st + P * kt + P],
                                      retz[:, 4 + hh, T * st:T * st + T], start=(kt == 0), stop=True, skip_group_check=True)
                    m.then_inc(s("ret_scored"), 1)
                if 1 <= step <= nr:
                    n, (st, hh) = RET_AT[l] + step - 1, RET[l][step - 1]
                    pe.wait_ge(s("decayed"), n + 1)
                    if n >= 2:
                        pe.wait_ge(s("ret_scaled"), n - 1)
                    if st == 0:
                        pe.wait_ge(s("q_decayed"), 2 * (4 * l + hh) + 2)
                    for kt in range(2):
                        m = pe.matmul(bank(6 + n % 2, 0, T), retv[:, 2 * st + kt, P * hh:P * hh + P], aux[:, n % 2, T * kt:T * kt + T],
                                      start=(kt == 0), stop=(st == 1 and kt == 1),
                                      skip_group_check=True)
                    if st == 0:
                        for dr in range(2):
                            m = pe.matmul(bank(6 + n % 2, 0, T), states[:, dr, hh, :], aux[:, 2 + n % 2, T * dr:T * dr + T],
                                          start=False, stop=(dr == 1), skip_group_check=True)
                    m.then_inc(s("ret_out"), 1)

                if 2 <= step <= nr + 1:
                    n = RET_AT[l] + step - 2
                    pe.wait_ge(s("ret_sq"), n + 1)
                    pe.matmul(bank(4 + (n + 1) % 2, 0, T), c("ones"), aux[:, 8, 0:T], start=True, stop=True)\
                        .then_inc(s("ret_ss"), 1)

            pe.wait_ge(block2_loaded, 32)
            for l in range(LAYERS):
                tok = 2 * T if l == 0 else T
                sumsq(5 + 2 * l, 2 * T)
                for j in range(4):
                    project2(("dk", l, j), l, 2 * T, first=(j == 0))
                for j in range(4):
                    project2(("dq", l, j), l, tok)
                    if j == 1:
                        rotate4("dk", l)
                for cc_ in range(4):
                    project_values("dv", l, cc_, 4)
                rotate4("dq", l)
                for j in range(4):
                    project2(("dg", l, j), l, tok)
                for slot, name in enumerate(slot_units(l)):
                    part = name[0]
                    if part in ("rv", "mv"):
                        project_values(part, l, name[2], 4 if part == "rv" or l == 0 else 2)
                    else:
                        project2(name, l, 2 * T if part == "rk" else tok)
                    for kind, step in SLOTS[l][slot]:
                        if kind == "diff":
                            diff(l, step)
                        elif kind == "rot":
                            rotate4(step, l)
                        elif kind == "ret":
                            ret(l, step)
                for g in range(4):
                    n = 4 * l + g
                    if g == 0:
                        wait_taken(pe, ("mv", l, tok // P - 1))
                        pe.wait_ge(s("ret_scaled"), RET_AT[l + 1])
                    if n >= 2:
                        pe.wait_ge(s("mixed"), n - 1)
                    for tt in range(tok // P):
                        pe.matmul(bank(4 + g % 2, P * tt, P), vn[:, tt, P * g:P * g + P], c("wsT", BW * l + P * g, BW * l + P * g + P),
                                  start=(tt == 0), stop=False, skip_group_check=True)
                        m = pe.matmul(bank(4 + g % 2, P * tt, P), c("ones")[0:1, :], bsrow[0:1, BW * l + P * g:BW * l + P * g + P],
                                      start=False, stop=True, skip_group_check=True)
                    m.then_inc(s("mix_done"), 1)
                for f in range(KT):
                    for b in range(3):
                        project2(("mlog", l, b, f), l, tok)
                    for b, o in enumerate((o_ret, o_mlp, o_dif)):
                        if b != 1:
                            wt = unit(("wbo", l, f, b // 2))
                        if f == 0 and b == 0:
                            pe.wait_ge(s("mixed"), 4 * l + 4)
                        bank_free(pe, ("wbo", l, b, f))
                        for k in range(4):
                            m = pe.matmul(bank(BANK["wbo", l, b, f][0], 0, tok), wt[:, BW * (b % 2) + P * k:BW * (b % 2) + P * k + P],
                                          o[:, k, 0:tok], start=(k == 0), stop=(k == 3))
                        if b != 0:
                            m.then_inc(units_multiplied, 1)
                for j in range(KT):
                    project2(("wo", l, j), l, tok, first=(j == 0))
                sumsq(6 + 2 * l, tok)

        @block.scalar
        def _(act):
            steps = [0]

            def link(ins):
                steps[0] += 1
                ins.then_inc(act_step, 1)
                act.wait_ge(act_step, steps[0])

            def squares(n, x, who, counts, tokens=T):
                for k in range(KT):
                    act.wait_ge(who, counts[k])
                    act.activation(sq[:, k, 0:T], x[:, k, :], ACT.Square).then_inc(squares_ready, 1)

            def root(n, src, tokens, sumsq_sem, count, width, done, col=0):
                act.wait_ge(sumsq_sem, count)
                link(act.activation(lnr[:, col:col + tokens], src, ACT.Ln, bias=eps[:, 0:1], scale=1.0 / width))
                act.activation(rstd[:, col:col + tokens], lnr[:, col:col + tokens], ACT.Exp, scale=-0.5).then_inc(done, 1)

            done = [0]

            def high_part(name, body=0):
                n, u = SPLIT[name], UNIT[name]
                act.wait_ge(unit_loaded[u % RING], 16 * (u // RING + 1) + 16 // RING * body)
                if n >= HI:
                    act.wait_ge(units_multiplied, UNIT[SPLIT_UNITS[n - HI]] + 1 + body)
                act.activation(w_parts(name)[0], ring[:, u % RING, :], ACT.Copy).then_inc(hi_ready, 1)
                done[0] = n + 1

            def high_parts(count):
                for n in range(done[0], min(done[0] + count, len(SPLIT_UNITS))):
                    high_part(SPLIT_UNITS[n])

            def prepare(name):
                upto = sum(1 for v in SPLIT_UNITS if UNIT[v] <= UNIT[name]) + 2
                while done[0] < min(upto, len(SPLIT_UNITS)) and UNIT[SPLIT_UNITS[done[0]]] <= UNIT[name] + 3:
                    high_parts(1)

            def ffn(tag, n):
                def gate(f, count):
                    act.wait_ge(units_multiplied, count)
                    act.activation(sil[:, f % 4, :], bank(4 + f % 4, 0, T), ACT.Silu).then_inc(silu_ready, 1)

                base = SPLIT[tag, "w1", 0]
                m0 = 26 * n
                part = lambda m, body=0: high_part(SPLIT_UNITS[base + m], body)
                part(3)
                gate(0, UNIT[tag, "w3", 0] + 1)
                if n == 1:
                    load_mod(act, m0 + 1)
                part(4)
                if n == 0:
                    act.wait_ge(s("angle_ready"), 1)
                    act.activation(s5v[:, 7:9, :], s5v[:, 5:7, :], ACT.Sin, scale=TWO_PI).then_inc(s("angle_sin"), 1)
                with act.Fori(0, (FT - 2) // 4) as it:
                    for f in range(1, 5):
                        part(3 * f + 2, 12 * it)
                        gate(f, UNIT[tag, "w3", f] + 1 + 12 * it)
                        part(3 * f + 3, 12 * it)
                        load_mod(act, m0 + f + 1, 4 * it)
                        part(3 * f + 4, 12 * it)
                part(FU - 1)
                gate(FT - 1, UNIT[tag, "w3", FT - 1] + 1)
                if n == 0:
                    load_mod(act, 22)

            def take(name, dst, func=ACT.Copy, tokens=T, unit=None, **kw):
                prepare(unit or name)
                product(act, *(unit or name))
                act.activation(dst, bank(BANK[name][0], 0, tokens), func, **kw).then_inc(act_evac, 1)

            def hn_high(n):
                for k in range(KT):
                    act.wait_ge(s("norm_full"), KT * n + k + 1)
                    act.activation(hn[0][:, k, 0:T], sq[:, k, 0:T], ACT.Copy).then_inc(s("hn_high"), 1)

            act.wait_ge(consts_loaded, 16 * NC_DMAS)
            act.wait_ge(s("eps_set"), 1)
            squares(0, h, consts_loaded, [16 * NC_DMAS] * KT)
            high_parts(1)
            root(0, bank(7, 0, T), T, sumsq_ready, 1, D, rstd_ready)
            hn_high(0)
            high_parts(2)
            act.wait_ge(s("cond_loaded"), 32)
            for st in range(2):
                act.activation(cond_silu(st), cond_silu(st), ACT.Silu).then_inc(cs_ready, 1)
            ffn("ffn1", 0)
            squares(1, h, resid_ready, [k // 2 + 1 for k in range(KT)])
            high_parts(1)
            root(1, bank(7, 0, T), T, sumsq_ready, 2, D, rstd_ready)
            hn_high(1)
            high_parts(1)
            for i in range(NST):
                act.wait_ge(s("turns_ready"), 2 * i + 2)
                act.activation(costab[:, i, :], costab[:, i, :], ACT.Sin, scale=TWO_PI)
                act.activation(sintab[:, i, :], sintab[:, i, :], ACT.Sin, scale=TWO_PI).then_inc(s("tables_ready"), 1)
                if i % 4 == 3:
                    take(("u", i // 4), uT[:, i // 4, :])
                    load_mod(act, 23 + i // 4)

            take(("kc",), zq[:, 6, :])
            take(("vc",), vcT)
            for j in range(4):
                take(("q", j), zq[:, j, :])
            take(("ks",), zq[:, 4, :])
            take(("kw",), zq[:, 5, :])
            act.wait_ge(s("blk_cleared"), 1)
            wait_taken(act, ("vc",))
            act.wait_ge(s("roped"), 1)
            for kv, src in enumerate((zq[:, 6, :], vcT)):
                bv = blk[:, kv, :].rearrange("p (l g c) -> p c g l", l=16, g=2)
                sv = src.rearrange("p (c l two) -> p c l two", l=8, two=2)
                for g in range(2):
                    for par in range(2):
                        for half in range(2):
                            m = act.activation(bv[HD * par:HD * par + HD, 0:NCMP, g, 8 * half:8 * half + 8],
                                               sv[HD * g:HD * g + HD, half:half + NCMP, :, par], ACT.Copy)
                m.then_inc(s("blk_filled"), 1)
            prepare(("vg", 2))
            product(act, "vg", 2)
            for tt in range(2):
                b = BANK["vg", tt][0]
                act.activation(gates[:, tt, :], bank(b, 256, 24), ACT.Sigmoid)
                act.activation(vtok[:, tt, :], bank(b, 0, 280), ACT.Copy).then_inc(act_evac, 1)
            for kv, tag in enumerate(("cmpk", "cmpv")):
                product(act, tag, 3)
                act.activation(gelu_rows[kv][0:32, :], ps[0:32, 512 * kv:512 * kv + 256], ACT.Gelu_apprx_tanh)\
                    .then_inc(s("cmp_hidden"), 1)
            for kv in range(2):
                act.wait_ge(s("cmp_turned"), kv + 1)
                act.activation(ghid[:, kv, :], bank(kv, 0, 64), ACT.Copy).then_inc(s("ghid_ready"), 1)
            act.wait_ge(s("kcmp"), 1)
            for g in range(2):
                act.activation(kbd[HD * g:HD * g + HD, 16 * g:16 * g + 16], ps[HD * g:HD * g + HD, 2 * 512:2 * 512 + 16],
                               ACT.Copy).then_inc(s("kbd_ready"), 1)
            act.wait_ge(s("cmp_shifted"), 1)
            act.activation(cex, csc, ACT.Exp, scale=HD ** -0.5).then_inc(s("cmp_exp"), 1)
            act.wait_ge(s("cmp_probsT"), 1)
            act.activation(pct, bank(1, 0, 2 * P), ACT.Copy).then_inc(s("pct_ready"), 1)

            def turn_copy(i):
                act.wait_ge(s("turned"), i + 1)
                if i >= 2:
                    act.wait_ge(s("weighed"), i - 1)
                act.activation(pt[:, i % 2, :], bank(2 + i % 2, 0, 384), ACT.Copy).then_inc(s("pt_ready"), 1)

            for i in range(NST + 2):
                if i < NST:
                    act.wait_ge(s("maxes"), i + 1)
                    act.activation(ex[:, i % 2, 0:P], bank(i % 2, 0, P), ACT.Exp, scale=HD ** -0.5,
                                   bias=stat[:, i % 2, 2:3], accum_out=stat[:, i % 2, 4:5]).then_inc(s("exps"), 1)
                    act.activation(ex[:, i % 2, P:3 * P], bank(i % 2, P, 2 * P), ACT.Exp, scale=HD ** -0.5,
                                   bias=stat[:, i % 2, 3:4], accum_out=stat[:, i % 2, 5:6]).then_inc(s("exps"), 1)
                if 1 <= i <= NST:
                    turn_copy(i - 1)
                if i < NST:
                    act.wait_ge(s("factors"), i + 1)
                    act.activation(prob[:, i % 2, 0:P], ex[:, i % 2, 0:P], ACT.Copy, scale=stat[:, i % 2, 8:9])\
                        .then_inc(s("probs"), 1)
                    act.activation(prob[:, i % 2, P:3 * P], ex[:, i % 2, P:3 * P], ACT.Copy, scale=stat[:, i % 2, 9:10])\
                        .then_inc(s("probs"), 1)
                if i >= 5 and (i - 5) % 4 == 0:
                    j = (i - 5) // 4
                    act.wait_ge(s("weighed"), 4 * j + 4)
                    act.activation(oT[:, j, :], ps[:, 5 * 512 + T * (j % 2):5 * 512 + T * (j % 2) + T], ACT.Copy)\
                        .then_inc(s("o_taken"), 1)
            for j in range(4):
                act.wait_ge(s("s5_y_taken"), j + 1)
                act.activation(yg[:, j, :], yg[:, j, :], ACT.Gelu_apprx_tanh).then_inc(s("gelu_ready"), 1)
            for j in range(4):
                take(("glu", j), sg[:, j, :], ACT.Sigmoid, unit=("glu", j // 2), bias=c("b_glu", j, j + 1))
            n_wout = BANK["wout", 0][3]
            squares(2, h, dve_evac, [n_wout + k for k in range(KT)])
            wait_taken(act, ("glu", 3))
            act.dma_start(pk[:, width(PACK):width(PACK + PACK2)], pack2).then_inc(block2_loaded, 16)
            act.dma_start(hc[:, :, :], ctx_in).then_inc(block2_loaded, 16)
            high_parts(1)
            root(2, bank(7, 0, T), T, sumsq_ready, 3, D, rstd_ready)
            hn_high(2)
            high_parts(2)
            ffn("ffn2", 1)
            squares(3, h, resid_ready, [4 + k // 2 + 1 for k in range(KT)])
            for j in range(4):
                take(("plew", j), pwp[:, 2 * j:2 * j + 2, :].rearrange("p a b -> p (a b)"), tokens=2 * T, unit=("plew", j // 2))
            root(3, bank(7, 0, T), T, sumsq_ready, 4, D, rstd_ready)
            hn_high(3)
            for j in range(KT):
                take(("pleg", j), plg[:, j, :], ACT.Sigmoid)
            squares(4, h, resid_ready, [8 + k + 1 for k in range(KT)])
            root(4, bank(7, 0, T), T, sumsq_ready, 5, D, rstd_ready)

            act.wait_ge(block2_loaded, 32)
            def diff(l, step):
                nd = len(DIFF[l])
                if step < nd:
                    n, (st, hh, qt) = DIFF_AT[l] + step, DIFF[l][step]
                    for m_ in range(2):
                        act.wait_ge(s("maxes2"), 2 * n + m_ + 1)
                        e = aux[:, 2 * (n % 2) + m_, T * st:2 * T]
                        act.activation(e, bank(4 + m_, T * st, 2 * T - T * st), ACT.Exp, scale=HD ** -0.5,
                                       bias=st2[:, n % 2, 2 + m_:3 + m_], accum_out=st2[:, n % 2, 4 + m_:5 + m_])\
                            .then_inc(s("exps2"), 1)
                if 1 <= step <= nd:
                    n, (st, hh, qt) = DIFF_AT[l] + step - 1, DIFF[l][step - 1]
                    act.wait_ge(s("turned2"), n + 1)
                    if n >= 2:
                        act.wait_ge(s("weighed2"), n - 1)
                    act.activation(aux[:, 6 + n % 2, T * st:2 * T], bank(6, T * st, 2 * T - T * st), ACT.Copy)\
                        .then_inc(s("attnT2"), 1)
                if 2 <= step <= nd + 1 and DIFF[l][step - 2][2] == 1:
                    n, k = DIFF_AT[l] + step - 2, HEAD_AT[l] + (step - 2) // 2
                    act.wait_ge(s("weighed2"), n + 1)
                    act.activation(aux[:, 8, 0:T], bank(7, 0, T), ACT.Square).then_inc(s("head_sq"), 1)
                    root(0, bank(7, T, T), T, s("head_ss"), k + 1, P, s("head_rstd"))

            def states_of(l):
                for hh in range(4):
                    for tt in range(2):
                        act.wait_ge(s("k_turned"), 8 * l + 2 * hh + 2)
                        if hh > 0:
                            act.wait_ge(s("states_done"), 4 * l + hh)
                        for dr in range(2):
                            m = act.activation(ktok[:, dr, tt, :], bank(4, P * tt, P), ACT.Copy,
                                               scale=lay[:, l, 8 * dr + 2 * hh + tt:8 * dr + 2 * hh + tt + 1])
                        m.then_inc(s("ktok_ready"), 1)

            def ret(l, step):
                nr = len(RET[l])
                if step == 0:
                    states_of(l)
                if step < nr and RET[l][step][0] == 0:
                    n, (st, hh) = RET_AT[l] + step, RET[l][step]
                    k = 4 * l + hh
                    if k >= 2:
                        act.wait_ge(s("q_decayed"), 2 * (k - 1))
                    for dr in range(2):
                        act.activation(aux[:, 4 + k % 2, T * dr:T * dr + T], c("steps"), ACT.Exp,
                                       scale=lay[:, l, 16 + 8 * dr + hh:17 + 8 * dr + hh],
                                       bias=lay[:, l, 16 + 12 * dr + hh:17 + 12 * dr + hh]).then_inc(s("state_decay"), 1)
                if 2 <= step <= nr + 1:
                    n = RET_AT[l] + step - 2
                    act.wait_ge(s("ret_out"), n + 1)
                    act.activation(aux[:, 8, 0:T], bank(6 + n % 2, 0, T), ACT.Square).then_inc(s("ret_sq"), 1)
                    if n >= 1:
                        act.wait_ge(s("ret_scaled"), n)
                    root(0, bank(4 + (n + 1) % 2, 0, T), T, s("ret_ss"), n + 1, P, s("ret_rstd"))

            def decay_tables(l, hh):
                n = 4 * l + hh
                if hh == 0 and l == 1:
                    act.wait_ge(s("decayed"), RET_AT[1])
                act.activation(dmat[:, hh, :], c("dist"), ACT.Exp, scale=lay[:, l, 16 + hh:17 + hh]).then_inc(s("decay_exp"), 1)
                if n > 0:
                    act.wait_ge(s("decay_masked"), 2 * n)
                act.activation(aux[:, 9, :], c("dist"), ACT.Exp, scale=lay[:, l, 24 + hh:25 + hh]).then_inc(s("decay_exp"), 1)

            for l in range(LAYERS):
                tok = 2 * T if l == 0 else T
                for k in range(KT):
                    if l == 1:
                        act.wait_ge(resid_ready, RESID_BLOCK2 + k + 1)
                        act.wait_ge(s("ctx_ready"), k + 1)
                    else:
                        act.wait_ge(resid_ready, RESID_BLOCK2 - KT + k + 1)
                    act.activation(sq2[:, k, 0:T], h[:, k, :], ACT.Square)
                    act.activation(sq2[:, k, T:2 * T], hc[:, k, :], ACT.Square).then_inc(squares_ready, 1)
                root(0, bank(7), 2 * T, sumsq_ready, 6 + 2 * l, D, rstd_ready)
                for k in range(KT):
                    for st in range(2):
                        act.wait_ge(scaled_ready, 16 * l + 2 * k + st + 1)
                        v = slice(T * st, T * st + T)
                        act.activation(hn[0][:, k, v], sq2[:, k, v], ACT.Identity, bias=mods[:, l, k, st:st + 1])\
                            .then_inc(s("hn_high2"), 1)
                    if k == 3:
                        prepare(("dk", l, 0))
                if l == 0:
                    link(act.activation(sp[:, 0, :], c("ret_logit"), ACT.Exp, scale=-1.0))
                    act.activation(sp[:, 1, :], sp[:, 0, :], ACT.Ln, bias=1.0).then_inc(s("lay_act"), 1)
                    act.wait_ge(s("lay_dve"), 1)
                    act.activation(sp[:, 3, 0:4], sp[:, 2, 0:4], ACT.Exp).then_inc(s("lay_act"), 1)
                    act.wait_ge(s("lay_dve"), 2)
                    act.activation(lay[:, :, 0:16], lay[:, :, 0:16], ACT.Exp).then_inc(s("lay_act"), 1)
                for part in ("dk", "dq"):
                    for j in range(4):
                        t_ = 2 * T if part == "dk" else tok
                        take((part, l, j), diffz[:, (0 if part == "dk" else 4) + j, 0:t_], tokens=t_)
                for tt in range(4):
                    take(("dv", l, tt), diffv[:, tt, :], tokens=BW, unit=("dv", l, 3))
                for j in range(4):
                    take(("dg", l, j), diffz[:, 8 + j, 0:tok], ACT.Silu, tokens=tok)
                if l == 0:
                    act.wait_ge(s("lay_dve"), 3)
                for slot, name in enumerate(slot_units(l)):
                    prepare(name)
                    part, j = name[0], name[2]
                    if part == "rk":
                        take(name, retz[:, j, 0:2 * T], tokens=2 * T)
                    if part == "rq":
                        take(name, retz[:, 4 + j, 0:tok], tokens=tok)
                    if part == "rv" and j == 3:
                        for tt in range(4):
                            take(("rv", l, tt), retv[:, tt, :], tokens=BW, unit=name)
                    if part == "rg":
                        take(name, retz[:, 8 + j, 0:tok], ACT.Silu, tokens=tok)
                    if part == "mu" and j == 0:
                        act.wait_ge(s("diff_scaled"), HEAD_AT[l + 1])
                    if part == "mu":
                        take(name, mlpu[:, j, 0:tok], tokens=tok)
                    if part == "mg":
                        take(name, mlpu[:, 4 + j, 0:tok], ACT.Silu, tokens=tok)
                    for kind, step in SLOTS[l][slot]:
                        if kind == "diff":
                            diff(l, step)
                        if kind == "tables":
                            decay_tables(l, step)
                        if kind == "ret":
                            ret(l, step)
                    if part == "mv" and j == 3:
                        for tt in range(tok // P):
                            n = VN_AT[l] + tt
                            act.wait_ge(s("var_ready"), n + 1)
                            link(act.activation(st2[:, n % 2, 10:11], st2[:, n % 2, 9:10], ACT.Ln, bias=eps[:, 0:1]))
                            act.activation(st2[:, n % 2, 11:12], st2[:, n % 2, 10:11], ACT.Exp, scale=-0.5)\
                                .then_inc(s("ln_rstd"), 1)
                for f in range(KT):
                    for b in range(3):
                        n = 8 * l + f
                        if n >= 2:
                            act.wait_ge(s("merged"), n - 1)
                        if f == 0:
                            act.wait_ge(s("ret_scaled"), RET_AT[l + 1])
                        take(("mlog", l, b, f), aux[:, 3 * (f % 2) + b, 0:tok], ACT.Sigmoid, tokens=tok)
                for k in range(KT):
                    if k == KT - 1:
                        prepare(("wo", l, 0))
                    act.wait_ge(s("merged"), KT * l + k + 1)
                    act.activation(hn[0][:, k, 0:tok], ymrg[:, k, 0:tok], ACT.Copy).then_inc(s("y_high"), 1)
                for j in range(KT):
                    take(("wo", l, j), unnormed[:, j, 0:tok], tokens=tok)
                for k in range(KT):
                    wait_taken(act, ("wo", l, k))
                    act.activation(sq2[:, k, 0:tok], unnormed[:, k, 0:tok], ACT.Square).then_inc(squares_ready, 1)
                root(0, bank(7, 0, tok), tok, sumsq_ready, 7 + 2 * l, D, rstd_ready)

        @block.vector
        def _(dve):
            steps = [0]

            def link(ins):
                steps[0] += 1
                ins.then_inc(dve_step, 1)
                dve.wait_ge(dve_step, steps[0])

            tt_, ts, stt = dve.tensor_tensor, dve.tensor_scalar, dve.scalar_tensor_tensor

            def norm(n, gain):
                dve.wait_ge(rstd_ready, n + 1)
                for k in range(KT + 2):
                    if k < KT:
                        stt(sq[:, k, 0:T], h[:, k, :], c(gain, k, k + 1), rstd[:, 0:T], ALU.mult, ALU.mult)\
                            .then_inc(s("norm_full"), 1)
                    if k >= 2:
                        dve.wait_ge(s("hn_high"), KT * n + k - 1)
                        tt_(hn[1][:, k - 2, 0:T], sq[:, k - 2, 0:T], hn[0][:, k - 2, 0:T].bitcast(F32), ALU.subtract)\
                            .then_inc(normed_ready, 1)

            def modulation(m, body=0):
                dve.wait_ge(s(f"mod_loaded{m % 2}"), 16 * (m // 2 + 1) + 8 * body)
                if m == 0:
                    dve.wait_ge(cs_ready, 2)
                else:
                    dve.wait_ge(s("mod_used"), m + body)
                out_at = lambda st: mods[:, :, :, :].rearrange("p l f s -> p (l f s)")[:, bass.ds(2 * (m + body) + st, 1)]
                stt(quarter(lnr[:, :].bitcast(BF16)), mod_slot(m), 1.0, cond_silu(0), ALU.mult, ALU.mult,
                    accum_out=out_at(0)).then_inc(s("mod_half"), 1)
                dve.wait_ge(s("mod_half"), m + 1 + body)
                stt(mod_slot(m), mod_slot(m), 1.0, cond_silu(1), ALU.mult, ALU.mult, accum_out=out_at(1)).then_inc(s("mod_used"), 1)

            def low_parts(tag, *which):
                for m in which:
                    low_part(dve, SPLIT_UNITS[SPLIT[tag, "w1", 0] + m])

            def final_norm():
                dve.wait_ge(rstd_ready, 5)
                for k in range(KT):
                    stt(h[:, k, :], h[:, k, :], c("g_final", k, k + 1), rstd[:, 0:T], ALU.mult, ALU.mult).then_inc(resid_ready, 1)

            def ffn(tag, n):
                def gated(f, count):
                    v, hi, lo = sil[:, f % 4, :], hid[0][:, f % 4, :], hid[1][:, f % 4, :]
                    dve.wait_ge(silu_ready, count)
                    tt_(v, v, bank(4 + f % 4, T, T), ALU.mult).then_inc(s("gated"), 1)
                    dve.wait_ge(s("gated"), count)
                    dve.tensor_copy(hi, v).then_inc(s("hid_high"), 1)
                    dve.wait_ge(s("hid_high"), count)
                    tt_(lo, v, hi.bitcast(F32), ALU.subtract).then_inc(hidden_ready, 1)

                base = SPLIT[tag, "w1", 0]
                m0 = 26 * n
                part = lambda m, body=0: low_part(dve, SPLIT_UNITS[base + m], body)
                part(2)
                part(3)
                gated(0, FT * n + 1)
                part(4)
                if n == 0:
                    dve.wait_ge(s("norm2_ready"), 1)
                    dve.reciprocal(s5v[:, DEN, :], s5v[:, DEN, :]).then_inc(s("norm2_inverted"), 1)
                modulation(m0)
                with dve.Fori(0, (FT - 2) // 4) as it:
                    for f in range(1, 5):
                        part(3 * f + 2, 12 * it)
                        gated(f, FT * n + f + 1 + 4 * it)
                        part(3 * f + 3, 12 * it)
                        modulation(m0 + f, 4 * it)
                        part(3 * f + 4, 12 * it)
                part(FU - 1)
                gated(FT - 1, FT * n + FT)
                modulation(m0 + FT - 1)
                product(dve, tag, "w2", FT - 1)
                for m in range(4):
                    hh = h[:, 2 * m:2 * m + 2, :].rearrange("p a b -> p (a b)")
                    stt(hh, bank(m), 0.5, hh, ALU.mult, ALU.add).then_inc(resid_ready, 1)

            dve.memset(eps[:, :], EPS).then_inc(s("eps_set"), 1)
            dve.wait_ge(consts_loaded, 16 * NC_DMAS)
            low_parts("ffn1", 0)
            norm(0, "g_ffn1")
            low_parts("ffn1", 1)
            ffn("ffn1", 0)
            dve.tensor_copy(negc[:, :], c("causal")).then_inc(masks_ready, 1)
            dve.tensor_copy(idb[:, :], c("ident")).then_inc(masks_ready, 1)
            dve.wait_ge(s("s5_bt"), 1)
            dve.tensor_copy(bT.rearrange("p a b c -> p (a b c)"), ps[:, 4 * 512:6 * 512]).then_inc(s("s5_b_copied"), 1)
            norm(1, "g_mix")
            for m in range(22, 26):
                modulation(m)

            t1024 = sq[:, 0:2, :].rearrange("p a b -> p (a b)")
            for n, (a, b) in enumerate(((6, 7), (4, 6), (0, 4))):
                w = b - a
                z = zq[:, a:b, :]
                tmp = t1024[:, 0:T * w].rearrange("p (a b) -> p a b", b=T)
                rot = ps[:, 4 * 512 + T * a:4 * 512 + T * b].rearrange("p (a b) -> p a b", b=T)
                tab = lambda name: c(name).unsqueeze(1).broadcast_to([P, w, T])
                dve.wait_ge(s("rotated"), 1 if n == 0 else 2)
                if n > 0:
                    dve.wait_ge(s("roped"), n)
                tt_(tmp, rot, tab("sin1"), ALU.mult)
                link(tt_(z, z, tab("cos1"), ALU.mult))
                tt_(z, z, tmp, ALU.add).then_inc(s("roped"), 1)
                if n == 0:
                    for kv in range(2):
                        dve.wait_ge(s("blk_filled"), kv + 1)
                        bv = blk[:, kv, :].rearrange("p (l c) -> p l c", l=16)
                        tt_(bv, bv, c("pe", 16 * kv, 16 * kv + 16).unsqueeze(2).broadcast_to([P, 16, 32]), ALU.add)\
                            .then_inc(s("blk_ready"), 1)
            dve.wait_ge(s("ghid_ready"), 2)
            dve.tensor_copy(grep.rearrange("p h (j c) -> p h j c", j=4),
                            ghid[:, 1, :].rearrange("p (h c) -> p h c", h=2).unsqueeze(2).broadcast_to([P, 2, 4, 32]))\
                .then_inc(s("grep_ready"), 1)
            dve.wait_ge(s("vcmp"), 1)
            for g in range(2):
                ts(vbd[:, HD * g:HD * g + HD], bank(3, 0, HD), c("gmask", g, g + 1), None, ALU.mult).then_inc(s("vbd_ready"), 1)
            dve.wait_ge(s("cmp_scores"), 1)
            heads = lambda v: v.rearrange("p (q h c) -> p q h c", q=2, c=16)
            flat = lambda v: v.rearrange("p (h c) -> p h c", c=16)
            mask = lambda name: c(name).rearrange("p (q c) -> p q c", q=2).unsqueeze(2).broadcast_to([P, 2, 8, 16])
            each = lambda n: cst[:, n, :].unsqueeze(2).broadcast_to([P, 16, 16])
            link(tt_(heads(csc), heads(bank(0, 0, 2 * P)), mask("cneg"), ALU.add))
            link(dve.tensor_reduce(cst[:, 0, :], flat(csc), AX_X, ALU.max))
            tt_(flat(csc), flat(csc), each(0), ALU.subtract).then_inc(s("cmp_shifted"), 1)
            dve.wait_ge(s("cmp_exp"), 1)
            link(tt_(heads(cex), heads(cex), mask("cmask"), ALU.mult))
            link(dve.tensor_reduce(cst[:, 1, :], flat(cex), AX_X, ALU.add))
            link(ts(cst[:, 1, :], cst[:, 1, :], 1e-30, None, ALU.max))
            link(dve.reciprocal(cst[:, 2, :], cst[:, 1, :]))
            wait_taken(dve, ("vg", 1))
            link(tt_(cst[:, 2, :].rearrange("p (q h) -> p q h", q=2), cst[:, 2, :].rearrange("p (q h) -> p q h", q=2),
                     gates[:, :, 0:8], ALU.mult))
            tt_(flat(cex), flat(cex), each(2), ALU.mult).then_inc(s("cmp_probs"), 1)

            for i in range(NST + 1):
                if i < NST:
                    st = stat[:, i % 2, :]
                    dve.wait_ge(s("scored"), i + 1)
                    dve.tensor_reduce(st[:, 0:1], bank(i % 2, 0, P), AX_X, ALU.max)
                    link(dve.tensor_reduce(st[:, 1:2], bank(i % 2, P, 2 * P), AX_X, ALU.max))
                    ts(st[:, 2:4], st[:, 0:2], -HD ** -0.5, None, ALU.mult).then_inc(s("maxes"), 1)
                    dve.wait_ge(s("s5_bu"), i + 1)
                    dve.wait_ge(s("tables_ready"), i + 1)
                    two = lambda v: v.rearrange("p (a b) -> p a b", a=2)
                    tab = lambda v: v[:, i, :].unsqueeze(1).broadcast_to([P, 2, T])
                    ra, rb, zi, ws = rotA[:, i % 2, :], rotB[:, i % 2, :], zin[:, i % 2, :], wst[:, i % 2, :]
                    tt_(two(ra), two(bank(6)), tab(costab), ALU.mult)
                    tt_(two(rb), two(bank(6)), tab(sintab), ALU.mult).then_inc(s("s5_prod"), 1)
                    dve.wait_ge(s("s5_prod"), i + 1)
                    tt_(zi[:, 0:T], ra[:, 0:T], rb[:, T:2 * T], ALU.add)
                    link(tt_(zi[:, T:2 * T], ra[:, T:2 * T], rb[:, 0:T], ALU.subtract))
                    if i >= 2:
                        dve.wait_ge(s("s5_back"), 2 * (i - 1))
                    for part in range(2):
                        v = slice(T * part, T * part + T)
                        dve.tensor_tensor_scan(ws[:, v], s5v[:, R, i:i + 1].broadcast_to([P, T]), zi[:, v], 0.0,
                                               ALU.mult, ALU.add).then_inc(s("s5_scanned"), 1)
                    dve.wait_ge(s("exps"), 2 * i + 2)
                    link(dve.reciprocal(st[:, 6:8], st[:, 4:6]))
                    gc = 8 * (1 + i % 2) + 2 * (i // 4) + i // 2 % 2
                    tt_(st[:, 8:10], st[:, 6:8], gates[:, :, gc:gc + 1].rearrange("p a b -> p (a b)"), ALU.mult)\
                        .then_inc(s("factors"), 1)
                if i >= 4 and i % 4 == 0:
                    j = i // 4 - 1
                    dve.wait_ge(s("s5_y"), i)
                    stt(yg[:, j, :], uT[:, j, :], c("s5_d", j, j + 1), bank(7, T * (j % 2), T), ALU.mult, ALU.add)\
                        .then_inc(s("s5_y_taken"), 1)
            for j in range(4):
                wait_taken(dve, ("glu", j))
                tt_(oT[:, 4 + j, :], yg[:, j, :], sg[:, j, :], ALU.mult).then_inc(s("s5_out"), 1)
            for j in range(KT):
                product(dve, "wout", j)
                tt_(h[:, j, :], h[:, j, :], bank(BANK["wout", j][0], 0, T), ALU.add).then_inc(dve_evac, 1)
            low_parts("ffn2", 0)
            norm(2, "g_ffn2")
            low_parts("ffn2", 1)
            ffn("ffn2", 1)
            norm(3, "g_ple")
            dve.wait_ge(s("mod_used"), MODS)
            mv = mods[:, :, :, :].rearrange("p l f s -> p (l f) s")
            tt_(mv, mv, c("b_mod").unsqueeze(2).broadcast_to([P, 48, 2]), ALU.add).then_inc(mods_ready, 1)
            dve.wait_ge(mods_ready, 1)
            for l in range(LAYERS):
                gp = lambda name: c(name, KT * l, KT * l + KT).unsqueeze(2).broadcast_to([P, KT, 2])
                stt(amp[:, l, :, :], mods[:, l, KT:2 * KT, :], 1.0, gp("g_pre"), ALU.add, ALU.mult).then_inc(mods_ready, 1)
                tt_(pgate[:, l, :, :], mods[:, l, 2 * KT:3 * KT, :], gp("g_post"), ALU.mult).then_inc(mods_ready, 1)
            for j in range(KT):
                wait_taken(dve, ("pleg", j))
                link(tt_(plg[:, j, :], plg[:, j, :], pwp[:, j, :], ALU.mult))
                tt_(h[:, j, :], h[:, j, :], plg[:, j, :], ALU.add).then_inc(resid_ready, 1)
            final_norm()

            dve.wait_ge(block2_loaded, 32)
            def rope(part, l):
                n = ROPES[part, l]
                z = (diffz if part[0] == "d" else retz)[:, (0 if part[1] == "k" else 4):(4 if part[1] == "k" else 8), 0:T]
                tmp_c = aux[:, 0:2, :].rearrange("p a b -> p (a b)").rearrange("p (a b) -> p a b", b=T)
                tmp_s = aux[:, 2:4, :].rearrange("p a b -> p (a b)").rearrange("p (a b) -> p a b", b=T)
                rot = ps[:, 4 * 512:6 * 512].rearrange("p (a b) -> p a b", b=T)
                dve.wait_ge(s("rotated2"), n + 1)
                link(tt_(tmp_s, rot, c("sin" + part[0]).unsqueeze(1).broadcast_to([P, 4, T]), ALU.mult))
                dve.wait_ge(s("cos2"), n + 1)
                tt_(z, tmp_c, tmp_s, ALU.add).then_inc(s("roped2"), 1)

            def diff(l, step):
                nd = len(DIFF[l])
                if step < nd:
                    n, (st, hh, qt) = DIFF_AT[l] + step, DIFF[l][step]
                    v = st2[:, n % 2, :]
                    for m_ in range(2):
                        dve.wait_ge(s("scored2"), 2 * n + m_ + 1)
                        link(dve.tensor_reduce(v[:, m_:m_ + 1], bank(4 + m_, T * st, 2 * T - T * st), AX_X, ALU.max))
                        ts(v[:, 2 + m_:3 + m_], v[:, m_:m_ + 1], -HD ** -0.5, None, ALU.mult).then_inc(s("maxes2"), 1)
                    dve.wait_ge(s("exps2"), 2 * n + 2)
                    link(dve.reciprocal(v[:, 6:8], v[:, 4:6]))
                    link(tt_(v[:, 7:8], v[:, 7:8], lay[:, l, 39:40], ALU.mult))
                    e0, e1 = (aux[:, 2 * (n % 2) + m_, T * st:2 * T] for m_ in range(2))
                    link(ts(e0, e0, v[:, 6:7], None, ALU.mult))
                    if n >= 2:
                        dve.wait_ge(s("turned2"), n - 1)
                    stt(aux[:, 4 + n % 2, T * st:2 * T], e1, v[:, 7:8], e0, ALU.mult, ALU.add).then_inc(s("attn2"), 1)
                if 2 <= step <= nd + 1 and DIFF[l][step - 2][2] == 1:
                    st, hh, _ = DIFF[l][step - 2]
                    dve.wait_ge(s("head_rstd"), HEAD_AT[l] + (step - 2) // 2 + 1)
                    stt(aux[:, 8, T:2 * T], bank(7, 0, T), 1.0 - LAM_INIT[l], rstd[:, 0:T], ALU.mult, ALU.mult)\
                        .then_inc(s("diff_scaled"), 1)
                    dve.wait_ge(s("diff_scaled"), HEAD_AT[l] + (step - 2) // 2 + 1)
                    o = o_dif[:, hh, T * st:T * st + T]
                    if hh == 0 and st == 0:
                        wait_taken(dve, ("dg", l, 3))
                    link(tt_(o, aux[:, 8, T:2 * T], o, ALU.mult))

            def states_of(l):
                for hh in range(4):
                    dve.wait_ge(s("states_done"), 4 * l + hh + 1)
                    dve.tensor_copy(states[:, :, hh, :], bank(5, 0, 2 * P).rearrange("p (d n) -> p d n", d=2))\
                        .then_inc(s("states_ready"), 1)

            def ret(l, step):
                nr = len(RET[l])
                if step == 0:
                    states_of(l)
                    dve.wait_ge(s("decay_masked"), 8 * l + 8)
                if step < nr:
                    n, (st, hh) = RET_AT[l] + step, RET[l][step]
                    dve.wait_ge(s("ret_scored"), n + 1)
                    if n >= 2:
                        dve.wait_ge(s("ret_out"), n - 1)
                    stt(aux[:, n % 2, :], bank(4 + n % 2), float(P) ** -0.5, dmat[:, hh, :], ALU.mult, ALU.mult)\
                        .then_inc(s("decayed"), 1)
                if 2 <= step <= nr + 1:
                    n, (st, hh) = RET_AT[l] + step - 2, RET[l][step - 2]
                    dve.wait_ge(s("ret_rstd"), n + 1)
                    tt_(aux[:, 8, T:2 * T], bank(6 + n % 2, 0, T), rstd[:, 0:T], ALU.mult).then_inc(s("ret_scaled"), 1)
                    dve.wait_ge(s("ret_scaled"), n + 1)
                    o = o_ret[:, hh, T * st:T * st + T]
                    if n == RET_AT[l]:
                        wait_taken(dve, ("rg", l, 3))
                    link(tt_(o, aux[:, 8, T:2 * T], o, ALU.mult))

            for l in range(LAYERS):
                tok = 2 * T if l == 0 else T
                if l == 0:
                    dve.wait_ge(mods_ready, 1 + 2 * LAYERS)
                dve.wait_ge(rstd_ready, 6 + 2 * l)
                for k in range(KT + 1):
                    for st, x in enumerate((h, hc)):
                        v = slice(T * st, T * st + T)
                        if k < KT:
                            stt(sq2[:, k, v], x[:, k, :], amp[:, l, k, st:st + 1], rstd[:, v], ALU.mult, ALU.mult)\
                                .then_inc(scaled_ready, 1)
                        if k >= 1:
                            dve.wait_ge(s("hn_high2"), 16 * l + 2 * k + st - 1)
                            stt(hn[1][:, k - 1, v], sq2[:, k - 1, v], mods[:, l, k - 1, st:st + 1],
                                hn[0][:, k - 1, v].bitcast(F32), ALU.add, ALU.subtract).then_inc(s("modulated"), 1)
                if l == 0:
                    dve.wait_ge(s("modulated"), 2 * KT)
                    link(tt_(aux[:, 0, 0:256], c("lamq"), c("lamk"), ALU.mult))
                    dve.tensor_reduce(sp[:, 2, 0:4], aux[:, 0, 0:256].rearrange("p (a b) -> p a b", b=HD), AX_X, ALU.add)\
                        .then_inc(s("lay_dve"), 1)
                    dve.wait_ge(s("lay_act"), 1)
                    both = sp[:, 1, :].rearrange("p (ly n) -> p ly n", ly=2)
                    link(ts(lay[:, :, 16:24], both, -1.0, None, ALU.mult))
                    ts(lay[:, :, 28:32], lay[:, :, 20:24], float(T), None, ALU.mult)
                    ts(lay[:, :, 24:28], both[:, :, 4:8], 1.0, None, ALU.mult)
                    for ly in range(LAYERS):
                        m = tt_(lay[:, ly, 0:16].rearrange("p (d h t) -> p d h t", d=2, h=4),
                                lay[:, ly, 16:24].rearrange("p (d h) -> p d h", d=2).unsqueeze(3).broadcast_to([P, 2, 4, 2]),
                                c("jrow").rearrange("p (d t) -> p d t", d=2).unsqueeze(2).broadcast_to([P, 2, 4, 2]), ALU.mult)
                    m.then_inc(s("lay_dve"), 1)
                    dve.wait_ge(s("lay_act"), 3)
                    for ly in range(LAYERS):
                        stt(lay[:, ly, 39:40], sp[:, 3, 2 * ly + 1:2 * ly + 2], -LAM_INIT[ly], sp[:, 3, 2 * ly:2 * ly + 1],
                            ALU.add, ALU.subtract)
                    ts(lay[:, :, 0:16], lay[:, :, 0:16], float(P) ** -0.5, None, ALU.mult).then_inc(s("lay_dve"), 1)
                rope("dk", l)
                rope("dq", l)
                for slot, name in enumerate(slot_units(l)):
                    for kind, step in SLOTS[l][slot]:
                        if kind == "diff":
                            diff(l, step)
                        if kind == "rot":
                            rope(step, l)
                        if kind == "ret":
                            ret(l, step)
                    if name[0] == "mv" and name[2] == 3:
                        for tt in range(tok // P):
                            n = VN_AT[l] + tt
                            product(dve, *name)
                            b = BANK["mv", l, tt][0]
                            link(dve.bn_stats(out=st2[:, n % 2, 0:6], in_=bank(b)))
                            dve.bn_aggr(out=st2[:, n % 2, 8:10], in_=st2[:, n % 2, 0:6]).then_inc(s("var_ready"), 1)
                            dve.wait_ge(s("ln_rstd"), n + 1)
                            ts(vn[:, tt, :], bank(b), st2[:, n % 2, 8:9], st2[:, n % 2, 11:12], ALU.subtract, ALU.mult)\
                                .then_inc(dve_evac, 1)
                for g in range(4):
                    n = 4 * l + g
                    dve.wait_ge(s("mix_done"), n + 1)
                    wait_taken(dve, ("mg", l, g))
                    tt_(mlpu[:, g, 0:tok], mlpu[:, g, 0:tok], bank(4 + g % 2, 0, tok), ALU.mult).then_inc(s("mixed_raw"), 1)
                    dve.wait_ge(s("mixed_raw"), n + 1)
                    tt_(mlpu[:, g, 0:tok], mlpu[:, g, 0:tok], mlpu[:, 4 + g, 0:tok], ALU.mult).then_inc(s("mixed"), 1)
                def y_low(k):
                    dve.wait_ge(s("y_high"), KT * l + k + 1)
                    tt_(hn[1][:, k, 0:tok], ymrg[:, k, 0:tok], hn[0][:, k, 0:tok].bitcast(F32), ALU.subtract).then_inc(s("y_low"), 1)

                for f in range(KT):
                    if f == KT - 1:
                        for k in range(KT - 1):
                            y_low(k)
                    y = ymrg[:, f, 0:tok]
                    for b in range(3):
                        product(dve, "wbo", l, f, 1 if b == 2 else 0)
                        wait_taken(dve, ("mlog", l, b, f))
                        t = y if b == 0 else aux[:, 5 + b, 0:tok]
                        tt_(t, bank(BANK["wbo", l, b, f][0], 0, tok), aux[:, 3 * (f % 2) + b, 0:tok], ALU.mult)\
                            .then_inc(dve_evac, 1)
                        if b > 0:
                            wait_taken(dve, ("wbo", l, b, f))
                            if b == 1:
                                link(tt_(y, y, t, ALU.add))
                            else:
                                tt_(y, y, t, ALU.add).then_inc(s("merged"), 1)
                y_low(KT - 1)
                dve.wait_ge(rstd_ready, 7 + 2 * l)
                for k in range(KT):
                    for st in range(tok // T):
                        v = unnormed[:, k, T * st:T * st + T]
                        m = stt(v, v, pgate[:, l, k, st:st + 1], rstd[:, T * st:T * st + T], ALU.mult, ALU.mult)
                    link(m)
                    for st in range(tok // T):
                        x = (h, hc)[st]
                        tt_(x[:, k, :], x[:, k, :], unnormed[:, k, T * st:T * st + T], ALU.add)\
                            .then_inc(resid_ready if st == 0 else s("ctx_ready"), 1)

        @block.gpsimd
        def _(pool):
            steps = [0]

            def link(ins):
                steps[0] += 1
                ins.then_inc(pool_step, 1)
                pool.wait_ge(pool_step, steps[0])

            made = [0]

            def low_until(name, past=0):
                for v in SPLIT_UNITS:
                    who, count = LOW[v]
                    if who == "pool" and count > made[0] and UNIT[v] <= UNIT[name] + past:
                        low_part(pool, v)
                        made[0] = count

            tt_, ts = pool.tensor_tensor, pool.tensor_scalar

            def stt(dst, x, scalar, y, op0, op1):
                link(ts(s5v[:, 21, :], x, scalar, None, op0))
                return tt_(dst, s5v[:, 21, :], y, op1)

            col = lambda n: s5v[:, n, :]

            def exact_exp(dst, src):
                x, n, f, q, e = (col(k) for k in (16, 17, 18, 19, 20))
                link(ts(x, src, -87.0, 88.0, ALU.max, ALU.min))
                link(ts(n, x, LOG2E, MAGIC, ALU.mult, ALU.add))
                link(ts(n, n, MAGIC, None, ALU.subtract))
                link(stt(f, n, -LN2_HI, x, ALU.mult, ALU.add))
                link(stt(f, n, -LN2_LO, f, ALU.mult, ALU.add))
                link(ts(q, f, TAYLOR[0], None, ALU.mult))
                for k in TAYLOR[1:]:
                    link(stt(q, q, k, f, ALU.add, ALU.mult))
                link(ts(e.bitcast(I32), n, 127.0, float(1 << 23), ALU.add, ALU.mult))
                link(stt(dst, q, 1.0, e, ALU.add, ALU.mult))

            pool.wait_ge(block1_loaded, 32)
            link(tt_(col(DEN), c("a_re"), c("a_re"), ALU.mult))
            link(tt_(col(TMP), c("a_im"), c("a_im"), ALU.mult))
            tt_(col(DEN), col(DEN), col(TMP), ALU.add).then_inc(s("norm2_ready"), 1)
            exact_exp(col(DT), c("log_dt"))
            link(tt_(col(LRE), c("a_re"), col(DT), ALU.mult))
            link(tt_(col(LIM), c("a_im"), col(DT), ALU.mult))
            link(ts(col(K), col(LIM), INV2PI, MAGIC, ALU.mult, ALU.add))
            link(ts(col(K), col(K), MAGIC, None, ALU.subtract))
            link(stt(col(GS), col(K), -PI2_HI, col(LIM), ALU.mult, ALU.add))
            link(stt(col(GS), col(K), -PI2_LO, col(GS), ALU.mult, ALU.add))
            link(ts(col(GS), col(GS), INV2PI, None, ALU.mult))
            link(ts(col(GS), col(GS), 0.5, -0.5, ALU.min, ALU.max))
            link(ts(col(GC), col(GS), 0.25, None, ALU.add))
            link(ts(col(K), col(GC), MAGIC, MAGIC, ALU.add, ALU.subtract))
            tt_(col(GC), col(GC), col(K), ALU.subtract).then_inc(s("angle_ready"), 1)
            exact_exp(col(R), col(LRE))
            pool.wait_ge(s("angle_sin"), 1)
            link(tt_(col(PR), col(R), col(COS), ALU.mult))
            link(ts(col(PR), col(PR), 1.0, None, ALU.subtract))
            link(tt_(col(QI), col(R), col(SIN), ALU.mult))
            pool.wait_ge(s("norm2_inverted"), 1)
            for dst, x, y, op in ((CR, PR, QI, ALU.add), (CI, QI, PR, ALU.subtract)):
                link(tt_(col(dst), col(x), c("a_re"), ALU.mult))
                link(tt_(col(TMP), col(y), c("a_im"), ALU.mult))
                link(tt_(col(dst), col(dst), col(TMP), op))
                link(tt_(col(dst), col(dst), col(DEN), ALU.mult))
            wide = lambda v: v.rearrange("p (a b) -> p a b", b=32)
            over = lambda n: col(n).unsqueeze(2).broadcast_to([P, NST, 32])
            t512 = uT[:, 2:4, :].rearrange("p a b -> p (a b)")
            for dst, x, y, op in ((bre, "b_re", "b_im", ALU.subtract), (bim, "b_im", "b_re", ALU.add)):
                link(tt_(wide(dst), wide(c(x)), over(CR), ALU.mult))
                link(tt_(wide(t512), wide(c(y)), over(CI), ALU.mult))
                tt_(dst, dst, t512, op).then_inc(s("s5_b_ready"), 1)
                pool.wait_ge(s("s5_b_ready"), 1 if dst is bre else 2)
            link(ts(cneg_re, c("c_re"), -1.0, None, ALU.mult))
            link(ts(cneg_im, c("c_im"), -1.0, None, ALU.mult))

            pool.wait_ge(s("angle_ready"), 1)
            for i in range(NST):
                for n, tab in enumerate((costab, sintab)):
                    v, k = tab[:, i, :], uT[:, n, :]
                    link(pool.tensor_scalar(v, c("steps"), s5v[:, 6, i:i + 1], 0.25 if n == 0 else 0.0, ALU.mult, ALU.add))
                    link(pool.tensor_scalar(k, v, MAGIC, MAGIC, ALU.add, ALU.subtract))
                    pool.tensor_tensor(v, v, k, ALU.subtract).then_inc(s("turns_ready"), 1)
            link(pool.memset(blk, 0.0))
            pool.memset(kbd, 0.0).then_inc(s("blk_cleared"), 1)
            low_until(("vg", 2))
            for i in range(NST):
                pool.wait_ge(s("s5_scanned"), 2 * i + 2)
                if i >= 2:
                    pool.wait_ge(s("s5_y"), i - 1)
                two = lambda v: v.rearrange("p (a b) -> p a b", a=2)
                for dst, tab in ((bakA, costab), (bakB, sintab)):
                    pool.tensor_tensor(two(dst[:, i % 2, :]), two(wst[:, i % 2, :]), tab[:, i, :].unsqueeze(1).broadcast_to([P, 2, T]),
                                       ALU.mult).then_inc(s("s5_back"), 1)
            def rope(part, l):
                n = ROPES[part, l]
                z = (diffz if part[0] == "d" else retz)[:, (0 if part[1] == "k" else 4):(4 if part[1] == "k" else 8), 0:T]
                tmp_c = aux[:, 0:2, :].rearrange("p a b -> p (a b)").rearrange("p (a b) -> p a b", b=T)
                pool.wait_ge(s("rotated2"), n + 1)
                pool.tensor_tensor(tmp_c, z, c("cos" + part[0]).unsqueeze(1).broadcast_to([P, 4, T]), ALU.mult)\
                    .then_inc(s("cos2"), 1)

            def decay_tables(l, hh):
                n = 4 * l + hh
                f, b = dmat[:, hh, :], aux[:, 9, :]
                three = lambda v: v.rearrange("p (a b) -> p a b", a=2)
                pool.wait_ge(s("decay_exp"), 2 * n + 1)
                link(pool.affine_select(out=three(f), in_=three(f), compare_op=ALU.is_ge, fill=0.0, base=0,
                                        pattern=[[-P, 2], [1, T]], channel_multiplier=-1))
                pool.wait_ge(s("decay_exp"), 2 * n + 2)
                pool.affine_select(out=three(b), in_=three(b), compare_op=ALU.is_ge, fill=0.0, base=0,
                                   pattern=[[P, 2], [-1, T]], channel_multiplier=1).then_inc(s("decay_masked"), 1)
                pool.wait_ge(s("decay_masked"), 2 * n + 1)
                pool.tensor_tensor(f, f, b, ALU.add).then_inc(s("decay_masked"), 1)

            def ret(l, step):
                if step < len(RET[l]) and RET[l][step][0] == 0:
                    n, (st, hh) = RET_AT[l] + step, RET[l][step]
                    k = 4 * l + hh
                    if hh == 0:
                        pool.wait_ge(s("states_ready"), 4 * l + 4)
                    if n >= 2:
                        pool.wait_ge(s("ret_out"), n - 1)
                    pool.wait_ge(s("state_decay"), 2 * k + 2)
                    for dr in range(2):
                        v = slice(T * dr, T * dr + T)
                        pool.tensor_tensor(aux[:, 2 + n % 2, v], retz[:, 4 + hh, 0:T], aux[:, 4 + k % 2, v], ALU.mult)\
                            .then_inc(s("q_decayed"), 1)

            low_until(("pleg", KT - 1))
            pool.wait_ge(block2_loaded, 32)
            for l in range(LAYERS):
                low_until(("dq", l, 3))
                rope("dk", l)
                low_until(("dv", l, 3))
                rope("dq", l)
                for slot, name in enumerate(slot_units(l)):
                    low_until(name, 2)
                    for kind, step in SLOTS[l][slot]:
                        if kind == "rot":
                            rope(step, l)
                        if kind == "tables":
                            decay_tables(l, step)
                        if kind == "ret":
                            ret(l, step)
                low_until(("wo", l, KT - 1))


def tiles(w, n_out=None):
    k, n = w.shape
    return w.reshape(k // P, P, n // P, P).transpose(2, 1, 0, 3).reshape(n // P, P, k)


def weight_stream(a):
    f32 = np.float32
    out = np.zeros((NU, P, UW), f32)

    def put(name, v):
        v = v.reshape(P, -1)
        out[UNIT[name]][:, 0:v.shape[1]] = v

    for tag in ("ffn1", "ffn2"):
        w1, w3 = tiles(a[tag + "_w1"][0]), tiles(a[tag + "_w3"][0])
        w2 = a[tag + "_w2"][0].reshape(FT, P, D)
        for f in range(FT):
            put((tag, "w1", f), w1[f])
            put((tag, "w3", f), w3[f])
            put((tag, "w2", f), w2[f])
    w = a["w_in"][0]
    at = [HEADS * HD + P * k for k in range(7)]
    q = w[:, 0:512].reshape(D, 2, 4, HD).transpose(0, 2, 1, 3).reshape(D, 512)
    for j, t in enumerate(tiles(q)):
        put(("q", j), t)
    kc, vc, ks, vs, kw, vw = (w[:, at[n]:at[n + 1]] for n in range(6))
    for name, part in (("kc", kc), ("vc", vc), ("ks", ks), ("kw", kw)):
        put((name,), tiles(part)[0])
    gate = w[:, at[6]:at[6] + 24].reshape(D, 2, 4, 3).transpose(0, 3, 2, 1).reshape(D, 24)
    vg = np.concatenate([vs, vw, gate], axis=1).reshape(KT, P, 280).transpose(1, 0, 2)
    for n in range(3):
        put(("vg", n), vg[:, 3 * n:3 * n + 3])
    for j, t in enumerate(tiles(w[:, at[6] + 24:])):
        put(("u", j), t)
    for tag, name in (("cmpk", "cmp_wk1"), ("cmpv", "cmp_wv1")):
        v = a[name][0].reshape(16, P, 256).transpose(1, 0, 2)
        for n in range(4):
            put((tag, n), v[:, 4 * n:4 * n + 4])
    glu = tiles(a["s5_w_glu"][0])
    for n in range(2):
        put(("glu", n), glu[2 * n:2 * n + 2].transpose(1, 0, 2))
    wout = a["w_out"][0]
    wout = np.concatenate([wout[0:512].reshape(2, 4, HD, D).transpose(1, 0, 2, 3).reshape(512, D), wout[512:]], axis=0)
    ple = a["w_ple"][0].reshape(2, P, KT, P).transpose(2, 1, 0, 3).reshape(KT, P, 2 * P)
    for n in range(2):
        put(("plew", n), ple[4 * n:4 * n + 4].transpose(1, 0, 2))
    for name, v in (("wout", wout), ("pleg", a["w_ple_gate"][0])):
        for j, t in enumerate(tiles(v)):
            put((name, j), t)
    order = ["rk", "rv", "dk", "dv", "rq", "rg", "dq", "dg", "mu", "mv", "mg"]
    for l in range(LAYERS):
        w = a["w_in_2"][l]
        for n, name in enumerate(order):
            part = w[:, BW * n:BW * n + BW]
            if name in ("rv", "dv", "mv"):
                v = part.reshape(KT, P, BW).transpose(1, 0, 2)
                for k in range(4):
                    put((name, l, k), v[:, 2 * k:2 * k + 2])
            else:
                for j, t in enumerate(tiles(part)):
                    put((name, l, j), t)
        for n, t in enumerate(tiles(w[:, 11 * BW:])):
            put(("mlog", l, n // KT, n % KT), t)
        bo = np.stack([tiles(a["w_branch_out_2"][l, b]) for b in range(3)])
        for f in range(KT):
            put(("wbo", l, f, 0), bo[0:2, f].transpose(1, 0, 2))
            put(("wbo", l, f, 1), bo[2, f])
        for j, t in enumerate(tiles(a["w_out_2"][l])):
            put(("wo", l, j), t)
    return out


def rope_table(head, pos_of, half_freqs):
    ang = np.concatenate([pos_of[n][:, None] * half_freqs[n][None, :] for n in range(len(pos_of))], axis=1)
    ang = np.tile(ang.T.astype(np.float32), (P // (head // 2), 1))
    return np.cos(ang).astype(np.float32), np.sin(ang).astype(np.float32)


def shape_constants():
    f32 = np.float32
    t = np.arange(T, dtype=f32)
    v = {"ident": np.eye(P, dtype=f32), "ones": np.ones((P, P), f32)}
    for name, head in (("rot64", 64), ("rot128", 128)):
        m = np.zeros((P, P), f32)
        for d in range(P):
            first = d % head < head // 2
            m[d + head // 2 if first else d - head // 2, d] = -1.0 if first else 1.0
        v[name] = m
    inv = (10000.0 ** (-np.arange(32, dtype=f32) / f32(32))).astype(f32)
    v["cos1"], v["sin1"] = rope_table(64, [t], [inv])
    row, colp = np.repeat(np.arange(T // 64, dtype=f32), 64), np.tile(np.arange(64, dtype=f32), T // 64)
    for name, head in (("r", 128), ("d", 64)):
        nf = head // 4
        inv = (10000.0 ** (-np.arange(nf, dtype=f32) / f32(nf))).astype(f32)
        v["cos" + name], v["sin" + name] = rope_table(head, [row, colp], [inv, inv])
    p = np.arange(P)
    v["causal"] = np.where(p[None, :] <= p[:, None], 0.0, NEG).astype(f32)
    q = p[:, None, None] + P * np.arange(2)[None, :, None]
    blk = np.arange(16)[None, None, :]
    ok = ((blk * CSTR + CLEN - 1 <= q) & (blk < NCMP)).reshape(P, 32)
    v["cmask"] = ok.astype(f32)
    v["cneg"] = np.where(ok, 0.0, NEG).astype(f32)
    v["gmask"] = np.stack([p // 16 % 2 == 0, p // 16 % 2 == 1], axis=1).astype(f32)
    v["steps"] = np.tile(t, (P, 1))
    v["dist"] = (t[None, None, :] - (p[:, None, None] + P * np.arange(2)[None, :, None])).reshape(P, 2 * T).astype(f32)
    j = p[:, None] + P * np.arange(2)[None, :]
    v["jrow"] = np.concatenate([T - 1 - j, j], axis=1).astype(f32)
    return v


def small_inputs(a):
    f32 = np.float32
    cols = lambda v: np.asarray(v, f32).reshape(-1, P).T
    wide = lambda v: np.tile(np.asarray(v, f32).reshape(1, -1), (P, 1))
    v = shape_constants()
    for name, key in (("g_ffn1", "norm_ffn1"), ("g_mix", "norm_mix"), ("g_ffn2", "norm_ffn2"), ("g_ple", "norm_ple"),
                      ("g_final", "norm_final"), ("g_pre", "g_pre_2"), ("g_post", "g_post_2"), ("b_mod", "b_mod_2"),
                      ("b_glu", "s5_b_glu"), ("s5_d", "s5_d"), ("a_re", "s5_a_re"), ("a_im", "s5_a_im")):
        v[name] = cols(a[key])
    v["log_dt"] = cols(np.repeat(a["s5_log_dt"][0], 64))
    for name, key in (("b_re", "s5_b_re"), ("b_im", "s5_b_im"), ("c_re", "s5_c_re"), ("c_im", "s5_c_im")):
        m = a[key][0] if name[0] == "b" else a[key][0].transpose(0, 2, 1)
        out = np.zeros((2, 64, NST, 2, 16), f32)
        m = m.reshape(NST, 2, 64, 16)
        for g in range(2):
            out[g, :, :, g, :] = m[:, g].transpose(1, 0, 2)
        v[name] = out.reshape(P, 512)
    v["pe"] = np.concatenate([a[k][0].reshape(16, P).T for k in ("cmp_pe_k", "cmp_pe_v")], axis=1)
    for name, key in (("w2k", "cmp_wk2"), ("w2v", "cmp_wv2")):
        v[name] = a[key][0].reshape(2, P, HD).transpose(1, 0, 2).reshape(P, P)
    v["lamq"], v["lamk"], v["ret_logit"] = wide(a["diff_lambda_q_2"]), wide(a["diff_lambda_k_2"]), wide(a["ret_decay_logit_2"])
    v["wsT"] = a["mlp_w_s_2"].transpose(3, 0, 1, 2).reshape(P, 2 * 4 * P)
    v["pT"] = a["p"][0, 0].T.reshape(2, P, T).transpose(1, 0, 2).reshape(P, 2 * T)
    join = lambda parts: np.ascontiguousarray(np.concatenate([np.asarray(v[n], f32).reshape(P, w) for n, w in parts], axis=1))
    return join(PACK + PACK1), join(PACK2)


def kernel(**inputs):
    import concourse.bacc as bacc
    from concourse.bass_utils import run_bass_kernel_spmd

    a = {k: np.asarray(v) for k, v in inputs.items()}
    by_feature = lambda x: np.ascontiguousarray(x[0].T.reshape(KT, P, T).transpose(1, 0, 2))
    pack, pack2 = small_inputs(a)
    arrays = {
        "stream": weight_stream(a),
        "mod_stream": np.ascontiguousarray(a["w_mod_2"].transpose(0, 2, 1)).reshape(MODS, P, 4, T),
        "cond": np.tile(np.stack([a["c_2"][0], a["c_ctx_2"]]).reshape(1, 2, 4, T), (P, 1, 1, 1)),
        "pack": pack,
        "pack2": pack2,
        "bs_rows": np.ascontiguousarray(a["mlp_b_s_2"].reshape(1, 2 * BW)),
        "x_in": by_feature(a["x"]),
        "ctx_in": by_feature(a["ctx_2"]),
    }
    nc = bacc.Bacc("TRN2", target_bir_lowering=False, num_devices=1)
    args = [nc.dram_tensor(n, v.shape, mybir.dt.from_np(v.dtype), kind="ExternalInput").ap() for n, v in arrays.items()]
    out = nc.dram_tensor("out", (P, KT, T), F32, kind="ExternalOutput").ap()
    two_block_kernel(nc, *args, out)
    r = run_bass_kernel_spmd(nc, [arrays], core_ids=[0])
    y = r.results[0]["out"]
    return np.ascontiguousarray(y.transpose(1, 0, 2).reshape(D, T).T)[None]
```
